# Optimizing a Trainium2 kernel written in Bass

```python
import math
import jax, jax.numpy as jnp
from jax import lax
import numpy as np

D_MODEL = 1024
BATCH = 1
SEQ = 256
DEPTH = 2

HEAD_DIM = 64
MOBA_HEADS = 4
DIFF_HEADS = 4
DSA_HEADS = 4
DIFF_V_DIM = 2 * HEAD_DIM
IDX_HEADS = 8
IDX_DIM = 64
MOBA_BLOCK = 256
MOBA_TOPK = 3
DSA_TOPK_MAX = 256
ROPE_THETA = 10000.0
EPS = 1e-6
Q_BLOCK = 128
MOBA_Q_CHUNK = 32
D_FF = -(-8 * D_MODEL // (3 * 256)) * 256

MOBA_W = MOBA_HEADS * HEAD_DIM
DIFF_QK_W = DIFF_HEADS * 2 * HEAD_DIM
DIFF_V_W = DIFF_HEADS * DIFF_V_DIM
DSA_W = DSA_HEADS * HEAD_DIM
IDX_Q_W = IDX_HEADS * IDX_DIM
MIX_W = MOBA_W + DIFF_V_W + DSA_W
IN_COLS = 3 * MOBA_W + 2 * DIFF_QK_W + DIFF_V_W + 3 * DSA_W + IDX_Q_W + IDX_DIM + IDX_HEADS


def rms_norm(x, g):
    xf = x.astype(jnp.float32)
    y = xf * lax.rsqrt(jnp.mean(xf * xf, axis=-1, keepdims=True) + EPS)
    return (y * g.astype(jnp.float32)).astype(x.dtype)

def rope_tables(seq, dim):
    inv = 1.0 / (ROPE_THETA ** (jnp.arange(0, dim, 2, dtype=jnp.float32) / dim))
    ang = jnp.arange(seq, dtype=jnp.float32)[:, None] * inv[None, :]
    return jnp.cos(ang), jnp.sin(ang)

def apply_rope(x, cos, sin):
    x1, x2 = jnp.split(x, 2, axis=-1)
    c = cos.astype(x.dtype)
    s = sin.astype(x.dtype)
    return jnp.concatenate([x1 * c - x2 * s, x1 * s + x2 * c], axis=-1)

def split_heads(t, n_heads):
    b, s, _ = t.shape
    return t.reshape(b, s, n_heads, -1).transpose(0, 2, 1, 3)

def merge_heads(t):
    b, h, s, d = t.shape
    return t.transpose(0, 2, 1, 3).reshape(b, s, h * d)

def moba_attention(q, k, v):
    B, H, S, D = q.shape
    nb = -(-S // MOBA_BLOCK)
    pad = nb * MOBA_BLOCK - S
    kb = jnp.pad(k, ((0, 0), (0, 0), (0, pad), (0, 0))).reshape(B, H, nb, MOBA_BLOCK, D)
    vb = jnp.pad(v, ((0, 0), (0, 0), (0, pad), (0, 0))).reshape(B, H, nb, MOBA_BLOCK, D)
    k_mean = jnp.mean(kb.astype(jnp.float32), axis=3).astype(k.dtype)
    n_sel = min(MOBA_TOPK, nb - 1)
    scale = D ** -0.5
    blk_ids = jnp.arange(nb)
    own_off = jnp.arange(MOBA_BLOCK)
    gather = jax.vmap(jax.vmap(lambda t, i: t[i]))

    def chunk(i):
        start = i * MOBA_Q_CHUNK
        qc = lax.dynamic_slice_in_dim(q, start, MOBA_Q_CHUNK, axis=2)
        qpos = start + jnp.arange(MOBA_Q_CHUNK)
        cur = start // MOBA_BLOCK
        k_own = lax.dynamic_index_in_dim(kb, cur, axis=2, keepdims=False)
        v_own = lax.dynamic_index_in_dim(vb, cur, axis=2, keepdims=False)
        own_pos = cur * MOBA_BLOCK + own_off
        s_own = jnp.einsum('bhcd,bhkd->bhck', qc, k_own).astype(jnp.float32) * scale
        s_own = jnp.where(own_pos[None, :] <= qpos[:, None], s_own, -jnp.inf)
        if n_sel == 0:
            p_own = jax.nn.softmax(s_own, axis=-1).astype(v.dtype)
            return jnp.einsum('bhck,bhkd->bhcd', p_own, v_own)
        gate = jnp.einsum('bhcd,bhnd->bhcn', qc, k_mean).astype(jnp.float32)
        gate = jnp.where(blk_ids < cur, gate, -jnp.inf)
        _, sel = lax.top_k(gate, n_sel)
        sel_ok = jnp.arange(n_sel) < cur
        k_sel = gather(kb, sel)
        v_sel = gather(vb, sel)
        s_sel = jnp.einsum('bhcd,bhcnkd->bhcnk', qc, k_sel).astype(jnp.float32) * scale
        s_sel = jnp.where(sel_ok[:, None], s_sel, -jnp.inf).reshape(B, H, MOBA_Q_CHUNK, n_sel * MOBA_BLOCK)
        p = jax.nn.softmax(jnp.concatenate([s_sel, s_own], axis=-1), axis=-1).astype(v.dtype)
        p_sel = p[..., :n_sel * MOBA_BLOCK].reshape(B, H, MOBA_Q_CHUNK, n_sel, MOBA_BLOCK)
        p_own = p[..., n_sel * MOBA_BLOCK:]
        return (jnp.einsum('bhcnk,bhcnkd->bhcd', p_sel, v_sel)
                + jnp.einsum('bhck,bhkd->bhcd', p_own, v_own))

    out = lax.map(chunk, jnp.arange(S // MOBA_Q_CHUNK))
    return out.transpose(1, 2, 0, 3, 4).reshape(B, H, S, D)

def diff_attention(q1, q2, k1, k2, v, lam):
    B, H, S, D = q1.shape
    scale = D ** -0.5
    kpos = jnp.arange(S)

    def block(i):
        start = i * Q_BLOCK
        qpos = start + jnp.arange(Q_BLOCK)
        mask = kpos[None, :] <= qpos[:, None]

        def probs(qf, kf):
            qb = lax.dynamic_slice_in_dim(qf, start, Q_BLOCK, axis=2)
            s = jnp.einsum('bhqd,bhkd->bhqk', qb, kf).astype(jnp.float32) * scale
            return jax.nn.softmax(jnp.where(mask, s, -jnp.inf), axis=-1)

        a = probs(q1, k1) - lam * probs(q2, k2)
        return jnp.einsum('bhqk,bhkv->bhqv', a.astype(v.dtype), v)

    out = lax.map(block, jnp.arange(S // Q_BLOCK))
    return out.transpose(1, 2, 0, 3, 4).reshape(B, H, S, v.shape[-1])

def dsa_attention(q, k, v, iq, ik, iw):
    B, H, S, D = q.shape
    n_top = min(DSA_TOPK_MAX, S // 4)
    scale = D ** -0.5
    kpos = jnp.arange(S)
    gather = jax.vmap(lambda t, i: t[:, i])

    def chunk(i):
        start = i * Q_BLOCK
        qpos = start + jnp.arange(Q_BLOCK)
        iqc = lax.dynamic_slice_in_dim(iq, start, Q_BLOCK, axis=2)
        iwc = lax.dynamic_slice_in_dim(iw, start, Q_BLOCK, axis=1)
        logits = jnp.einsum('bhcd,bsd->bhcs', iqc, ik).astype(jnp.float32) * (IDX_DIM ** -0.5)
        score = jnp.einsum('bch,bhcs->bcs', iwc.astype(jnp.float32), jax.nn.relu(logits))
        score = jnp.where(kpos[None, :] <= qpos[:, None], score, -jnp.inf)
        _, sel = lax.top_k(score, n_top)
        sel_ok = sel <= qpos[None, :, None]
        qc = lax.dynamic_slice_in_dim(q, start, Q_BLOCK, axis=2)
        k_sel = gather(k, sel)
        v_sel = gather(v, sel)
        s = jnp.einsum('bhcd,bhcnd->bhcn', qc, k_sel).astype(jnp.float32) * scale
        s = jnp.where(sel_ok[:, None], s, -jnp.inf)
        p = jax.nn.softmax(s, axis=-1).astype(v.dtype)
        return jnp.einsum('bhcn,bhcnd->bhcd', p, v_sel)

    out = lax.map(chunk, jnp.arange(S // Q_BLOCK))
    return out.transpose(1, 2, 0, 3, 4).reshape(B, H, S, D)

def first_inputs(seed: int = 0) -> dict:
    key = jax.random.key(seed)
    ks = jax.random.split(key, 12)
    f32 = jnp.float32

    def nrm(k, shape, scale):
        return jax.random.normal(k, shape, f32) * scale

    return {
        "x": nrm(ks[0], (BATCH, SEQ, D_MODEL), 1.0),
        "attn_norm_g": 1.0 + nrm(ks[1], (DEPTH, D_MODEL), 0.05),
        "w_in": nrm(ks[2], (DEPTH, D_MODEL, IN_COLS), D_MODEL ** -0.5),
        "q_norm_g": 1.0 + nrm(ks[3], (DEPTH, 3, HEAD_DIM), 0.05),
        "k_norm_g": 1.0 + nrm(ks[4], (DEPTH, 3, HEAD_DIM), 0.05),
        "diff_lambda": nrm(ks[5], (DEPTH, 4, HEAD_DIM), 0.1),
        "diff_subln_g": 1.0 + nrm(ks[6], (DEPTH, DIFF_V_DIM), 0.05),
        "w_out": nrm(ks[7], (DEPTH, MIX_W, D_MODEL), MIX_W ** -0.5),
        "ffn_norm_g": 1.0 + nrm(ks[8], (DEPTH, D_MODEL), 0.05),
        "w_gate": nrm(ks[9], (DEPTH, D_MODEL, D_FF), D_MODEL ** -0.5),
        "w_up": nrm(ks[10], (DEPTH, D_MODEL, D_FF), D_MODEL ** -0.5),
        "w_down": nrm(ks[11], (DEPTH, D_FF, D_MODEL), D_FF ** -0.5),
    }

def first_block(x, attn_norm_g, w_in, q_norm_g, k_norm_g, diff_lambda, diff_subln_g,
              w_out, ffn_norm_g, w_gate, w_up, w_down):
    S = x.shape[1]
    cos, sin = rope_tables(S, HEAD_DIM)
    sizes = [MOBA_W] * 3 + [DIFF_QK_W, DIFF_QK_W, DIFF_V_W] + [DSA_W] * 3 + [IDX_Q_W, IDX_DIM, IDX_HEADS]
    offsets = []
    acc = 0
    for sz in sizes[:-1]:
        acc += sz
        offsets.append(acc)

    for l in range(DEPTH):
        h = rms_norm(x, attn_norm_g[l])
        proj = h @ w_in[l]
        (mq, mk, mv, dq, dk, dv, sq, sk, sv, iq, ik, iw) = jnp.split(proj, offsets, axis=-1)
        qg, kg = q_norm_g[l], k_norm_g[l]

        def qk(t, nh, g):
            return apply_rope(rms_norm(split_heads(t, nh), g), cos, sin)

        moba = moba_attention(qk(mq, MOBA_HEADS, qg[0]), qk(mk, MOBA_HEADS, kg[0]),
                              split_heads(mv, MOBA_HEADS))

        dq_h = qk(dq, 2 * DIFF_HEADS, qg[1])
        dk_h = qk(dk, 2 * DIFF_HEADS, kg[1])
        lam_init = 0.8 - 0.6 * math.exp(-0.3 * l)
        lp = diff_lambda[l].astype(jnp.float32)
        lam = jnp.exp(jnp.sum(lp[0] * lp[1])) - jnp.exp(jnp.sum(lp[2] * lp[3])) + lam_init
        diff = diff_attention(dq_h[:, 0::2], dq_h[:, 1::2], dk_h[:, 0::2], dk_h[:, 1::2],
                              split_heads(dv, DIFF_HEADS), lam)
        diff = rms_norm(diff, diff_subln_g[l]) * (1.0 - lam_init)

        iq_h = apply_rope(split_heads(iq, IDX_HEADS), cos, sin)
        ik_r = apply_rope(ik, cos, sin)
        dsa = dsa_attention(qk(sq, DSA_HEADS, qg[2]), qk(sk, DSA_HEADS, kg[2]),
                            split_heads(sv, DSA_HEADS), iq_h, ik_r,
                            iw * (IDX_HEADS ** -0.5))

        mix = jnp.concatenate([merge_heads(moba), merge_heads(diff), merge_heads(dsa)], axis=-1)
        x = x + mix @ w_out[l]

        h2 = rms_norm(x, ffn_norm_g[l])
        x = x + (jax.nn.silu(h2 @ w_gate[l]) * (h2 @ w_up[l])) @ w_down[l]
    return x


DEPTH_2 = 1

NEG_INF = -1e30
FORCE_SCORE = 1e4
N_BRANCH = 3

GMLP_WIDTH = 1024
GMLP_GROUPS = 4
GMLP_GROUP_DIM = GMLP_WIDTH // GMLP_GROUPS
GMLP_CHUNK = 128

NSA_HEADS = 16
NSA_KV_GROUPS = 4
NSA_HEAD_DIM = 64
NSA_HPG = NSA_HEADS // NSA_KV_GROUPS
NSA_Q_WIDTH = NSA_HEADS * NSA_HEAD_DIM
NSA_KV_WIDTH = NSA_KV_GROUPS * NSA_HEAD_DIM
CMP_BLOCK = 32
CMP_STRIDE = 16
CMP_HIDDEN = 256
SEL_BLOCK = 64
SEL_TOP_N = 16
WINDOW = 512
NSA_Q_CHUNK = 64

RNN_WIDTH = 1024
RNN_HEADS = 16
RNN_HEAD_DIM = RNN_WIDTH // RNN_HEADS
CONV_WIDTH = 4
LRU_C = 8.0

D_FF_2 = -(-8 * D_MODEL // (3 * 256)) * 256

IN_SPLITS = (GMLP_WIDTH, GMLP_WIDTH, NSA_Q_WIDTH, 6 * NSA_KV_WIDTH, N_BRANCH * NSA_HEADS, RNN_WIDTH, RNN_WIDTH, N_BRANCH * D_MODEL)
D_IN = sum(IN_SPLITS)


def rms_norm_2(x, g):
    xf = x.astype(jnp.float32)
    y = xf * lax.rsqrt(jnp.mean(xf * xf, axis=-1, keepdims=True) + EPS)
    return (y * g.astype(jnp.float32)).astype(x.dtype)

def layer_norm(x, g, b):
    xf = x.astype(jnp.float32)
    mu = jnp.mean(xf, axis=-1, keepdims=True)
    var = jnp.mean(jnp.square(xf - mu), axis=-1, keepdims=True)
    y = (xf - mu) * lax.rsqrt(var + EPS) * g.astype(jnp.float32) + b.astype(jnp.float32)
    return y.astype(x.dtype)

def gmlp_mixer(u, v, ln_g, ln_b, w_s, b_s):
    B, S, _ = u.shape
    n_chunks = S // GMLP_CHUNK
    vn = layer_norm(v, ln_g, ln_b).reshape(B, n_chunks, GMLP_CHUNK, GMLP_GROUPS, GMLP_GROUP_DIM)
    causal = jnp.tril(jnp.ones((GMLP_CHUNK, GMLP_CHUNK), w_s.dtype))
    w = w_s * causal
    mixed = jnp.einsum('gts,bnsgd->bntgd', w, vn) + b_s.T[None, None, :, :, None]
    return u * mixed.reshape(B, S, GMLP_WIDTH)

def nsa_mixer(q, k_cmp, v_cmp, k_slc, v_slc, k_win, v_win, branch_gates,
              pe_k, pe_v, wk1, wk2, wv1, wv2):
    B, S, _ = q.shape
    G, HP, DH = NSA_KV_GROUPS, NSA_HPG, NSA_HEAD_DIM
    scale = DH ** -0.5
    qh = q.reshape(B, S, G, HP, DH).transpose(0, 2, 3, 1, 4)

    def kv_heads(t):
        return t.reshape(B, S, G, DH).transpose(0, 2, 1, 3)

    k_cmp, v_cmp, k_slc, v_slc, k_win, v_win = map(kv_heads, (k_cmp, v_cmp, k_slc, v_slc, k_win, v_win))
    pos = jnp.arange(S)

    n_cmp = (S - CMP_BLOCK) // CMP_STRIDE + 1
    blk_idx = jnp.arange(n_cmp)[:, None] * CMP_STRIDE + jnp.arange(CMP_BLOCK)[None, :]

    def compress(t, pe, w1, w2):
        blocks = t[:, :, blk_idx] + pe
        flat = blocks.reshape(B, G, n_cmp, CMP_BLOCK * DH)
        return jax.nn.gelu(flat @ w1) @ w2

    kc = compress(k_cmp, pe_k, wk1, wk2)
    vc = compress(v_cmp, pe_v, wv1, wv2)
    cmp_end = jnp.arange(n_cmp) * CMP_STRIDE + CMP_BLOCK - 1
    valid_c = cmp_end[None, :] <= pos[:, None]
    s_c = jnp.einsum('bghsd,bgnd->bghsn', qh, kc).astype(jnp.float32) * scale
    s_c = jnp.where(valid_c, s_c, NEG_INF)
    p_c = jax.nn.softmax(s_c, axis=-1) * jnp.any(valid_c, axis=-1)[:, None].astype(jnp.float32)
    o_cmp = jnp.einsum('bghsn,bgnd->bghsd', p_c.astype(vc.dtype), vc)

    n_sel = S // SEL_BLOCK
    c_start = np.arange(n_cmp) * CMP_STRIDE
    s_start = np.arange(n_sel) * SEL_BLOCK
    overlap = np.clip(np.minimum(c_start[:, None] + CMP_BLOCK, s_start[None, :] + SEL_BLOCK)
                      - np.maximum(c_start[:, None], s_start[None, :]), 0, None) / CMP_BLOCK
    overlap = jnp.asarray(overlap, jnp.float32)
    imp = jnp.einsum('bghsn,nj->bgsj', p_c, overlap)
    cur = (pos // SEL_BLOCK)[:, None]
    j = jnp.arange(n_sel)[None, :]
    forced = (j == 0) | (j == cur) | (j == cur - 1)
    imp = jnp.where(forced, FORCE_SCORE, jnp.where(j > cur, NEG_INF, imp))
    top_n = min(SEL_TOP_N, n_sel)
    _, sel_idx = lax.top_k(imp, top_n)

    k_sb = k_slc.reshape(B, G, n_sel, SEL_BLOCK, DH)
    v_sb = v_slc.reshape(B, G, n_sel, SEL_BLOCK, DH)
    pad = jnp.zeros((B, G, WINDOW, DH), k_win.dtype)
    k_wp = jnp.concatenate([pad, k_win], axis=2)
    v_wp = jnp.concatenate([pad, v_win], axis=2)
    gather = jax.vmap(jax.vmap(lambda blocks, ix: blocks[ix]))

    C = NSA_Q_CHUNK
    n_chunks = S // C
    q_ch = jnp.moveaxis(qh.reshape(B, G, HP, n_chunks, C, DH), 3, 0)
    idx_ch = jnp.moveaxis(sel_idx.reshape(B, G, n_chunks, C, top_n), 2, 0)

    def chunk_fn(args):
        c, qc, ic = args
        t = c * C + jnp.arange(C)
        kg = gather(k_sb, ic)
        vg = gather(v_sb, ic)
        kpos = ic[..., None] * SEL_BLOCK + jnp.arange(SEL_BLOCK)
        s = jnp.einsum('bghcd,bgckld->bghckl', qc, kg).astype(jnp.float32) * scale
        s = jnp.where((kpos <= t[:, None, None])[:, :, None], s, NEG_INF)
        p = jax.nn.softmax(s.reshape(B, G, HP, C, top_n * SEL_BLOCK), axis=-1).reshape(s.shape)
        o_s = jnp.einsum('bghckl,bgckld->bghcd', p.astype(vg.dtype), vg)
        kw = lax.dynamic_slice_in_dim(k_wp, c * C, WINDOW + C, axis=2)
        vw = lax.dynamic_slice_in_dim(v_wp, c * C, WINDOW + C, axis=2)
        wpos = c * C - WINDOW + jnp.arange(WINDOW + C)
        wmask = (wpos[None, :] >= 0) & (wpos[None, :] <= t[:, None]) & (wpos[None, :] > t[:, None] - WINDOW)
        sw = jnp.einsum('bghcd,bgkd->bghck', qc, kw).astype(jnp.float32) * scale
        sw = jnp.where(wmask, sw, NEG_INF)
        o_w = jnp.einsum('bghck,bgkd->bghcd', jax.nn.softmax(sw, axis=-1).astype(vw.dtype), vw)
        return o_s, o_w

    o_slc, o_win = lax.map(chunk_fn, (jnp.arange(n_chunks), q_ch, idx_ch))
    o_slc = jnp.moveaxis(o_slc, 0, 3).reshape(B, G, HP, S, DH)
    o_win = jnp.moveaxis(o_win, 0, 3).reshape(B, G, HP, S, DH)

    g = jax.nn.sigmoid(branch_gates).reshape(B, S, G, HP, N_BRANCH).transpose(0, 2, 3, 1, 4)
    o = g[..., 0:1] * o_cmp + g[..., 1:2] * o_slc + g[..., 2:3] * o_win
    return o.transpose(0, 3, 1, 2, 4).reshape(B, S, NSA_Q_WIDTH)

def rglru_mixer(xr, gate, conv_w, conv_b, w_a, b_a, w_x, b_x, lam):
    B, S, _ = xr.shape
    xc = lax.conv_general_dilated(xr, conv_w[:, None, :], window_strides=(1,),
                                  padding=[(CONV_WIDTH - 1, 0)],
                                  dimension_numbers=('NWC', 'WIO', 'NWC'),
                                  feature_group_count=RNN_WIDTH) + conv_b
    xh = xc.reshape(B, S, RNN_HEADS, RNN_HEAD_DIM)
    r = jax.nn.sigmoid(jnp.einsum('bshi,hio->bsho', xh, w_a).reshape(B, S, RNN_WIDTH) + b_a)
    i = jax.nn.sigmoid(jnp.einsum('bshi,hio->bsho', xh, w_x).reshape(B, S, RNN_WIDTH) + b_x)
    log_a = -LRU_C * r.astype(jnp.float32) * jax.nn.softplus(-lam.astype(jnp.float32))
    a = jnp.exp(log_a)
    b_in = jnp.sqrt(-jnp.expm1(2.0 * log_a)) * (i * xc).astype(jnp.float32)

    def combine(left, right):
        a1, b1 = left
        a2, b2 = right
        return a2 * a1, a2 * b1 + b2

    _, h = lax.associative_scan(combine, (a, b_in), axis=1)
    return h.astype(xr.dtype) * jax.nn.gelu(gate)

def hybrid_layer(x, g_pre_mix, g_post_mix, g_pre_ffn, g_post_ffn, w_in,
                 gmlp_ln_g, gmlp_ln_b, gmlp_ws, gmlp_bs,
                 nsa_pe_k, nsa_pe_v, nsa_wk1, nsa_wk2, nsa_wv1, nsa_wv2,
                 rnn_conv_w, rnn_conv_b, rnn_wa, rnn_ba, rnn_wx, rnn_bx, rnn_lam,
                 w_br_a, w_br_b, w_br_c, w_o, w_ffn_in, w_ffn_out):
    B, S, _ = x.shape
    h = rms_norm_2(x, g_pre_mix)
    z = h @ w_in
    split_points = [int(p) for p in np.cumsum(IN_SPLITS)[:-1]]
    u, v, q, kv, nsa_g, xr, rg, mg = jnp.split(z, split_points, axis=-1)
    k_cmp, v_cmp, k_slc, v_slc, k_win, v_win = jnp.split(kv, 6, axis=-1)

    y_a = gmlp_mixer(jax.nn.gelu(u), jax.nn.gelu(v), gmlp_ln_g, gmlp_ln_b, gmlp_ws, gmlp_bs)
    y_b = nsa_mixer(q, k_cmp, v_cmp, k_slc, v_slc, k_win, v_win, nsa_g,
                    nsa_pe_k, nsa_pe_v, nsa_wk1, nsa_wk2, nsa_wv1, nsa_wv2)
    y_c = rglru_mixer(xr, rg, rnn_conv_w, rnn_conv_b, rnn_wa, rnn_ba, rnn_wx, rnn_bx, rnn_lam)

    gates = jax.nn.sigmoid(mg).reshape(B, S, N_BRANCH, D_MODEL)
    merged = (gates[:, :, 0] * (y_a @ w_br_a)
              + gates[:, :, 1] * (y_b @ w_br_b)
              + gates[:, :, 2] * (y_c @ w_br_c))
    x = x + rms_norm_2(merged @ w_o, g_post_mix)

    hf = rms_norm_2(x, g_pre_ffn)
    f_gate, f_up = jnp.split(hf @ w_ffn_in, 2, axis=-1)
    f = (jax.nn.silu(f_gate) * f_up) @ w_ffn_out
    return x + rms_norm_2(f, g_post_ffn)

def second_inputs(seed: int = 0) -> dict:
    key = jax.random.key(seed)
    keys = iter(jax.random.split(key, 48))
    L = DEPTH_2

    def nrm(shape, scale):
        return jax.random.normal(next(keys), shape, jnp.float32) * scale

    def gain(n):
        return 1.0 + nrm((L, n), 0.05)

    u_lam = jax.random.uniform(next(keys), (L, RNN_WIDTH), jnp.float32, minval=0.9, maxval=0.999)
    a0 = u_lam ** (1.0 / LRU_C)
    rnn_lam = jnp.log(a0) - jnp.log1p(-a0)

    return {
        "x": nrm((BATCH, SEQ, D_MODEL), 1.0),
        "g_pre_mix": gain(D_MODEL),
        "g_post_mix": gain(D_MODEL),
        "g_pre_ffn": gain(D_MODEL),
        "g_post_ffn": gain(D_MODEL),
        "w_in": nrm((L, D_MODEL, D_IN), D_MODEL ** -0.5),
        "gmlp_ln_g": gain(GMLP_WIDTH),
        "gmlp_ln_b": nrm((L, GMLP_WIDTH), 0.05),
        "gmlp_ws": nrm((L, GMLP_GROUPS, GMLP_CHUNK, GMLP_CHUNK), GMLP_CHUNK ** -0.5),
        "gmlp_bs": 1.0 + nrm((L, GMLP_GROUPS, GMLP_CHUNK), 0.1),
        "nsa_pe_k": nrm((L, CMP_BLOCK, NSA_HEAD_DIM), 0.1),
        "nsa_pe_v": nrm((L, CMP_BLOCK, NSA_HEAD_DIM), 0.1),
        "nsa_wk1": nrm((L, CMP_BLOCK * NSA_HEAD_DIM, CMP_HIDDEN), (CMP_BLOCK * NSA_HEAD_DIM) ** -0.5),
        "nsa_wk2": nrm((L, CMP_HIDDEN, NSA_HEAD_DIM), CMP_HIDDEN ** -0.5),
        "nsa_wv1": nrm((L, CMP_BLOCK * NSA_HEAD_DIM, CMP_HIDDEN), (CMP_BLOCK * NSA_HEAD_DIM) ** -0.5),
        "nsa_wv2": nrm((L, CMP_HIDDEN, NSA_HEAD_DIM), CMP_HIDDEN ** -0.5),
        "rnn_conv_w": nrm((L, CONV_WIDTH, RNN_WIDTH), CONV_WIDTH ** -0.5),
        "rnn_conv_b": nrm((L, RNN_WIDTH), 0.05),
        "rnn_wa": nrm((L, RNN_HEADS, RNN_HEAD_DIM, RNN_HEAD_DIM), RNN_HEAD_DIM ** -0.5),
        "rnn_ba": nrm((L, RNN_WIDTH), 0.1),
        "rnn_wx": nrm((L, RNN_HEADS, RNN_HEAD_DIM, RNN_HEAD_DIM), RNN_HEAD_DIM ** -0.5),
        "rnn_bx": nrm((L, RNN_WIDTH), 0.1),
        "rnn_lam": rnn_lam,
        "w_br_a": nrm((L, GMLP_WIDTH, D_MODEL), GMLP_WIDTH ** -0.5),
        "w_br_b": nrm((L, NSA_Q_WIDTH, D_MODEL), NSA_Q_WIDTH ** -0.5),
        "w_br_c": nrm((L, RNN_WIDTH, D_MODEL), RNN_WIDTH ** -0.5),
        "w_o": nrm((L, D_MODEL, D_MODEL), D_MODEL ** -0.5),
        "w_ffn_in": nrm((L, D_MODEL, 2 * D_FF_2), D_MODEL ** -0.5),
        "w_ffn_out": nrm((L, D_FF_2, D_MODEL), D_FF_2 ** -0.5),
    }

def second_block(x, g_pre_mix, g_post_mix, g_pre_ffn, g_post_ffn, w_in,
              gmlp_ln_g, gmlp_ln_b, gmlp_ws, gmlp_bs,
              nsa_pe_k, nsa_pe_v, nsa_wk1, nsa_wk2, nsa_wv1, nsa_wv2,
              rnn_conv_w, rnn_conv_b, rnn_wa, rnn_ba, rnn_wx, rnn_bx, rnn_lam,
              w_br_a, w_br_b, w_br_c, w_o, w_ffn_in, w_ffn_out):
    for l in range(DEPTH_2):
        x = hybrid_layer(x, g_pre_mix[l], g_post_mix[l], g_pre_ffn[l], g_post_ffn[l], w_in[l],
                         gmlp_ln_g[l], gmlp_ln_b[l], gmlp_ws[l], gmlp_bs[l],
                         nsa_pe_k[l], nsa_pe_v[l], nsa_wk1[l], nsa_wk2[l], nsa_wv1[l], nsa_wv2[l],
                         rnn_conv_w[l], rnn_conv_b[l], rnn_wa[l], rnn_ba[l], rnn_wx[l], rnn_bx[l], rnn_lam[l],
                         w_br_a[l], w_br_b[l], w_br_c[l], w_o[l], w_ffn_in[l], w_ffn_out[l])
    return x


def setup_inputs(seed=0):
    out = dict(first_inputs(seed))
    for name, value in second_inputs(seed + 1).items():
        if name != "x":
            out[name + "_2"] = value
    return out


def reference(
    x, attn_norm_g, w_in, q_norm_g, k_norm_g, diff_lambda, diff_subln_g, w_out, ffn_norm_g,
    w_gate, w_up, w_down, g_pre_mix_2, g_post_mix_2, g_pre_ffn_2, g_post_ffn_2, w_in_2,
    gmlp_ln_g_2, gmlp_ln_b_2, gmlp_ws_2, gmlp_bs_2, nsa_pe_k_2, nsa_pe_v_2, nsa_wk1_2,
    nsa_wk2_2, nsa_wv1_2, nsa_wv2_2, rnn_conv_w_2, rnn_conv_b_2, rnn_wa_2, rnn_ba_2, rnn_wx_2,
    rnn_bx_2, rnn_lam_2, w_br_a_2, w_br_b_2, w_br_c_2, w_o_2, w_ffn_in_2, w_ffn_out_2,
):
    x = first_block(
        x, attn_norm_g, w_in, q_norm_g, k_norm_g, diff_lambda, diff_subln_g, w_out, ffn_norm_g,
        w_gate, w_up, w_down,
    )
    return second_block(
        x, g_pre_mix_2, g_post_mix_2, g_pre_ffn_2, g_post_ffn_2, w_in_2, gmlp_ln_g_2,
        gmlp_ln_b_2, gmlp_ws_2, gmlp_bs_2, nsa_pe_k_2, nsa_pe_v_2, nsa_wk1_2, nsa_wk2_2,
        nsa_wv1_2, nsa_wv2_2, rnn_conv_w_2, rnn_conv_b_2, rnn_wa_2, rnn_ba_2, rnn_wx_2,
        rnn_bx_2, rnn_lam_2, w_br_a_2, w_br_b_2, w_br_c_2, w_o_2, w_ffn_in_2, w_ffn_out_2,
    )


_drawn_inputs = setup_inputs


def setup_inputs(seed=0):
    import zlib

    import numpy as np

    out = dict(_drawn_inputs(seed))
    spreads = {}
    factors = {'gmlp_ln_g_2': 5.362,
     'gmlp_ln_b_2': 5.463,
     'nsa_pe_k_2': 64.0,
     'nsa_pe_v_2': 4.14,
     'rnn_ba_2': 8.0,
     'rnn_bx_2': 3.636,
     'gmlp_bs_2': 3.2,
     'nsa_wk1_2': 3.962,
     'nsa_wk2_2': 3.897}
    for name, (base, spread) in spreads.items():
        noise = np.random.default_rng([zlib.crc32(name.encode()), seed]).standard_normal(out[name].shape)
        drawn = base * np.exp(spread * noise) if base else spread * noise
        out[name] = __import__('jax').numpy.asarray(drawn.astype(out[name].dtype))
    for name, factor in factors.items():
        out[name] = (out[name] * factor).astype(out[name].dtype)
    return out
```

```python
from contextlib import ExitStack

import numpy as np

import concourse.bass as bass
from concourse import mybir

F32 = mybir.dt.float32
F32R = mybir.dt.float32r
ALU = mybir.AluOpType
ACT = mybir.ActivationFunctionType
AX = mybir.AxisListType

P = 128
SEQ = 256
RT = SEQ // P
D = 1024
KT = D // P
LAYERS = 2
HD = 64
EPS = 1e-6
NEG = -1e30
TAKEN = -3e38
DFF = 2816
COLS = 512
UNIT = COLS
SLOT = 6 * UNIT
TOPK = 64
IDX_HEADS = 8
FF_STEP = 256
FF_STEPS = DFF // FF_STEP

IQ, IK, IW, SQ, SK, MV, SV, DQ, DK, DV, MQ, MK = (
    0, 512, 576, 584, 840, 1096, 1352, 1608, 2120, 2632, 3144, 3400)
Z_COLS = 3656
LN_EXP = "natural_log_exp_and_others"
NARROW = 72
T_IQ, T_SQ, T_SK, T_DQ, T_DK, T_MQ, T_MK, T_IK = 0, 4, 6, 8, 12, 16, 18, 20
PAIRS1 = 22
HALVES = 10
Q2, KC2, VC2, KS2, VS2, KW2, VW2, G2, U2 = 0, 1024, 1280, 1536, 1792, 2048, 2304, 2560, 2608
GATES = 48
CMP = 15
KV_GROUPS = 4
COMP = 2 * KV_GROUPS * CMP
COMP_K = 16
B2 = 2 * PAIRS1
PAIRS2 = 30
T2_KS, T2_KW, T2_KC, T2_V = 8, 12, 16, 17
F_CK, F_CV, F_Q, F_SK, F_WK, F_HT, F_KC, F_VC, F_MIX, F_GATE = 1, 3, 5, 9, 11, 13, 14, 15, 16, 20
NGRP = 4


class Progress:

    def __init__(self, sem):
        self.sem, self.n = sem, 0

    def __call__(self, instruction):
        instruction.then_inc(self.sem, 1)
        self.n += 1

    def wait(self, eng):
        eng.wait_ge(self.sem, self.n)

    def restart(self, eng):
        if self.n:
            eng.wait_ge(self.sem, self.n)
            eng.sem_clear(self.sem)
            self.n = 0


def AP_of(base, offset, pattern):
    return bass.AP(base.tensor, base.offset + offset, [list(base.ap[0])] + pattern)


def block_one_and_two(nc, t):
    ctx = ExitStack()
    with ctx:
        def sb(name, shape, dt=F32):
            return ctx.enter_context(nc.sbuf_tensor(name, shape, dt))

        def sem(name):
            return ctx.enter_context(nc.semaphore(name))

        raw = [sb(f"raw{j}", [P, SLOT]) for j in range(2)]
        whi = [sb(f"whi{j}", [P, SLOT], F32R) for j in range(2)]
        wlo = [sb(f"wlo{j}", [P, SLOT], F32R) for j in range(2)]
        x = sb("x", [P, RT, D])
        hT = [sb(f"hT_{s}", [P, KT, SEQ], F32R) for s in ("hi", "lo")]
        mixT = [sb(f"mixT_{s}", [P, KT, SEQ], F32R) for s in ("hi", "lo")]
        ffT = [sb(f"ffT_{s}", [P, 2, SEQ], F32R) for s in ("hi", "lo")]
        mix = sb("mix", [P, RT, D])
        z = sb("z", [P, RT, Z_COLS])
        headsT = sb("headsT", [P, 21, SEQ])
        probs = sb("probs", [P, 3, COLS])
        probsT = sb("probsT", [P, 3, COLS])
        scr = sb("scr", [P, 2, COLS])
        sqr = sb("sqr", [P, COLS])
        gain = sb("gain", [P, D])
        ident = sb("ident", [P, P])
        causal = sb("causal", [P, 3 * P])
        index = sb("index", [P, 3 * P])
        chosen = index
        rope_c = sb("rope_c", [P, RT, HD])
        rope_s = sb("rope_s", [P, RT, HD])
        gain_c = sb("gain_c", [P, RT, 6, HD])
        gain_s = sb("gain_s", [P, RT, 6, HD])
        hgain = headsT[:, T_MK:T_IK, :].rearrange("p a b -> p (a b)")[:, 0:6 * HD].rearrange("p (n d) -> p n d", d=HD)
        lamp = headsT[:, T_IK, :].rearrange("p (n d) -> p n d", d=HD)
        sub_g = sb("sub_g", [P, 2 * HD])
        flat = [m[:, :, :].rearrange("p k c -> p (k c)")[:, 0:COMP_K * COMP]
                .rearrange("p (j m) -> p j m", m=COMP) for m in mixT]
        flat_f = mix[:, :, :].rearrange("p r c -> p (r c)")[:, 0:COMP_K * COMP]
        small = gain_s[:, :, :, :].rearrange("p a b c -> p (a b c)")
        wk2 = small[:, 0:256].rearrange("p (k c) -> p k c", k=2)
        wv2 = small[:, 256:384].rearrange("p (k c) -> p k c", k=2)
        pe_kv = small[:, 384:416].rearrange("p (v j) -> p v j", v=2)
        par = small[:, 416:416 + 68]
        par_bs, par_cw, par_cb, par_ba, par_bx, par_lam = (
            par[:, a:b] for a, b in ((0, 4), (4, 36), (36, 44), (44, 52), (52, 60), (60, 68)))
        cmask = index[:, 0:2 * CMP].rearrange("p (r n) -> p r n", r=2)
        any_ok = index[:, 32:33]
        cstat = index[:, 64:96]
        ccoef = index[:, 96:128]
        w_s = gain_c[:, :, :, :].rearrange("p a b c -> p (a b c)")[:, 0:4 * P].rearrange("p (g t) -> p g t", g=4)
        hidT = probsT[:, 2, 0:4 * COMP]
        bn = rope_c[:, :, :].rearrange("p r d -> p (r d)")
        sp = rope_s[:, :, :].rearrange("p r d -> p (r d)")
        lam_c = sb("lam_c", [P, 2])
        lam = sb("lam", [P, 4])
        eps = sb("eps", [P, 1])
        ssq = sb("ssq", [P, 16])
        nmax = sb("nmax", [P, 8])
        sums = sb("sums", [P, 2, 8])
        inv = sb("inv", [P, 8])
        hss = sb("hss", [P, RT, 8])
        hrs = sb("hrs", [P, RT, 8])
        top8 = sb("top8", [P, 2, 8])
        dstat = sb("dstat", [P, 8])
        bank = [ctx.enter_context(nc.psum_tensor(f"bank{i}", [P, COLS], F32)) for i in range(8)]

        raw_loaded = [sem(f"raw_loaded{j}") for j in range(2)]
        hi_ready = [sem(f"hi_ready{j}") for j in range(2)]
        lo_ready = [sem(f"lo_ready{j}") for j in range(2)]
        used = [sem(f"used{j}") for j in range(2)]
        half_ready = sem("half_ready")
        z_act = sem("z_act")
        z_dve = sem("z_dve")
        out_added = sem("out_added")
        const_ready = sem("const_ready")
        x_loaded = sem("x_loaded")
        gain_loaded = sem("gain_loaded")
        gain_free = sem("gain_free")
        rope_loaded = sem("rope_loaded")
        par_loaded = sem("par_loaded")
        sq_ready = sem("sq_ready")
        rs_ready = sem("rs_ready")
        rows_ready = sem("rows_ready")
        turned = sem("turned")
        turned_hi = sem("turned_hi")
        turned_lo = sem("turned_lo")
        squares = sem("squares")
        ssq_ready = sem("ssq_ready")
        hrs_ready = sem("hrs_ready")
        prep = sem("prep")
        heads_turned = sem("heads_turned")
        heads_act = sem("heads_act")
        heads_dve = sem("heads_dve")
        idx_ready = sem("idx_ready")
        idx_relu = sem("idx_relu")
        idx_acc = sem("idx_acc")
        scores = sem("scores")
        masked = sem("masked")
        exped = sem("exped")
        pT_ready = sem("pT_ready")
        pT_act = sem("pT_act")
        pT_dve = sem("pT_dve")
        pv_ready = sem("pv_ready")
        o_done = sem("o_done")
        lam_sum = sem("lam_sum")
        lam_exp = sem("lam_exp")
        dsq = sem("dsq")
        drs = sem("drs")
        gu_ready = sem("gu_ready")
        silu_ready = sem("silu_ready")
        gu_free = sem("gu_free")
        ff_turned = sem("ff_turned")
        ff_hi = sem("ff_hi")
        ff_lo = sem("ff_lo")
        down_ready = sem("down_ready")
        down_added = sem("down_added")
        out_sem = sem("out_sem")
        free = [sem(f"free{r}") for r in range(2)]
        filled = sem("filled")
        read67 = [sem(f"read{b}") for b in (6, 7)]
        small_loaded = sem("small_loaded")
        ws_loaded = sem("ws_loaded")
        ws_ready = sem("ws_ready")
        rg_loaded = sem("rg_loaded")
        cmask_ready = sem("cmask_ready")
        sp_abs = sem("sp_abs")
        sp_exp = sem("sp_exp")
        sp_one = sem("sp_one")
        sp_ln = sem("sp_ln")
        sp_ready = sem("sp_ready")
        dup_ready = sem("dup_ready")
        flat_done = sem("flat_done")
        flat_hi = sem("flat_hi")
        flat_lo = sem("flat_lo")
        pad_ready = sem("pad_ready")
        cs_ready = sem("cs_ready")
        cm_ready = sem("cm_ready")
        ce_ready = sem("ce_ready")
        cn_ready = sem("cn_ready")
        ct_ready = sem("ct_ready")
        cT_act = sem("cT_act")
        cT_dve = sem("cT_dve")
        cv_ready = sem("cv_ready")
        cv_done = sem("cv_done")
        var_ready = sem("var_ready")
        vrs_ready = sem("vrs_ready")
        vn_ready = sem("vn_ready")
        merged_done = sem("merged_done")
        xc_ready = sem("xc_ready")
        rg_ready = sem("rg_ready")
        u_ready = sem("u_ready")
        gx_done = sem("gx_done")
        u_read = sem("u_read")
        root_ready = sem("root_ready")
        yc_ready = sem("yc_ready")
        yc_hi = sem("yc_hi")
        yc_lo = sem("yc_lo")
        x_added = sem("x_added")
        dve = Progress(sem("dve_own"))
        act = Progress(sem("act_own"))
        pool = Progress(sem("pool_own"))
        pe = Progress(sem("pe_own"))

        block = ctx.enter_context(nc.Block())

        def index_heads(u):
            return [2 * i + u for i in range(4)] if u < 2 else [4 * ((u - 2) // 2) + u % 2 + 2 * i for i in range(2)]

        def product(b):
            return b - (b > 6)

        def half_of(b):
            return LAYERS * HALVES + product(b) + 1

        def channels(c):
            return z[:, c // 4, (c % 4) * SEQ:(c % 4 + 1) * SEQ]

        def merged(r, n):
            return z[:, r, U2 + n * COLS:U2 + (n + 1) * COLS]

        def scr_ik(r):
            return scr[:, r, 0:P]

        def ffn_elements(c, j):
            if c == 0:
                return (6 * UNIT, 2 * UNIT)[j]
            if c == FF_STEPS:
                return 2 * UNIT
            return 6 * UNIT

        @block.sync
        def _(eng):
            def load(p, j, src):
                n = src.shape[1]
                eng.wait_ge(lo_ready[j], p + 1)
                eng.dma_start(raw[j][:, 0:n], src).then_inc(raw_loaded[j], 16)

            for r in range(RT):
                eng.dma_start(x[:, r, :], t["x"][r * P:(r + 1) * P, :]).then_inc(x_loaded, 16)

            def ffn_loads(p0, l, between, early=lambda: None):
                for j in range(2):
                    lo_, n = (0, 6 * UNIT) if j == 0 else (6 * UNIT, 2 * UNIT)
                    load(p0, j, t["ff_first"][l, :, lo_:lo_ + n])
                early()
                between()
                with eng.Fori(1, FF_STEPS) as c:
                    for j in range(2):
                        load(p0 + c, j, t["ff_loop"][l, c - 1, j])
                for j in range(2):
                    load(p0 + FF_STEPS, j, t["ff_last"][l, j])

            def next_gain(i, src):
                eng.wait_ge(gain_free, i)
                eng.dma_start(gain[:, :], src.partition_broadcast(P)).then_inc(gain_loaded, 16)

            def layer_parameters(l):
                for dst, name in ((hgain, "head_gains"), (lamp, "diff_lambda"), (sub_g[:, :], "diff_subln_g"),
                                  (lam_c[:, :], "lam_init")):
                    eng.dma_start(dst, t[name][l].partition_broadcast(P)).then_inc(par_loaded, 16)

            eng.dma_start(gain[:, :], t["attn_norm_g"][0, :].partition_broadcast(P)).then_inc(gain_loaded, 16)
            layer_parameters(0)
            with eng.Fori(0, LAYERS) as l:
                for g in range(8):
                    if g == 4:
                        next_gain(2 * l + 1, t["ffn_norm_g"][l, :])
                    for j in range(2):
                        if g == 1:
                            load(l * PAIRS1 + g, j, t["w1_narrow"][l, j])
                        else:
                            load(l * PAIRS1 + g, j, t["w1_groups"][l, g - (g > 1), j])
                for g in range(2):
                    for j in range(2):
                        load(l * PAIRS1 + 8 + g, j, t["w1_out"][l, g, j])

                def next_parameters():
                    next_gain(2 * l + 2, t["next_norm_g"][l, :])
                    layer_parameters(l + 1)
                ffn_loads(l * PAIRS1 + 10, l, next_parameters)
            for dst, name in ((small[:, 0:416], "small2"), (par, "channel2")):
                eng.dma_start(dst, t[name]).then_inc(small_loaded, 16)
            eng.dma_start(w_s, t["w_s"]).then_inc(ws_loaded, 16)
            with eng.Fori(0, 4) as g:
                for j in range(2):
                    load(B2 + g, j, t["w2_groups"][g, j])
            for j in range(2):
                load(B2 + 4, j, t["w2_narrow"][j])
            for j in range(2):
                load(B2 + 5, j, t["w2_groups"][4, j])
            next_gain(5, t["rows2"][0, :])
            with eng.Fori(0, 2) as g:
                for j in range(2):
                    load(B2 + 6 + g, j, t["w2_comp"][g, j])
            eng.wait_ge(filled, F_CV + 1)
            eng.dma_start(z[:, 0, KC2:KC2 + 512], t["w_gates"][0]).then_inc(rg_loaded, 16)
            eng.dma_start(z[:, 1, KC2:KC2 + 512], t["w_gates"][1]).then_inc(rg_loaded, 16)
            with eng.Fori(0, 4) as g:
                for j in range(2):
                    load(B2 + 8 + g, j, t["w2_groups"][5 + g, j])
            next_gain(6, t["rows2"][1, :])
            with eng.Fori(0, 18) as g:
                for j in range(2):
                    load(B2 + 12 + g, j, t["w2_groups"][9 + g, j])
            next_gain(7, t["rows2"][2, :])
            def post_gain():
                next_gain(8, t["rows2"][3, :])
            ffn_loads(B2 + PAIRS2, LAYERS, lambda: None, early=post_gain)
            next_gain(9, t["rows2"][4, :])
            for r in range(RT):
                eng.wait_ge(x_added, RT + r + 1)
                eng.dma_start(t["out"][r * P:(r + 1) * P, :], x[:, r, :]).then_inc(out_sem, 16)
            eng.wait_ge(out_sem, 16 * RT)

        @block.gpsimd
        def _(eng):
            eng.memset(eps[:, :], EPS).then_inc(const_ready, 1)
            pool(eng.memset(ident[:, :], 0.0))
            pool(eng.memset(causal[:, :], 0.0))
            pool.wait(eng)
            eng.affine_select(out=ident[:, :], in_=ident[:, :], compare_op=ALU.not_equal, fill=1.0,
                              base=0, pattern=[[-1, P]], channel_multiplier=1).then_inc(const_ready, 1)
            for c in (0, 2):
                part = causal[:, c * P:(c + 1) * P]
                eng.affine_select(out=part, in_=part, compare_op=ALU.is_ge, fill=NEG,
                                  base=0, pattern=[[-1, P]], channel_multiplier=1).then_inc(const_ready, 1)
            eng.dma_start(rope_c[:, :, :], t["rope_c"]).then_inc(rope_loaded, 16)
            eng.dma_start(rope_s[:, :, :], t["rope_s"]).then_inc(rope_loaded, 16)

            eng.wait_ge(gain_free, 4)
            pool(eng.memset(index[:, 0:48], 0.0))
            pool.wait(eng)
            for r in range(RT):
                pool(eng.affine_select(out=cmask[:, r, :], in_=cmask[:, r, :], compare_op=ALU.is_ge, fill=NEG,
                                       base=r * P - 31, pattern=[[-16, CMP]], channel_multiplier=1))
            eng.affine_select(out=any_ok, in_=any_ok, compare_op=ALU.is_ge, fill=1.0, base=30,
                              pattern=[[0, 1]], channel_multiplier=-1).then_inc(cmask_ready, 1)
            pool.wait(eng)
            eng.wait_ge(ws_loaded, 16)
            eng.affine_select(out=w_s, in_=w_s, compare_op=ALU.is_ge, fill=0.0, base=0,
                              pattern=[[0, 4], [1, P]], channel_multiplier=-1).then_inc(ws_ready, 1)

        @block.tensor
        def _(eng):
            def three(out, a, a_cols, j, w, start, stop, first=True, n=COLS):
                wh, wl = whi[j][:, w:w + n], wlo[j][:, w:w + n]
                hi, lo = (s[:, a, a_cols] for s in three.act)
                eng.matmul(out, lhsT=hi, rhs=wh, start=start, stop=False)
                eng.matmul(out, lhsT=hi, rhs=wl, start=False, stop=False)
                return eng.matmul(out, lhsT=lo, rhs=wh, start=False, stop=stop)

            def chunk(p, j, n=COLS):
                eng.wait_ge(lo_ready[j], p + 2)
                for r in range(RT):
                    for k in range(4):
                        mm = three(bank[r][:, 0:n], 4 * j + k, slice(r * P, (r + 1) * P), j, k * n,
                                   start=(j == 0 and k == 0), stop=(j == 1 and k == 3), n=n)
                    if j == 1 and r == 0:
                        mm.then_inc(half_ready, 1)
                mm.then_inc(used[j], 1)

            def turn_rows(i, src=None):
                for r in range(RT):
                    eng.wait_ge(rows_ready, i * RT + r + 1)
                    for h in range(2):
                        b, n = bank[6 + h], i * 4 + 2 * r + h
                        if r:
                            eng.wait_ge(turned_lo, n - 1)
                        for k in range(4):
                            c = (4 * h + k) * P
                            rows = mix[:, r, c:c + P] if src is None else src[:, r, c:c + P]
                            mm = eng.transpose(b[:, k * P:(k + 1) * P], rows, ident[:, :])
                        mm.then_inc(turned, 1)

            def turn_heads(l, s, src, pairs):
                eng.wait_ge(prep, l * 6 + s + 1)
                if s > 0:
                    eng.wait_ge(heads_act, l * 6 + s)
                    eng.wait_ge(heads_dve, l * 5 + (1 if s < 3 else s - 1))
                for i in range(0, pairs, 2):
                    for q in range(min(2, pairs - i)):
                        for r in range(RT):
                            mm = eng.transpose(bank[6 + i // 2][:, (q * RT + r) * P:(q * RT + r + 1) * P],
                                               src(i + q, r), ident[:, :])
                    mm.then_inc(heads_turned, 1)

            def index_scores(l, u):
                if u == 0:
                    eng.wait_ge(heads_act, l * 6 + 2)
                    eng.wait_ge(heads_dve, l * 5 + 1)
                if u >= 3:
                    eng.wait_ge(idx_relu, l * 6 + u - 2)
                b = bank[2 + u % 3]
                keys = P if u < 2 else SEQ
                for i, h in enumerate(index_heads(u)):
                    half = slice(HD * (h % 2), HD * (h % 2) + HD)
                    rows = slice(0, P) if u < 2 else slice(P, SEQ)
                    mm = eng.matmul(b[:, i * keys:(i + 1) * keys], lhsT=headsT[half, T_IQ + h // 2, rows],
                                    rhs=headsT[half, T_IK, 0:keys], start=True, stop=True)
                mm.then_inc(idx_ready, 1)

            def attend_scores(A, q, k):
                eng.wait_ge(pT_act, 2 * A + 2)
                eng.wait_ge(pT_dve, A + 1)
                for odd in range(2):
                    for u in (0, 1 + odd):
                        keys, rows = (P, slice(0, P)) if u == 0 else (SEQ, slice(P, SEQ))
                        if odd and u == 0:
                            pe.wait(eng)
                        for h in (odd, 2 + odd):
                            half = slice(HD * odd, HD * odd + HD)
                            c = h * P if u == 0 else (h // 2) * SEQ
                            mm = eng.matmul(bank[2 + u][:, c:c + keys],
                                            lhsT=headsT[half, q(h), rows], rhs=headsT[half, k(h), 0:keys],
                                            start=True, stop=True)
                        if odd:
                            mm.then_inc(scores, 2 if u == 0 else 1)
                        elif u == 0:
                            pe(mm)

            def attend_turn(A):
                for u in range(3):
                    eng.wait_ge(exped, 3 * A + (1 if u == 0 else 3))
                    for h in range(4):
                        if u == 0:
                            src = probs[:, 0, h * P:(h + 1) * P]
                        else:
                            c = (h // 2) * SEQ + (u - 1) * P
                            src = probs[:, 1 + h % 2, c:c + P]
                        mm = eng.transpose(bank[2 + u][:, h * P:(h + 1) * P], src, ident[:, :])
                    mm.then_inc(pT_ready, 1)

            def attend_values(A, v, dv):
                eng.wait_ge(pT_act, 2 * A + 4)
                eng.wait_ge(pT_dve, A + 2)
                eng.wait_ge(o_done, A + 2)
                for r in range(RT):
                    for h in range(4):
                        out = bank[5][:, (4 * r + h) * dv:(4 * r + h + 1) * dv] if dv == HD else \
                            bank[5 + r][:, h * dv:(h + 1) * dv]
                        for kt in range(r + 1):
                            mm = eng.matmul(out, lhsT=probsT[:, r + kt, h * P:(h + 1) * P], rhs=v(kt, h),
                                            start=(kt == 0), stop=(kt == r))
                mm.then_inc(pv_ready, 1)

            def ffn(p0, l):
                def gate_up(p, c):
                    eng.wait_ge(lo_ready[0], p + 2)
                    for r in range(RT):
                        if c is not None:
                            eng.wait_ge(gu_free, l * 2 * FF_STEPS + 2 * c - 1 + r)
                        for k in range(6):
                            mm = three(bank[r][:, :], k, slice(r * P, (r + 1) * P), 0, k * UNIT,
                                       start=(k == 0), stop=False)
                    mm.then_inc(used[0], 1)
                    eng.wait_ge(lo_ready[1], p + 2)
                    for r in range(RT):
                        for k in range(6, 8):
                            mm = three(bank[r][:, :], k, slice(r * P, (r + 1) * P), 1, (k - 6) * UNIT,
                                       start=False, stop=(k == 7))
                        mm.then_inc(gu_ready, 1)

                def down(c, first, last):
                    eng.wait_ge(ff_lo, l * 2 * FF_STEPS + 2 * c + 2)
                    three.act = ffT
                    for kk in range(2):
                        j, w0 = (kk, 0) if last else (1, (2 + 2 * kk) * UNIT)
                        if last:
                            eng.wait_ge(lo_ready[j], p0 + FF_STEPS + 2)
                        for r in range(RT):
                            for n in range(2):
                                mm = three(bank[2 + 2 * r + n][:, :], kk, slice(r * P, (r + 1) * P), j,
                                           w0 + n * UNIT, start=(first and kk == 0), stop=(last and kk == 1))
                                if last and kk == 1 and not (r == 1 and n == 1):
                                    mm.then_inc(down_ready, 1)
                        if last or kk == 1:
                            mm.then_inc(used[j], 1)
                    three.act = hT

                def turn(c, frees_slot=False):
                    for r in range(RT):
                        eng.wait_ge(gu_free, l * 2 * FF_STEPS + 2 * c + 1 + r)
                        for k in range(2):
                            mm = eng.transpose(bank[6 + r][:, k * P:(k + 1) * P],
                                               probs[:, r, k * P:(k + 1) * P], ident[:, :])
                            if frees_slot and r == 0 and k == 0:
                                mm.then_inc(used[1], 1)
                        mm.then_inc(ff_turned, 1)

                three.act = hT
                gate_up(p0, None)
                turn(0, frees_slot=True)
                gate_up(p0 + 1, 1)
                down(0, True, False)
                turn(1)
                with eng.Fori(2, FF_STEPS) as c:
                    gate_up(p0 + c, c)
                    down(c - 1, False, False)
                    turn(c)
                down(FF_STEPS - 1, False, True)

            eng.wait_ge(const_ready, 4)
            eng.sem_inc(used[0], 1)
            eng.sem_inc(used[1], 1)
            eng.sem_inc(pv_ready, 1)
            with eng.Fori(0, LAYERS) as l:
                p, A = l * PAIRS1, l * NGRP

                def pair_head(i, jj):
                    if jj == 0 and i > 0:
                        eng.wait_ge(z_act, l * 8 + i)
                        eng.wait_ge(z_dve, l * 8 + i)
                    chunk(p + i, jj, NARROW if i == 1 else COLS)

                def zcols(c0):
                    return lambda i, r: z[:, r, c0 + i * P:c0 + (i + 1) * P]

                turn_rows(l * 3)
                eng.wait_ge(turned_lo, l * 12 + 4)
                three.act = hT
                pair_head(0, 0); pair_head(0, 1)
                pair_head(1, 0); pair_head(1, 1)
                pair_head(2, 0); turn_heads(l, 0, zcols(IQ), 4)
                pair_head(2, 1); turn_heads(l, 1, lambda i, r: scr_ik(r), 1)
                pair_head(3, 0)
                for u in range(3):
                    index_scores(l, u)
                pair_head(3, 1)
                for u in range(3, 6):
                    index_scores(l, u)
                pair_head(4, 0); turn_heads(l, 2, zcols(SQ), 4)
                pair_head(4, 1)
                pair_head(5, 0); pair_head(5, 1); turn_heads(l, 3, zcols(DQ), 4)
                pair_head(6, 0)
                eng.wait_ge(idx_relu, l * 6 + 6)
                eng.wait_ge(heads_act, l * 6 + 3)
                eng.wait_ge(heads_dve, l * 5 + 2)
                attend_scores(A, lambda h: T_SQ + h // 2, lambda h: T_SK + h // 2)
                pair_head(6, 1); turn_heads(l, 4, zcols(DK), 4)
                attend_turn(A)
                pair_head(7, 0)
                attend_values(A, lambda kt, h: z[:, kt, SV + h * HD:SV + (h + 1) * HD], HD)
                eng.wait_ge(heads_act, l * 6 + 5)
                eng.wait_ge(heads_dve, l * 5 + 4)
                attend_scores(A + 1, lambda h: T_DQ + h // 2, lambda h: T_DK + h // 2)
                pair_head(7, 1)
                attend_turn(A + 1)
                attend_values(A + 1, lambda kt, h: z[:, kt, DV + (h // 2) * 2 * HD:DV + (h // 2 + 1) * 2 * HD], 2 * HD)
                attend_scores(A + 2, lambda h: T_DQ + 2 + h // 2, lambda h: T_DK + 2 + h // 2)
                eng.wait_ge(o_done, A + 4)
                turn_heads(l, 5, zcols(MQ), 4)
                attend_turn(A + 2)
                eng.wait_ge(heads_act, l * 6 + 6)
                eng.wait_ge(heads_dve, l * 5 + 5)
                attend_values(A + 2, lambda kt, h: z[:, kt, DV + (2 + h // 2) * 2 * HD:DV + (3 + h // 2) * 2 * HD], 2 * HD)
                attend_scores(A + 3, lambda h: T_MQ + h // 2, lambda h: T_MK + h // 2)
                attend_turn(A + 3)
                attend_values(A + 3, lambda kt, h: z[:, kt, MV + h * HD:MV + (h + 1) * HD], HD)
                turn_rows(l * 3 + 1)
                eng.wait_ge(turned_lo, l * 12 + 8)
                eng.wait_ge(z_act, l * 8 + 8)
                eng.wait_ge(z_dve, l * 8 + 8)
                three.act = mixT
                for i in range(2):
                    if i:
                        eng.wait_ge(out_added, l * 4 + 2)
                    chunk(p + 8 + i, 0); chunk(p + 8 + i, 1)
                three.act = hT
                turn_rows(l * 3 + 2)
                eng.wait_ge(turned_lo, l * 12 + 12)
                eng.wait_ge(out_added, l * 4 + 4)
                ffn(p + 10, l)
                pe.restart(eng)

            p, A = B2, LAYERS * NGRP

            def product_chunk(b, j, n=COLS):
                if j == 0 and b > 0:
                    for r in range(RT):
                        eng.wait_ge(free[r], product(b))
                chunk(p + b, j, n)

            def channel_chunk(b, j):
                if j == 0:
                    for r in range(RT):
                        eng.wait_ge(free[r], product(b))
                eng.wait_ge(lo_ready[j], p + b + 2)
                for c in range(4):
                    out = bank[c // 2][:, (c % 2) * SEQ:(c % 2 + 1) * SEQ]
                    for k in range(4):
                        w = slice(k * COLS + c * P, k * COLS + (c + 1) * P)
                        for n, (a, h) in enumerate(((whi, 0), (wlo, 0), (whi, 1))):
                            mm = eng.matmul(out, lhsT=a[j][:, w], rhs=hT[h][:, 4 * j + k, :],
                                            start=(j == 0 and k == 0 and n == 0 and c % 2 == 0),
                                            stop=(j == 1 and k == 3 and n == 2), skip_group_check=True)
                    if j == 1 and c == 1:
                        mm.then_inc(half_ready, 1)
                mm.then_inc(used[j], 1)

            def compress(b, j):
                c = 2 * (b - 6) + j
                if c == 0:
                    for r in range(RT):
                        eng.wait_ge(free[r], product(6))
                    eng.wait_ge(flat_lo, 1)
                eng.wait_ge(lo_ready[j], p + b + 2)
                three.act = flat
                for v in range(2):
                    for k in range(4):
                        mm = three(bank[v][0:COMP, 0:SEQ], 4 * c + k, slice(0, COMP), j, k * COLS + v * SEQ,
                                   start=(c == 0 and k == 0), stop=(c == 3 and k == 3), n=SEQ)
                    if c == 3 and v == 0:
                        mm.then_inc(half_ready, 1)
                mm.then_inc(used[j], 1)
                three.act = hT

            def wait_fill(n, at):
                if at:
                    eng.wait_ge(read67[n], at)

            def turn_four(src, at):
                for n in range(2):
                    wait_fill(n, at)
                    for q in range(2):
                        for r in range(RT):
                            mm = eng.transpose(bank[6 + n][:, (q * RT + r) * P:(q * RT + r + 1) * P],
                                               src(2 * n + q, r), ident[:, :])
                    mm.then_inc(filled, 1)

            def group_scores(i):
                g = i % 4
                attend_scores(A + i, lambda h: 2 * g + h // 2, lambda h: (T2_KS, T2_KW)[i // 4] + g)

            def group_values(i):
                c0 = (VS2, VW2)[i // 4] + (i % 4) * HD
                attend_values(A + i, lambda kt, h: z[:, kt, c0:c0 + HD], HD)

            turn_rows(6)
            eng.wait_ge(turned_lo, 28)
            three.act = hT
            product_chunk(0, 0); product_chunk(0, 1)
            product_chunk(1, 0); product_chunk(1, 1)
            eng.wait_ge(dup_ready, 1)
            turn_four(lambda g, r: scr[:, r, g * P:(g + 1) * P], 0)
            product_chunk(2, 0)
            eng.wait_ge(dup_ready, 2)
            turn_four(lambda g, r: probs[:, r, g * P:(g + 1) * P], 1)
            product_chunk(2, 1)
            product_chunk(3, 0); product_chunk(3, 1)
            for n in range(2):
                if n == 0:
                    for r in range(RT):
                        eng.wait_ge(free[r], 3)
                turn_four(lambda i, r, n=n: z[:, r, Q2 + (4 * n + i) * P:Q2 + (4 * n + i + 1) * P], 2 + n)
            product_chunk(4, 0, GATES); product_chunk(4, 1, GATES)
            product_chunk(5, 0)
            eng.wait_ge(dup_ready, 3)
            turn_four(lambda g, r: scr[:, r, g * P:(g + 1) * P], 4)
            product_chunk(5, 1)
            compress(6, 0); compress(6, 1)
            eng.wait_ge(dup_ready, 4)
            turn_four(lambda g, r: probs[:, r, g * P:(g + 1) * P], 5)
            compress(7, 0); compress(7, 1)
            product_chunk(8, 0)
            eng.wait_ge(free[0], 7)
            eng.wait_ge(free[1], 7)
            wait_fill(1, 6)
            for i in range(4):
                mm = eng.transpose(bank[7][:, i * COMP:(i + 1) * COMP], sqr[0:COMP, i * P:(i + 1) * P],
                                   ident[0:COMP, 0:COMP])
            mm.then_inc(filled, 1)
            product_chunk(8, 1)
            eng.wait_ge(read67[1], 7)
            wait_fill(0, 6)
            for k in range(2):
                mm = eng.matmul(bank[6][:, 0:COMP // 2], lhsT=wk2[:, k, :], rhs=hidT[:, k * COMP:k * COMP + COMP // 2],
                                start=(k == 0), stop=(k == 1))
            mm.then_inc(filled, 1)
            eng.wait_ge(pad_ready, 1)
            wait_fill(1, 7)
            for g in range(KV_GROUPS):
                for k in range(2):
                    mm = eng.matmul(bank[7][:, g * HD:(g + 1) * HD], lhsT=scr[:, k, g * P:(g + 1) * P],
                                    rhs=wv2[:, k, :], start=(k == 0), stop=(k == 1))
            mm.then_inc(filled, 1)
            product_chunk(9, 0)
            eng.wait_ge(read67[0], 7)
            for odd in range(2):
                half = slice(HD * odd, HD * odd + HD)
                for r in range(RT):
                    for i in range(8):
                        g = i // 2
                        mm = eng.matmul(bank[2 + odd][:, r * P + i * 16:r * P + i * 16 + CMP],
                                        lhsT=headsT[half, i, r * P:(r + 1) * P],
                                        rhs=headsT[half, T2_KC, g * CMP:(g + 1) * CMP], start=True, stop=True)
                mm.then_inc(cs_ready, 1)
            product_chunk(9, 1)
            eng.wait_ge(cn_ready, 1)
            for r in range(RT):
                for g in range(KV_GROUPS):
                    mm = eng.transpose(bank[2 + r][:, g * P:(g + 1) * P], probs[:, r, g * P:(g + 1) * P], ident[:, :])
                mm.then_inc(ct_ready, 1)
            product_chunk(10, 0)
            eng.wait_ge(cT_act, 1)
            eng.wait_ge(cT_dve, 1)
            eng.wait_ge(read67[1], 8)
            for r in range(RT):
                if r:
                    eng.wait_ge(cv_done, 1)
                for g in range(KV_GROUPS):
                    mm = eng.matmul(bank[4 + g // 2][:, (g % 2) * SEQ:(g % 2 + 1) * SEQ],
                                    lhsT=probsT[:, r, g * P:(g + 1) * P], rhs=headsT[:, T2_V + g, :],
                                    start=True, stop=True)
                mm.then_inc(cv_ready, 1)
            product_chunk(10, 1)
            eng.wait_ge(cv_done, 2)
            group_scores(0)
            product_chunk(11, 0)
            attend_turn(A)
            product_chunk(11, 1)
            group_values(0); group_scores(1)
            eng.wait_ge(ws_ready, 1)
            for r in range(RT):
                eng.wait_ge(vn_ready, r + 1)
                for g in range(4):
                    if g % 2 == 0:
                        wait_fill(g // 2, (7, 8)[g // 2] + r)
                    mm = eng.matmul(bank[6 + g // 2][:, (g % 2) * SEQ:(g % 2 + 1) * SEQ], lhsT=w_s[:, g, :],
                                    rhs=z[:, r, g * SEQ:(g + 1) * SEQ], start=True, stop=True)
                    if g % 2:
                        mm.then_inc(filled, 1)
            product_chunk(12, 0)
            attend_turn(A + 1)
            product_chunk(12, 1)
            group_values(1); group_scores(2)
            turn_rows(7, z[:, :, U2:U2 + D])
            eng.wait_ge(turned_lo, 32)
            three.act = mixT
            product_chunk(13, 0)
            attend_turn(A + 2)
            product_chunk(13, 1)
            three.act = hT
            for b, i in ((14, 2), (15, 3), (16, 4), (17, 5), (18, 6), (19, 7)):
                one = channel_chunk if b >= 16 else product_chunk
                group_values(i); group_scores(i + 1) if i < 7 else None
                if b == 15:
                    three.act = mixT
                one(b, 0)
                if i < 7:
                    attend_turn(A + i + 1)
                one(b, 1)
                three.act = hT
            eng.wait_ge(rg_loaded, 32)

            def gates(c):
                eng.wait_ge(xc_ready, c + 1)
                if c < 2:
                    eng.wait_ge(turned_lo, 32)
                wait_fill(c % 2, (9, 10)[c % 2] + c // 2)
                for v in range(2):
                    for h in range(2):
                        half = slice(HD * h, HD * h + HD)
                        w = z[half, v, KC2 + c * HD:KC2 + (c + 1) * HD]
                        mm = eng.matmul(bank[6 + c % 2][half, v * SEQ:(v + 1) * SEQ], lhsT=w,
                                        rhs=channels(c)[half, :], start=True, stop=True)
                mm.then_inc(filled, 1)

            product_chunk(20, 0)
            for c in range(4):
                gates(c)
            product_chunk(20, 1)
            for c in range(4, 8):
                gates(c)
            eng.wait_ge(read67[0], 13)
            eng.wait_ge(read67[1], 14)
            turn_rows(8)
            eng.wait_ge(turned_lo, 36)
            for b in range(21, 28):
                three.act = (mixT if b % 2 else hT)
                if b == 25:
                    eng.wait_ge(yc_lo, 1)
                product_chunk(b, 0); product_chunk(b, 1)
            turn_rows(9, z[:, :, U2:U2 + D])
            eng.wait_ge(turned_lo, 40)
            three.act = mixT
            for b in (28, 29):
                product_chunk(b, 0); product_chunk(b, 1)
            three.act = hT
            turn_rows(10)
            eng.wait_ge(turned_lo, 44)
            for r in range(RT):
                eng.wait_ge(free[r], product(30))
            ffn(p + PAIRS2, LAYERS)

        @block.scalar
        def _(eng):
            def split_hi(p, j, n):
                eng.wait_ge(raw_loaded[j], 16 * p + 16)
                eng.wait_ge(used[j], p + 1)
                eng.activation(whi[j][:, 0:n], raw[j][:, 0:n], ACT.Copy).then_inc(hi_ready[j], 1)

            def norm_stats(i):
                for r in range(RT):
                    act(eng.activation(mix[:, r, :], x[:, r, :], ACT.Square, accum_out=ssq[:, r:r + 1]))
                act.wait(eng)
                act(eng.activation(ssq[:, 2:4], ssq[:, 0:2], ACT.Ln, bias=eps[:, 0:1], scale=1.0 / D))
                act.wait(eng)
                eng.activation(ssq[:, 4:6], ssq[:, 2:4], ACT.Exp, scale=-0.5).then_inc(rs_ready, 1)

            def turned_hi_copy(i, dst, scale=1.0):
                for r in range(RT):
                    for h in range(2):
                        eng.wait_ge(turned, i * 4 + 2 * r + h + 1)
                        eng.activation(dst[0][:, 4 * h:4 * h + 4, r * P:(r + 1) * P],
                                       bank[6 + h][:, :].rearrange("p (k c) -> p k c", k=4),
                                       ACT.Copy, scale=scale).then_inc(turned_hi, 1)

            def copy_z0(p, l, i, c0, n=COLS):
                eng.wait_ge(half_ready, p)
                eng.activation(z[:, 0, c0:c0 + n], bank[0][:, 0:n], ACT.Copy).then_inc(z_act, 1)

            def head_stats(l, s):
                for r in range(RT):
                    n = 2 * s + r
                    c0 = (SQ, DQ, DK, MQ)[s]
                    if r == 0:
                        eng.wait_ge(z_dve, l * 8 + (3, 5, 6, 8)[s])
                        eng.wait_ge(z_act, l * 8 + (3, 5, 6, 8)[s])
                    if s or r:
                        eng.wait_ge(ssq_ready, l * 8 + n)
                    eng.activation(sqr[:, :], z[:, r, c0:c0 + COLS], ACT.Square).then_inc(squares, 1)
                    eng.wait_ge(ssq_ready, l * 8 + n + 1)
                    act(eng.activation(ssq[:, 8:16], hss[:, r, :], ACT.Ln, bias=eps[:, 0:1], scale=1.0 / HD))
                    act.wait(eng)
                    eng.activation(hrs[:, r, :], ssq[:, 8:16], ACT.Exp, scale=-0.5).then_inc(hrs_ready, 1)

            def heads_copy(l, s):
                n = (0, 2, 3, 5, 7, 9)[s]
                eng.wait_ge(heads_turned, l * 11 + n + 1)
                t0 = (T_IQ, T_IK, T_SQ, T_DQ, T_DK, T_MQ)[s]
                m = 1 if s == 1 else 2
                eng.activation(headsT[:, t0:t0 + m, :], bank[6][:, 0:m * SEQ].rearrange("p (m c) -> p m c", m=m),
                               ACT.Copy).then_inc(heads_act, 1)

            def index_relu(l, u):
                eng.wait_ge(idx_ready, l * 6 + u + 1)
                if u >= 3:
                    eng.wait_ge(idx_acc, l * 6 + u - 2)
                eng.activation(probs[:, u % 3, :], bank[2 + u % 3][:, :], ACT.Relu, scale=HD ** -0.5)\
                   .then_inc(idx_relu, 1)

            def attend_exp(A, par):
                eng.wait_ge(o_done, A + 1)
                for u in range(3):
                    eng.wait_ge(masked, 3 * A + u + 1)
                    heads = range(4) if u == 0 else range(2)
                    keys = P if u == 0 else SEQ
                    for h in heads:
                        c = h if u == 0 else 4 + 2 * h + u - 1
                        part = probs[:, u, h * keys:(h + 1) * keys]
                        ins = eng.activation(part, part, ACT.Exp, bias=nmax[:, c:c + 1],
                                             accum_out=sums[:, par, c:c + 1])
                        if h == heads[-1]:
                            ins.then_inc(exped, 1)
                        else:
                            act(ins)

            def attend_copy(A):
                for u in range(2):
                    eng.wait_ge(pT_ready, 3 * A + u + 1)
                    eng.wait_ge(pv_ready, A + 1)
                    eng.activation(probsT[:, u, :], bank[2 + u][:, :], ACT.Copy).then_inc(pT_act, 1)

            def diff_stats(l, i):
                eng.wait_ge(dsq, l * 2 + i + 1)
                act(eng.activation(ssq[:, 6:10], dstat[:, 0:4], ACT.Ln, bias=eps[:, 0:1], scale=1.0 / (2 * HD)))
                act.wait(eng)
                eng.activation(dstat[:, 4:8], ssq[:, 6:10], ACT.Exp, scale=-0.5).then_inc(drs, 1)

            def ffn(p0, l, after_n):
                def step(c, n0, n1):
                    split_hi(p0 + c + 1, 0, n0)
                    for r in range(RT):
                        n = l * 2 * FF_STEPS + 2 * c + r
                        eng.wait_ge(gu_ready, n + 1)
                        eng.activation(sqr[:, r * FF_STEP:(r + 1) * FF_STEP], bank[r][:, 0:FF_STEP],
                                       ACT.Silu).then_inc(silu_ready, 1)
                    split_hi(p0 + c + 1, 1, n1)
                    for r in range(RT):
                        n = l * 2 * FF_STEPS + 2 * c + r
                        eng.wait_ge(ff_turned, n + 1)
                        eng.activation(ffT[0][:, :, r * P:(r + 1) * P],
                                       bank[6 + r][:, 0:2 * P].rearrange("p (k c) -> p k c", k=2),
                                       ACT.Copy).then_inc(ff_hi, 1)

                eng.preload_act_table(ACT.Silu)
                with eng.Fori(0, FF_STEPS - 1) as c:
                    step(c, ffn_elements(1, 0), ffn_elements(1, 1))
                step(FF_STEPS - 1, 2 * UNIT, 2 * UNIT)
                eng.preload_act_table_set(LN_EXP)
                if after_n is not None:
                    for j in range(2):
                        after_n(p0 + FF_STEPS + 1, j)

            eng.wait_ge(const_ready, 4)
            eng.wait_ge(x_loaded, 16 * RT)
            eng.sem_inc(pT_act, 2)
            for j in range(2):
                split_hi(0, j, 4 * UNIT)
            act.restart(eng)
            eng.preload_act_table_set(LN_EXP)
            with eng.Fori(0, LAYERS) as l:
                p, A = l * PAIRS1, l * NGRP
                hi = lambda i, j: split_hi(p + i, j, 4 * (NARROW if i == 1 else COLS))
                hr = lambda i: l * HALVES + i + 1
                norm_stats(l)
                turned_hi_copy(l * 3, hT)
                hi(1, 0); copy_z0(hr(0), l, 0, IQ); hi(1, 1)
                hi(2, 0); copy_z0(hr(1), l, 1, IK, NARROW); hi(2, 1)
                eng.wait_ge(lam_sum, l + 1)
                eng.activation(lam[:, 2:4], lam[:, 0:2], ACT.Exp).then_inc(lam_exp, 1)
                hi(3, 0); heads_copy(l, 0); copy_z0(hr(2), l, 2, SQ); hi(3, 1); heads_copy(l, 1)
                hi(4, 0)
                for u in range(3):
                    index_relu(l, u)
                copy_z0(hr(3), l, 3, MV); hi(4, 1)
                for u in range(3, 6):
                    index_relu(l, u)
                head_stats(l, 0)
                hi(5, 0); heads_copy(l, 2); copy_z0(hr(4), l, 4, DQ); hi(5, 1)
                head_stats(l, 1)
                hi(6, 0); copy_z0(hr(5), l, 5, DK); hi(6, 1); heads_copy(l, 3)
                head_stats(l, 2)
                hi(7, 0); attend_exp(A, 0); copy_z0(hr(6), l, 6, DV); hi(7, 1); heads_copy(l, 4); attend_copy(A)
                hi(8, 0); attend_exp(A + 1, 1); copy_z0(hr(7), l, 7, MQ); hi(8, 1)
                head_stats(l, 3)
                attend_copy(A + 1)
                diff_stats(l, 0)
                attend_exp(A + 2, 0)
                heads_copy(l, 5)
                attend_copy(A + 2)
                diff_stats(l, 1)
                attend_exp(A + 3, 1)
                attend_copy(A + 3)
                turned_hi_copy(l * 3 + 1, mixT)
                hi(9, 0); hi(9, 1)
                for j in range(2):
                    split_hi(p + 10, j, ffn_elements(0, j))
                eng.wait_ge(out_added, l * 4 + 4)
                norm_stats(l)
                turned_hi_copy(l * 3 + 2, hT)

                def after(pp, j):
                    split_hi(pp, j, 4 * UNIT)
                ffn(p + 10, l, after)
                act.restart(eng)
                eng.wait_ge(down_added, l * 4 + 4)

            A = LAYERS * NGRP

            def hi2(b, j):
                n = ffn_elements(0, j) if b == PAIRS2 else 4 * (GATES if b == 4 else COLS)
                split_hi(B2 + b, j, n)

            def whole(b, r):
                if r == 0:
                    eng.wait_ge(half_ready, half_of(b))
                else:
                    eng.wait_ge(used[1], B2 + b + 2)

            def take(b, r, dst, func, n=COLS, scale=1.0):
                whole(b, r)
                eng.activation(dst, bank[r][:, 0:n], func, scale=scale).then_inc(free[r], 1)

            def fill_copy(n, count, t0):
                eng.wait_ge(filled, count)
                eng.activation(headsT[:, t0:t0 + 2, :], bank[6][:, :].rearrange("p (m c) -> p m c", m=2),
                               ACT.Copy).then_inc(read67[0], 1)

            def branch_gate(b, r):
                n = {12: 0, 14: 1, 20: 2, 22: 3, 24: 4, 26: 5}[b]
                if n:
                    eng.wait_ge(merged_done, 2 * n)
                take(b, r, scr[:, r, :], ACT.Tanh, scale=0.5)

            def gates(c):
                eng.wait_ge(filled, F_GATE + c)
                if c >= 2:
                    eng.wait_ge(gx_done, c - 1)
                b, buf = bank[6 + c % 2], probs[:, c % 2, :]
                act(eng.activation(buf[:, 0:SEQ], b[:, 0:SEQ], ACT.Tanh, scale=0.5, bias=sp[:, 88 + c:89 + c]))
                eng.activation(buf[:, SEQ:2 * SEQ], b[:, SEQ:2 * SEQ], ACT.Tanh, scale=0.5,
                               bias=sp[:, 96 + c:97 + c]).then_inc(read67[c % 2], 1)
                act.wait(eng)
                eng.activation(headsT[:, c, :], buf[:, 0:SEQ], ACT.Tanh, scale=sp[:, 80 + c:81 + c],
                               bias=sp[:, 80 + c:81 + c]).then_inc(u_ready, 1)

            def row_stats(i, src, junk):
                eng.preload_act_table_set(LN_EXP)
                for r in range(RT):
                    act(eng.activation(junk[:, r, 0:D], src[:, r, 0:D], ACT.Square, accum_out=ssq[:, r:r + 1]))
                act.wait(eng)
                act(eng.activation(ssq[:, 2:4], ssq[:, 0:2], ACT.Ln, bias=eps[:, 0:1], scale=1.0 / D))
                act.wait(eng)
                eng.activation(ssq[:, 4:6], ssq[:, 2:4], ACT.Exp, scale=-0.5).then_inc(rs_ready, 1)

            norm_stats(4)
            eng.wait_ge(sp_abs, 1)
            eng.activation(sp[:, 8:16], sp[:, 0:8], ACT.Exp).then_inc(sp_exp, 1)
            eng.wait_ge(sp_one, 1)
            eng.activation(sp[:, 24:32], sp[:, 16:24], ACT.Ln).then_inc(sp_ln, 1)
            turned_hi_copy(6, hT)
            hi2(1, 0); take(0, 0, z[:, 0, KC2:KC2 + COLS], ACT.Copy); hi2(1, 1)
            hi2(2, 0); take(1, 0, z[:, 0, Q2:Q2 + COLS], ACT.Copy, scale=HD ** -0.5); hi2(2, 1)
            hi2(3, 0); take(2, 0, z[:, 0, Q2 + COLS:Q2 + D], ACT.Copy, scale=HD ** -0.5); hi2(3, 1)
            hi2(4, 0); take(3, 0, z[:, 0, KS2:KS2 + COLS], ACT.Copy); hi2(4, 1)
            fill_copy(0, F_Q, 0)
            fill_copy(0, F_Q + 2, 4)
            hi2(5, 0)
            take(4, 0, z[:, 0, G2:G2 + GATES], ACT.Tanh, GATES, 0.5)
            take(4, 1, z[:, 1, G2:G2 + GATES], ACT.Tanh, GATES, 0.5)
            hi2(5, 1)
            eng.wait_ge(flat_done, 1)
            eng.activation(flat[0].rearrange("p j m -> p (j m)"), flat_f, ACT.Copy).then_inc(flat_hi, 1)
            hi2(6, 0); fill_copy(0, F_SK, T2_KS); take(5, 0, z[:, 0, KW2:KW2 + COLS], ACT.Copy); hi2(6, 1)
            hi2(7, 0); fill_copy(0, F_WK, T2_KW); hi2(7, 1)
            hi2(8, 0)
            for v in range(2):
                whole(7, v)
                eng.activation(sqr[0:COMP, v * SEQ:(v + 1) * SEQ], bank[v][0:COMP, 0:SEQ],
                               ACT.Gelu_apprx_tanh).then_inc(free[v], 1)
            hi2(8, 1)
            hi2(9, 0)
            eng.wait_ge(filled, F_HT)
            eng.activation(hidT, bank[7][:, 0:4 * COMP], ACT.Copy).then_inc(read67[1], 1)
            eng.wait_ge(filled, F_Q + 3)
            take(8, 0, z[:, 0, 0:COLS], ACT.Gelu_apprx_tanh)
            take(8, 1, z[:, 1, 0:COLS], ACT.Gelu_apprx_tanh)
            hi2(9, 1)
            eng.wait_ge(filled, F_KC)
            eng.activation(headsT[:, T2_KC, 0:COMP // 2], bank[6][:, 0:COMP // 2], ACT.Copy).then_inc(read67[0], 1)
            eng.wait_ge(cm_ready, 1)
            wide = probs[:, 0:2, :].rearrange("p r (h n) -> p (r h) n", n=32)[:, :, 0:CMP]
            eng.activation(wide, wide, ACT.Exp).then_inc(ce_ready, 1)
            hi2(10, 0)
            take(9, 0, z[:, 0, COLS:D], ACT.Gelu_apprx_tanh)
            take(9, 1, z[:, 1, COLS:D], ACT.Gelu_apprx_tanh)
            hi2(10, 1)
            eng.wait_ge(ct_ready, 1)
            eng.activation(probsT[:, 0, :], bank[2][:, :], ACT.Copy).then_inc(cT_act, 1)
            eng.preload_act_table_set(LN_EXP)
            eng.wait_ge(var_ready, 1)
            act(eng.activation(bn[:, 30:32], bn[:, 24:28].rearrange("p (r s) -> p r s", s=2)[:, :, 1], ACT.Ln,
                               bias=eps[:, 0:1]))
            act.wait(eng)
            eng.activation(bn[:, 28:30], bn[:, 30:32], ACT.Exp, scale=-0.5).then_inc(vrs_ready, 1)
            hi2(11, 0)
            take(10, 0, z[:, 0, U2:U2 + COLS], ACT.Gelu_apprx_tanh)
            take(10, 1, z[:, 1, U2:U2 + COLS], ACT.Gelu_apprx_tanh)
            hi2(11, 1)
            attend_exp(A, 0)
            hi2(12, 0); attend_copy(A)
            take(11, 0, z[:, 0, U2 + COLS:U2 + D], ACT.Gelu_apprx_tanh)
            take(11, 1, z[:, 1, U2 + COLS:U2 + D], ACT.Gelu_apprx_tanh)
            hi2(12, 1)
            for b in range(12, 19):
                i = b - 11
                attend_exp(A + i, i % 2)
                hi2(b + 1, 0)
                attend_copy(A + i)
                if b in (12, 14):
                    branch_gate(b, 0); branch_gate(b, 1)
                if b == 18:
                    for r in range(2):
                        take(b, r, headsT[:, 8 + 2 * r:10 + 2 * r, :].rearrange("p a c -> p (a c)"), ACT.Gelu_apprx_tanh)
                hi2(b + 1, 1)
                if b == 12:
                    turned_hi_copy(7, mixT)
            hi2(20, 0)
            for r in range(2):
                take(19, r, headsT[:, 12 + 2 * r:14 + 2 * r, :].rearrange("p a c -> p (a c)"), ACT.Gelu_apprx_tanh)
            hi2(20, 1)
            hi2(21, 0)
            for c in range(4):
                gates(c)
            branch_gate(20, 0); branch_gate(20, 1)
            hi2(21, 1)
            for c in range(4, 8):
                gates(c)
            turned_hi_copy(8, mixT)
            hi2(22, 0); hi2(22, 1)
            eng.wait_ge(u_read, 1)
            eng.activation(headsT[:, 0:8, :], headsT[:, 0:8, :], ACT.Sqrt).then_inc(root_ready, 1)
            hi2(23, 0); branch_gate(22, 0); branch_gate(22, 1); hi2(23, 1)
            hi2(24, 0); hi2(24, 1)
            hi2(25, 0); branch_gate(24, 0); branch_gate(24, 1); hi2(25, 1)
            eng.wait_ge(yc_ready, 1)
            eng.wait_ge(used[1], B2 + 23 + 2)
            eng.activation(mixT[0][:, :, :], headsT[:, 0:8, :], ACT.Copy).then_inc(yc_hi, 1)
            hi2(26, 0); hi2(26, 1)
            hi2(27, 0); branch_gate(26, 0); branch_gate(26, 1); hi2(27, 1)
            hi2(28, 0); hi2(28, 1)
            turned_hi_copy(9, mixT, scale=0.5)
            hi2(29, 0); take(28, 0, mix[:, 0, 0:COLS], ACT.Copy); hi2(29, 1)
            hi2(30, 0); take(29, 0, mix[:, 0, COLS:D], ACT.Copy); hi2(30, 1)
            for r in range(RT):
                eng.wait_ge(free[r], product(30))
            row_stats(5, mix, z)
            eng.wait_ge(x_added, RT)
            row_stats(6, x, z)
            turned_hi_copy(10, hT)
            ffn(B2 + PAIRS2, LAYERS, None)
            eng.wait_ge(down_added, 4 * LAYERS + 4)
            row_stats(7, mix, z)

        @block.vector
        def _(eng):
            def split_lo(p, j, n):
                eng.wait_ge(hi_ready[j], p + 1)
                eng.tensor_tensor(wlo[j][:, 0:n], raw[j][:, 0:n], whi[j][:, 0:n].bitcast(F32),
                                  ALU.subtract).then_inc(lo_ready[j], 1)

            def norm_rows(i, gain_i=None):
                eng.wait_ge(rs_ready, i + 1)
                eng.wait_ge(gain_loaded, 16 * (i if gain_i is None else gain_i) + 16)
                for r in range(RT):
                    eng.scalar_tensor_tensor(out=mix[:, r, :], in0=x[:, r, :], scalar=ssq[:, 4 + r:5 + r],
                                             in1=gain[:, :], op0=ALU.mult, op1=ALU.mult)\
                       .then_inc(rows_ready, 1)

            def turned_lo_copy(i, dst, scale=None):
                for r in range(RT):
                    for h in range(2):
                        n = i * 4 + 2 * r + h
                        eng.wait_ge(turned_hi, n + 1)
                        cols = slice(r * P, (r + 1) * P)
                        high = dst[0][:, 4 * h:4 * h + 4, cols].bitcast(F32)
                        low = dst[1][:, 4 * h:4 * h + 4, cols]
                        src = bank[6 + h][:, :].rearrange("p (k c) -> p k c", k=4)
                        if scale is None:
                            ins = eng.tensor_tensor(low, src, high, ALU.subtract)
                        else:
                            ins = eng.scalar_tensor_tensor(out=low, in0=src, scalar=scale, in1=high,
                                                           op0=ALU.mult, op1=ALU.subtract)
                        ins.then_inc(turned_lo, 1)

            def copy_z1(p, c0, n=COLS):
                eng.wait_ge(used[1], p + 2)
                eng.tensor_copy(z[:, 1, c0:c0 + n], bank[1][:, 0:n]).then_inc(z_dve, 1)

            def tables(l):
                eng.wait_ge(par_loaded, 64 * l + 64)
                dve(eng.tensor_scalar(hgain[:, 0:3, :], hgain[:, 0:3, :], HD ** -0.5, None, ALU.mult))
                dve.wait(eng)
                h = HD // 2
                for r in range(RT):
                    dve(eng.tensor_tensor(gain_c[:, r], hgain[:, :, :],
                                          rope_c[:, r, :].unsqueeze(1).to_broadcast([P, 6, HD]), ALU.mult))
                    for a, b in ((0, h), (h, 0)):
                        dve(eng.tensor_tensor(gain_s[:, r, :, a:a + h], hgain[:, :, b:b + h],
                                              rope_s[:, r, a:a + h].unsqueeze(1).to_broadcast([P, 6, h]), ALU.mult))
                dve(eng.tensor_tensor(scr[:, 0, 0:HD], lamp[:, 0, :], lamp[:, 1, :], ALU.mult))
                dve(eng.tensor_tensor(scr[:, 0, HD:2 * HD], lamp[:, 2, :], lamp[:, 3, :], ALU.mult))
                dve.wait(eng)
                eng.tensor_reduce(lam[:, 0:2], scr[:, 0, 0:2 * HD].rearrange("p (a d) -> p a d", a=2), AX.X,
                                  ALU.add).then_inc(lam_sum, 1)

            def lambda_value(l):
                eng.wait_ge(lam_exp, l + 1)
                dve(eng.tensor_tensor(lam[:, 0:1], lam[:, 2:3], lam[:, 3:4], ALU.subtract))
                dve.wait(eng)
                dve(eng.tensor_tensor(lam[:, 0:1], lam[:, 0:1], lam_c[:, 0:1], ALU.add))
                dve(eng.tensor_scalar(sub_g[:, :], sub_g[:, :], lam_c[:, 1:2], None, ALU.mult))
                dve.wait(eng)

            def rotate(src, ct, st, n, dst=None, scale=None, last=None):
                h = HD // 2
                a = scr[:, 0, 0:n * HD].rearrange("p (n d) -> p n d", d=HD)
                b = scr[:, 1, 0:n * HD].rearrange("p (n d) -> p n d", d=HD)
                m = len(ct)
                for i in range(m):
                    hs = slice(i * n // m, (i + 1) * n // m)
                    w = n // m
                    dve(eng.tensor_tensor(a[:, hs, :], src[:, hs, :], ct[i].unsqueeze(1).to_broadcast([P, w, HD]), ALU.mult))
                    for u, v in ((0, h), (h, 0)):
                        dve(eng.tensor_tensor(b[:, hs, u:u + h], src[:, hs, v:v + h],
                                              st[i][:, u:u + h].unsqueeze(1).to_broadcast([P, w, h]), ALU.mult))
                dve.wait(eng)
                out = src if dst is None else dst
                if scale is None:
                    ins = eng.tensor_tensor(out, a, b, ALU.add)
                else:
                    dve(eng.tensor_tensor(a, a, b, ALU.add))
                    dve.wait(eng)
                    eng.wait_ge(hrs_ready, scale[0])
                    ins = eng.tensor_tensor(out, a, scale[1], ALU.mult)
                if last is not None:
                    ins.then_inc(last, 1)
                else:
                    dve(ins)
                    dve.wait(eng)

            def prep_index_q(l):
                eng.wait_ge(z_act, l * 8 + 1)
                for r in range(RT):
                    src = z[:, r, IQ:IQ + COLS].rearrange("p (n d) -> p n d", d=HD)
                    rotate(src, [rope_c[:, r, :]], [rope_s[:, r, :]], 8, last=prep if r else None)

            def prep_index_k(l):
                eng.wait_ge(z_act, l * 8 + 2)
                eng.wait_ge(prep, l * 6 + 1)
                for r in range(RT):
                    src = z[:, r, IK:IK + HD].rearrange("p (n d) -> p n d", d=HD)
                    rotate(src, [rope_c[:, r, :]], [rope_s[:, r, :]], 1)
                    dve(eng.tensor_scalar(z[:, r, IW:IW + IDX_HEADS], z[:, r, IW:IW + IDX_HEADS],
                                          IDX_HEADS ** -0.5, None, ALU.mult))
                dve.wait(eng)
                dve(eng.tensor_copy(scr_ik(0).rearrange("p (a d) -> p a d", a=2),
                                    z[:, 0, IK:IK + HD].unsqueeze(1).to_broadcast([P, 2, HD])))
                eng.tensor_copy(scr_ik(1).rearrange("p (a d) -> p a d", a=2),
                                z[:, 1, IK:IK + HD].unsqueeze(1).to_broadcast([P, 2, HD])).then_inc(prep, 1)

            def prep_heads(l, s):
                c0 = (SQ, DQ, DK, MQ)[s]
                gains = ((2, 5), (1,), (4,), (0, 3))[s]
                if s == 0:
                    eng.wait_ge(heads_turned, l * 11 + 3)
                for r in range(RT):
                    n = l * 8 + 2 * s + r
                    eng.wait_ge(squares, n + 1)
                    eng.tensor_reduce(hss[:, r, :], sqr[:, :].rearrange("p (n d) -> p n d", d=HD), AX.X,
                                      ALU.add).then_inc(ssq_ready, 1)
                    src = z[:, r, c0:c0 + COLS].rearrange("p (n d) -> p n d", d=HD)

                    rotate(src, [gain_c[:, r, g, :] for g in gains], [gain_s[:, r, g, :] for g in gains], 8,
                           scale=(n + 1, hrs[:, r, :].unsqueeze(2).to_broadcast([P, 8, HD])),
                           last=prep if r else None)

            def heads_copy(l, s):
                n = (0, None, 3, 5, 7, 9)[s]
                eng.wait_ge(heads_turned, l * 11 + n + 2)
                t0 = (T_IQ, None, T_SQ, T_DQ, T_DK, T_MQ)[s] + 2
                eng.tensor_copy(headsT[:, t0:t0 + 2, :], bank[7][:, :].rearrange("p (m c) -> p m c", m=2))\
                   .then_inc(heads_dve, 1)

            def index_sum(l, u):
                eng.wait_ge(idx_relu, l * 6 + u + 1)
                r, keys = (0, P) if u < 2 else (1, SEQ)
                acc = index[:, 0:P] if u < 2 else index[:, P:3 * P]
                for i, h in enumerate(index_heads(u)):
                    part, w = probs[:, u % 3, i * keys:(i + 1) * keys], z[:, r, IW + h:IW + h + 1]
                    if h == 0:
                        ins = eng.tensor_scalar(acc, part, w, None, ALU.mult)
                    else:
                        ins = eng.scalar_tensor_tensor(out=acc, in0=part, scalar=w, in1=acc, op0=ALU.mult,
                                                       op1=ALU.add)
                    if i == (3 if u < 2 else 1):
                        ins.then_inc(idx_acc, 1)
                        eng.wait_ge(idx_acc, l * 6 + u + 1)
                    else:
                        dve(ins)
                        dve.wait(eng)

            def topk_rounds(a, b):
                if a == 0:
                    dve(eng.tensor_tensor(index[:, :], index[:, :], causal[:, :], ALU.add))
                    dve.wait(eng)
                for _ in range(a, b):
                    for r, part in enumerate((index[:, 0:P], index[:, P:3 * P])):
                        dve(eng.max(top8[:, r, :], part))
                    dve.wait(eng)
                    for r, part in enumerate((index[:, 0:P], index[:, P:3 * P])):
                        dve(eng.match_replace(part, top8[:, r, :], part, TAKEN))
                    dve.wait(eng)

            def topk_mask():
                dve(eng.tensor_scalar(chosen[:, :], index[:, :], TAKEN / 2, NEG, ALU.is_gt, ALU.mult))
                dve.wait(eng)
                dve(eng.tensor_tensor(chosen[:, :], chosen[:, :], causal[:, :], ALU.add))
                dve.wait(eng)

            def attend_mask(A, mask):
                for u in range(3):
                    eng.wait_ge(scores, 3 * A + u + 1)
                    n, keys = (4, P) if u == 0 else (2, SEQ)
                    m = mask[:, 0:P] if u == 0 else mask[:, P:3 * P]
                    part = probs[:, u, :].rearrange("p (n k) -> p n k", n=n)
                    dve(eng.tensor_tensor(part, bank[2 + u][:, :].rearrange("p (n k) -> p n k", n=n),
                                          m.unsqueeze(1).to_broadcast([P, n, keys]), ALU.add))
                    dve.wait(eng)
                    top = nmax[:, 0:4] if u == 0 else \
                        nmax[:, 4:8].rearrange("p (n two) -> p n two", two=2)[:, :, u - 1]
                    eng.tensor_reduce(top, part, AX.X, ALU.max, negate=True).then_inc(masked, 1)

            def attend_copy(A):
                eng.wait_ge(pT_ready, 3 * A + 3)
                eng.wait_ge(pv_ready, A + 1)
                eng.tensor_copy(probsT[:, 2, :], bank[4][:, :]).then_inc(pT_dve, 1)

            def attend_out(A, par, dst):
                eng.wait_ge(pv_ready, A + 2)
                dve(eng.reciprocal(inv[:, :], sums[:, par, :]))
                dve.wait(eng)
                for r in range(RT):
                    ins = eng.tensor_tensor(dst(r), bank[5][:, r * SEQ:(r + 1) * SEQ].rearrange("p (n d) -> p n d", d=HD),
                                            inv[:, 4 * r:4 * r + 4].unsqueeze(2).to_broadcast([P, 4, HD]), ALU.mult)
                    if r:
                        ins.then_inc(o_done, 1)
                    else:
                        dve(ins)

            def diff_out(l, A, par, i):
                eng.wait_ge(pv_ready, A + 2)
                dve(eng.reciprocal(inv[:, :], sums[:, par, :]))
                dve.wait(eng)
                odd = inv[:, :].rearrange("p (n two) -> p n two", two=2)[:, :, 1:2]
                dve(eng.tensor_scalar(odd, odd, lam[:, 0:1], None, ALU.mult))
                dve.wait(eng)
                W = 2 * HD
                for r in range(RT):
                    o = bank[5 + r][:, :].rearrange("p (n two d) -> p n two d", two=2, d=W)
                    c = inv[:, 4 * r:4 * r + 4].rearrange("p (n two) -> p n two", two=2)
                    for w in range(2):
                        ins = eng.tensor_tensor(scr[:, w, r * 2 * W:(r + 1) * 2 * W].rearrange("p (n d) -> p n d", d=W),
                                                o[:, :, w, :], c[:, :, w:w + 1].to_broadcast([P, 2, W]), ALU.mult)
                        if r and w:
                            ins.then_inc(o_done, 1)
                            eng.wait_ge(o_done, A + 3)
                        else:
                            dve(ins)
                dve.wait(eng)
                dve(eng.tensor_tensor(scr[:, 0, :], scr[:, 0, :], scr[:, 1, :], ALU.subtract))
                dve.wait(eng)
                dve(eng.tensor_tensor(scr[:, 1, :], scr[:, 0, :], scr[:, 0, :], ALU.mult))
                dve.wait(eng)
                eng.tensor_reduce(dstat[:, 0:4], scr[:, 1, :].rearrange("p (n d) -> p n d", d=W), AX.X, ALU.add)\
                   .then_inc(dsq, 1)
                a4 = scr[:, 0, :].rearrange("p (n d) -> p n d", d=W)
                dve(eng.tensor_tensor(a4, a4, sub_g[:, :].unsqueeze(1).to_broadcast([P, 4, W]), ALU.mult))
                dve.wait(eng)
                eng.wait_ge(drs, l * 2 + i + 1)
                dve(eng.tensor_tensor(mix[:, :, SEQ + 2 * i * W:SEQ + 2 * (i + 1) * W].rearrange("p r (n d) -> p r n d", d=W),
                                      scr[:, 0, :].rearrange("p (r n d) -> p r n d", r=2, d=W),
                                      dstat[:, 4:8].rearrange("p (r n) -> p r n", r=2).unsqueeze(3).to_broadcast([P, 2, 2, W]),
                                      ALU.mult))
                dve.wait(eng)

            def ffn(p0, l, after):
                def step(c, n0, n1):
                    split_lo(p0 + c + 1, 0, n0)
                    for r in range(RT):
                        n = l * 2 * FF_STEPS + 2 * c + r
                        eng.wait_ge(silu_ready, n + 1)
                        eng.tensor_tensor(probs[:, r, 0:FF_STEP], sqr[:, r * FF_STEP:(r + 1) * FF_STEP],
                                          bank[r][:, FF_STEP:2 * FF_STEP], ALU.mult).then_inc(gu_free, 1)
                    split_lo(p0 + c + 1, 1, n1)
                    for r in range(RT):
                        n = l * 2 * FF_STEPS + 2 * c + r
                        eng.wait_ge(ff_hi, n + 1)
                        eng.tensor_tensor(ffT[1][:, :, r * P:(r + 1) * P],
                                          bank[6 + r][:, 0:2 * P].rearrange("p (k c) -> p k c", k=2),
                                          ffT[0][:, :, r * P:(r + 1) * P].bitcast(F32), ALU.subtract)\
                           .then_inc(ff_lo, 1)

                with eng.Fori(0, FF_STEPS - 1) as c:
                    step(c, ffn_elements(1, 0), ffn_elements(1, 1))
                step(FF_STEPS - 1, 2 * UNIT, 2 * UNIT)
                for r in range(RT):
                    for n in range(2):
                        i = 2 * r + n
                        if i < 3:
                            eng.wait_ge(down_ready, l * 3 + i + 1)
                        else:
                            eng.wait_ge(used[1], p0 + FF_STEPS + 2)
                        part = x[:, r, n * COLS:(n + 1) * COLS]
                        if after is None:
                            ins = eng.tensor_copy(mix[:, r, n * COLS:(n + 1) * COLS], bank[2 + i][:, :])
                        else:
                            ins = eng.tensor_tensor(part, part, bank[2 + i][:, :], ALU.add)
                        ins.then_inc(down_added, 1)
                if after is not None:
                    after()

            eng.wait_ge(const_ready, 4)
            for j in range(2):
                eng.sem_inc(lo_ready[j], 1)
            eng.sem_inc(pT_dve, 1)
            eng.sem_inc(o_done, 2)
            for j in range(2):
                split_lo(0, j, 4 * UNIT)
            eng.wait_ge(rope_loaded, 32)
            eng.wait_ge(x_loaded, 16 * RT)
            dve.restart(eng)
            with eng.Fori(0, LAYERS) as l:
                p, A = l * PAIRS1, l * NGRP
                lo = lambda i, j: split_lo(p + i, j, 4 * (NARROW if i == 1 else COLS))

                def take(c0, n, width):
                    return lambda r: mix[:, r, c0:c0 + n * width].rearrange("p (n d) -> p n d", d=width)

                norm_rows(2 * l)
                eng.wait_ge(rows_ready, 6 * l + 2)
                eng.sem_inc(gain_free, 1)
                turned_lo_copy(l * 3, hT)
                tables(l)
                lo(1, 0); copy_z1(p, IQ); lo(1, 1)
                eng.wait_ge(z_dve, l * 8 + 1)
                prep_index_q(l)
                lo(2, 0); copy_z1(p + 1, IK, NARROW); lo(2, 1)
                eng.wait_ge(z_dve, l * 8 + 2)
                prep_index_k(l)
                lambda_value(l)
                lo(3, 0); heads_copy(l, 0); copy_z1(p + 2, SQ); lo(3, 1)
                lo(4, 0)
                for u in range(3):
                    index_sum(l, u)
                copy_z1(p + 3, MV); lo(4, 1)
                for u in range(3, 6):
                    index_sum(l, u)
                prep_heads(l, 0)
                lo(5, 0); heads_copy(l, 2); topk_rounds(0, 2); copy_z1(p + 4, DQ); lo(5, 1)
                prep_heads(l, 1); topk_rounds(2, 4)
                lo(6, 0); topk_rounds(4, 6); copy_z1(p + 5, DK); lo(6, 1); heads_copy(l, 3)
                topk_rounds(6, 8); topk_mask(); prep_heads(l, 2)
                lo(7, 0); attend_mask(A, chosen); copy_z1(p + 6, DV); lo(7, 1); heads_copy(l, 4); attend_copy(A)
                lo(8, 0); attend_out(A, 0, take(768, 4, HD)); attend_mask(A + 1, causal)
                copy_z1(p + 7, MQ); lo(8, 1)
                prep_heads(l, 3)
                attend_copy(A + 1)
                diff_out(l, A + 1, 1, 0)
                attend_mask(A + 2, causal)
                heads_copy(l, 5)
                attend_copy(A + 2)
                diff_out(l, A + 2, 0, 1)
                attend_mask(A + 3, causal)
                attend_copy(A + 3)
                attend_out(A + 3, 1, take(0, 4, HD))
                eng.wait_ge(o_done, A + 6)
                dve.wait(eng)
                eng.sem_inc(rows_ready, 2)
                turned_lo_copy(l * 3 + 1, mixT)

                def add_out(i, r):
                    if r == 0:
                        eng.wait_ge(half_ready, l * HALVES + 8 + i + 1)
                    else:
                        eng.wait_ge(used[1], p + 8 + i + 2)
                    part = x[:, r, i * COLS:(i + 1) * COLS]
                    eng.tensor_tensor(part, part, bank[r][:, :], ALU.add).then_inc(out_added, 1)

                lo(9, 0); add_out(0, 0); add_out(0, 1); lo(9, 1)
                split_lo(p + 10, 0, ffn_elements(0, 0))
                add_out(1, 0); add_out(1, 1)
                split_lo(p + 10, 1, ffn_elements(0, 1))
                norm_rows(2 * l + 1)
                eng.wait_ge(rows_ready, 6 * l + 6)
                eng.sem_inc(gain_free, 1)
                turned_lo_copy(l * 3 + 2, hT)

                def after():
                    for j in range(2):
                        split_lo(p + PAIRS1, j, 4 * UNIT)
                ffn(p + 10, l, after)
                dve.restart(eng)
                eng.wait_ge(down_added, l * 4 + 4)

            A = LAYERS * NGRP

            def lo2(b, j):
                n = ffn_elements(0, j) if b == PAIRS2 else 4 * (GATES if b == 4 else COLS)
                split_lo(B2 + b, j, n)

            def whole(b, r):
                if r == 0:
                    eng.wait_ge(half_ready, half_of(b))
                else:
                    eng.wait_ge(used[1], B2 + b + 2)

            def take1(b, dst, scale=None):
                whole(b, 1)
                if scale is None:
                    ins = eng.tensor_copy(dst, bank[1][:, :])
                else:
                    ins = eng.tensor_scalar(dst, bank[1][:, :], scale, None, ALU.mult)
                ins.then_inc(free[1], 1)

            def twice(dst, c0, count):
                for r in range(RT):
                    ins = eng.tensor_copy(dst[:, r, :].rearrange("p (g a d) -> p g a d", g=KV_GROUPS, a=2),
                                          z[:, r, c0:c0 + KV_GROUPS * HD].rearrange("p (g d) -> p g d", d=HD)
                                          .unsqueeze(2).to_broadcast([P, KV_GROUPS, 2, HD]))
                    if r:
                        ins.then_inc(dup_ready, 1)
                    else:
                        dve(ins)

            def blocks(v, first):
                dst = flat_f.rearrange("p (j v g n) -> p j v g n", v=2, g=KV_GROUPS, n=CMP)
                for g in range(KV_GROUPS):
                    b = bank[6 + g // 2]
                    if g % 2 == 0:
                        eng.wait_ge(filled, first + g // 2)
                    for h in range(2):
                        half = slice(HD * h, HD * h + HD)
                        src = AP_of(b[half, :], (g % 2) * SEQ + h, [[2, COMP_K], [16, CMP]])
                        ins = eng.tensor_tensor(dst[half, :, v, g, :], src,
                                                pe_kv[half, v, :].unsqueeze(2).to_broadcast([HD, COMP_K, CMP]),
                                                ALU.add)
                        if g % 2 and h:
                            ins.then_inc(read67[g // 2], 1)
                        else:
                            dve(ins)

            def fill_copy(count, t0):
                eng.wait_ge(filled, count)
                eng.tensor_copy(headsT[:, t0:t0 + 2, :], bank[7][:, :].rearrange("p (m c) -> p m c", m=2))\
                   .then_inc(read67[1], 1)

            def gate_of(r, g, branch):
                a = G2 + 12 * g
                return z[:, r, a:a + 12].rearrange("p (h b) -> p h b", b=3)[:, :, branch]

            def group_out(i):
                g, branch = i % 4, 1 + i // 4
                eng.wait_ge(pv_ready, A + i + 2)
                dve(eng.reciprocal(inv[:, :], sums[:, i % 2, :]))
                dve.wait(eng)
                for r in range(RT):
                    dve(eng.tensor_tensor(inv[:, 4 * r:4 * r + 4], inv[:, 4 * r:4 * r + 4], gate_of(r, g, branch),
                                          ALU.mult))
                dve.wait(eng)
                eng.tensor_tensor(sqr[:, :].rearrange("p (n d) -> p n d", d=HD),
                                  bank[5][:, :].rearrange("p (n d) -> p n d", d=HD),
                                  inv[:, :].unsqueeze(2).to_broadcast([P, 8, HD]), ALU.mult).then_inc(o_done, 1)
                eng.wait_ge(o_done, A + i + 3)
                part = mix[:, :, g * SEQ:(g + 1) * SEQ]
                dve(eng.tensor_tensor(part, part, sqr[:, :].rearrange("p (r c) -> p r c", r=2), ALU.add))
                dve.wait(eng)

            def merge(b):
                n = (b // 2) % 2
                first = b < 16
                for r in range(RT):
                    whole(b, r)
                    eng.wait_ge(free[r], product(b))
                    dst = merged(r, n) if first else scr[:, r, :]
                    eng.scalar_tensor_tensor(out=dst, in0=scr[:, r, :], scalar=1.0, in1=bank[r][:, :],
                                             op0=ALU.add, op1=ALU.mult).then_inc(free[r], 1)
                    eng.wait_ge(free[r], product(b) + 1)
                    if first:
                        eng.sem_inc(merged_done, 1)
                    else:
                        eng.tensor_tensor(merged(r, n), merged(r, n), scr[:, r, :], ALU.add).then_inc(merged_done, 1)

            def convolve(b):
                for q in range(4):
                    c = 4 * (b - 16) + q
                    if q % 2 == 0:
                        whole(b, q // 2)
                    src, dst = bank[q // 2][:, (q % 2) * SEQ:(q % 2 + 1) * SEQ], channels(c)
                    cw = lambda j: par_cw[:, 4 * c + j:4 * c + j + 1]
                    dve(eng.tensor_scalar(dst, src, cw(3), par_cb[:, c:c + 1], ALU.mult, ALU.add))
                    dve.wait(eng)
                    for back in (1, 2, 3):
                        ins = eng.scalar_tensor_tensor(out=dst[:, back:], in0=src[:, 0:SEQ - back],
                                                       scalar=cw(3 - back), in1=dst[:, back:],
                                                       op0=ALU.mult, op1=ALU.add)
                        if back == 3 and q % 2:
                            ins.then_inc(free[q // 2], 1)
                            eng.wait_ge(free[q // 2], product(b) + 1)
                            eng.sem_inc(xc_ready, 2)
                        else:
                            dve(ins)
                            dve.wait(eng)

            def gated_input(c):
                eng.wait_ge(read67[c % 2], (10, 11)[c % 2] + c // 2)
                eng.wait_ge(u_ready, c + 1)
                eng.scalar_tensor_tensor(out=channels(c), in0=probs[:, c % 2, SEQ:2 * SEQ], scalar=1.0,
                                         in1=channels(c), op0=ALU.add, op1=ALU.mult).then_inc(gx_done, 1)

            def post_add(i, gain_i, last_of):
                eng.wait_ge(rs_ready, i + 1)
                eng.wait_ge(gain_loaded, 16 * gain_i + 16)
                for r in range(RT):
                    dve(eng.scalar_tensor_tensor(out=z[:, r, 0:D], in0=mix[:, r, :], scalar=ssq[:, 4 + r:5 + r],
                                                 in1=gain[:, :], op0=ALU.mult, op1=ALU.mult))
                dve.wait(eng)
                eng.sem_inc(gain_free, 1)
                for r in range(RT):
                    eng.tensor_tensor(x[:, r, :], x[:, r, :], z[:, r, 0:D], ALU.add).then_inc(x_added, 1)
                eng.wait_ge(x_added, last_of)

            norm_rows(4)
            eng.wait_ge(small_loaded, 32)
            dve(eng.tensor_scalar(sp[:, 0:8], par_lam, -1.0, None, ALU.mult))
            dve(eng.tensor_scalar(sp[:, 32:40], par_lam, -1.0, 0.0, ALU.mult, ALU.max))
            dve.wait(eng)
            eng.tensor_tensor(sp[:, 0:8], sp[:, 0:8], par_lam, ALU.min).then_inc(sp_abs, 1)
            dve(eng.tensor_scalar(sp[:, 88:96], par_ba, 0.5, None, ALU.mult))
            dve(eng.tensor_scalar(sp[:, 96:104], par_bx, 0.5, None, ALU.mult))
            eng.wait_ge(sp_exp, 1)
            eng.tensor_scalar(sp[:, 16:24], sp[:, 8:16], 1.0, None, ALU.add).then_inc(sp_one, 1)
            eng.wait_ge(sp_one, 1)
            dve(eng.tensor_scalar(sp[:, 40:48], sp[:, 16:24], 1.0, None, ALU.subtract))
            dve.wait(eng)
            dve(eng.tensor_scalar(sp[:, 48:56], sp[:, 40:48], 1e-30, None, ALU.max))
            dve(eng.tensor_scalar(sp[:, 56:64], sp[:, 40:48], 0.0, None, ALU.is_equal))
            dve.wait(eng)
            dve(eng.reciprocal(sp[:, 64:72], sp[:, 48:56]))
            dve(eng.tensor_tensor(sp[:, 56:64], sp[:, 56:64], sp[:, 8:16], ALU.mult))
            dve.wait(eng)
            dve(eng.tensor_tensor(sp[:, 64:72], sp[:, 64:72], sp[:, 8:16], ALU.mult))
            dve(eng.tensor_tensor(sp[:, 32:40], sp[:, 32:40], sp[:, 56:64], ALU.add))
            dve.wait(eng)
            eng.wait_ge(sp_ln, 1)
            dve(eng.tensor_tensor(sp[:, 64:72], sp[:, 64:72], sp[:, 24:32], ALU.mult))
            dve.wait(eng)
            dve(eng.tensor_tensor(sp[:, 72:80], sp[:, 64:72], sp[:, 32:40], ALU.add))
            dve.wait(eng)
            dve(eng.tensor_scalar(sp[:, 80:88], sp[:, 72:80], 2.0, None, ALU.mult))
            eng.wait_ge(rows_ready, 14)
            eng.sem_inc(gain_free, 1)
            turned_lo_copy(6, hT)
            lo2(1, 0); take1(0, z[:, 1, KC2:KC2 + COLS]); lo2(1, 1)
            for r in range(RT):
                eng.wait_ge(free[r], 1)
            twice(scr, KC2, 1)
            twice(probs, VC2, 2)
            lo2(2, 0); take1(1, z[:, 1, Q2:Q2 + COLS], HD ** -0.5); lo2(2, 1)
            blocks(0, F_CK)
            lo2(3, 0)
            blocks(1, F_CV)
            dve.wait(eng)
            eng.wait_ge(read67[0], 2)
            eng.wait_ge(read67[1], 2)
            eng.sem_inc(flat_done, 1)
            take1(2, z[:, 1, Q2 + COLS:Q2 + D], HD ** -0.5); lo2(3, 1)
            lo2(4, 0); take1(3, z[:, 1, KS2:KS2 + COLS]); lo2(4, 1)
            for r in range(RT):
                eng.wait_ge(free[r], 4)
            twice(scr, KS2, 3)
            fill_copy(F_Q + 1, 2)
            fill_copy(F_Q + 3, 6)
            lo2(5, 0)
            eng.wait_ge(flat_hi, 1)
            eng.tensor_tensor(flat[1].rearrange("p j m -> p (j m)"), flat_f,
                              flat[0].rearrange("p j m -> p (j m)").bitcast(F32), ALU.subtract).then_inc(flat_lo, 1)
            lo2(5, 1)
            for r in range(RT):
                eng.wait_ge(free[r], 5)
                dve(eng.tensor_scalar(z[:, r, G2:G2 + GATES], z[:, r, G2:G2 + GATES], 0.5, 0.5, ALU.mult, ALU.add))
            lo2(6, 0); fill_copy(F_SK + 1, T2_KS + 2); take1(5, z[:, 1, KW2:KW2 + COLS])
            for r in range(RT):
                eng.wait_ge(free[r], 6)
            eng.wait_ge(filled, F_CV + 1)
            twice(probs, KW2, 4)
            lo2(6, 1)
            lo2(7, 0); fill_copy(F_WK + 1, T2_KW + 2); lo2(7, 1)
            eng.wait_ge(par_loaded, 64 * (LAYERS + 1))
            dve(eng.memset(scr[:, :, :], 0.0))
            dve(eng.memset(headsT[:, T2_V:T2_V + 4, :], 0.0))
            dve(eng.memset(probs[:, 0:2, :], 0.0))
            dve.wait(eng)
            lo2(8, 0); lo2(8, 1)
            lo2(9, 0)
            eng.wait_ge(read67[1], 7)
            for k in range(2):
                ins = eng.tensor_copy(scr[:, k, :].rearrange("p (g h n) -> p g h n", g=4, h=4)[:, :, :, 0:CMP],
                                      hidT[:, (2 + k) * COMP + COMP // 2:(3 + k) * COMP]
                                      .rearrange("p (g n) -> p g n", n=CMP).unsqueeze(2).to_broadcast([P, 4, 4, CMP]))
                if k:
                    ins.then_inc(pad_ready, 1)
                else:
                    dve(ins)
            lo2(9, 1)
            eng.wait_ge(filled, F_VC)
            for h in range(4):
                part = slice(32 * h, 32 * h + 32)
                ins = eng.tensor_copy(headsT[part, T2_V:T2_V + 4, h * HD:(h + 1) * HD],
                                      bank[7][part, 0:4 * HD].rearrange("p (g d) -> p g d", d=HD))
                if h == 3:
                    ins.then_inc(read67[1], 1)
                else:
                    dve(ins)
            wide = probs[:, 0:2, :].rearrange("p r (h n) -> p (r h) n", n=32)[:, :, 0:CMP]
            eng.wait_ge(cmask_ready, 1)
            for odd in range(2):
                eng.wait_ge(cs_ready, odd + 1)
                for r in range(RT):
                    dve(eng.tensor_tensor(probs[:, r, :].rearrange("p (h o n) -> p h o n", o=2, n=32)[:, :, odd, 0:CMP],
                                          bank[2 + odd][:, r * P:(r + 1) * P].rearrange("p (h n) -> p h n", n=16)[:, :, 0:CMP],
                                          cmask[:, r, :].unsqueeze(1).to_broadcast([P, 8, CMP]), ALU.add))
            dve.wait(eng)
            dve(eng.tensor_reduce(cstat, wide, AX.X, ALU.max))
            dve.wait(eng)
            eng.tensor_tensor(wide, wide, cstat.unsqueeze(2).to_broadcast([P, 32, CMP]), ALU.subtract)\
               .then_inc(cm_ready, 1)
            lo2(10, 0)
            eng.wait_ge(ce_ready, 1)
            dve(eng.tensor_reduce(cstat, wide, AX.X, ALU.add))
            dve.wait(eng)
            dve(eng.reciprocal(ccoef, cstat))
            dve.wait(eng)
            for r in range(RT):
                c = ccoef[:, 16 * r:16 * r + 16]
                dve(eng.tensor_tensor(c, c, z[:, r, G2:G2 + GATES].rearrange("p (h b) -> p h b", b=3)[:, :, 0], ALU.mult))
            dve.wait(eng)
            dve(eng.tensor_scalar(ccoef[:, 0:16], ccoef[:, 0:16], any_ok, None, ALU.mult))
            dve.wait(eng)
            eng.tensor_tensor(wide, wide, ccoef.unsqueeze(2).to_broadcast([P, 32, CMP]), ALU.mult)\
               .then_inc(cn_ready, 1)
            for r in range(RT):
                eng.wait_ge(free[r], 9)
            lo2(10, 1)
            eng.wait_ge(ct_ready, 2)
            eng.tensor_copy(probsT[:, 1, :], bank[3][:, :]).then_inc(cT_dve, 1)
            for r in range(RT):
                for n in range(2):
                    dve(eng.bn_stats(bn[:, 12 * r + 6 * n:12 * r + 6 * n + 6], z[:, r, n * COLS:(n + 1) * COLS]))
            dve.wait(eng)
            for r in range(RT):
                ins = eng.bn_aggr(bn[:, 24 + 2 * r:26 + 2 * r], bn[:, 12 * r:12 * r + 12])
                if r:
                    ins.then_inc(var_ready, 1)
                else:
                    dve(ins)
            lo2(11, 0)
            for r in range(RT):
                eng.wait_ge(cv_ready, r + 1)
                dve(eng.tensor_copy(mix[:, r, 0:COLS], bank[4][:, :]))
                eng.tensor_copy(mix[:, r, COLS:D], bank[5][:, :]).then_inc(cv_done, 1)
            dve.wait(eng)
            eng.wait_ge(vrs_ready, 1)
            eng.wait_ge(gain_loaded, 96)
            for r in range(RT):
                v = z[:, r, 0:D]
                dve(eng.tensor_scalar(v, v, bn[:, 24 + 2 * r:25 + 2 * r], bn[:, 28 + r:29 + r], ALU.subtract, ALU.mult))
            lo2(11, 1)
            attend_mask(A, causal)
            dve.wait(eng)
            for r in range(RT):
                dve(eng.tensor_tensor(z[:, r, 0:D], z[:, r, 0:D], gain[:, :], ALU.mult))
            dve.wait(eng)
            eng.sem_inc(gain_free, 1)
            lo2(12, 0)
            attend_copy(A)
            lo2(12, 1)
            eng.wait_ge(gain_loaded, 112)
            for r in range(RT):
                eng.tensor_tensor(z[:, r, 0:D], z[:, r, 0:D], gain[:, :], ALU.add).then_inc(vn_ready, 1)
            eng.wait_ge(vn_ready, 2)
            eng.sem_inc(gain_free, 1)
            group_out(0)
            attend_mask(A + 1, causal)
            eng.wait_ge(free[0], product(12))
            eng.wait_ge(free[1], product(12))
            for r in range(RT):
                for g in range(4):
                    if g % 2 == 0:
                        eng.wait_ge(filled, F_MIX + 2 * r + g // 2)
                    u = z[:, r, U2 + g * SEQ:U2 + (g + 1) * SEQ]
                    ins = eng.scalar_tensor_tensor(out=u, in0=bank[6 + g // 2][:, (g % 2) * SEQ:(g % 2 + 1) * SEQ],
                                                   scalar=par_bs[:, g:g + 1], in1=u, op0=ALU.add, op1=ALU.mult)
                    if g % 2:
                        ins.then_inc(read67[g // 2], 1)
                    else:
                        dve(ins)
            dve.wait(eng)
            eng.wait_ge(read67[0], 9)
            eng.wait_ge(read67[1], 10)
            eng.sem_inc(rows_ready, 2)
            for b in range(12, 19):
                i = b - 11
                if b > 12:
                    group_out(i - 1)
                    attend_mask(A + i, causal)
                lo2(b + 1, 0)
                attend_copy(A + i)
                if b in (13, 15):
                    merge(b)
                if b in (16, 17):
                    convolve(b)
                lo2(b + 1, 1)
                if b == 12:
                    turned_lo_copy(7, mixT)
            group_out(7)
            eng.sem_inc(rows_ready, 2)
            lo2(20, 0); lo2(20, 1)
            lo2(21, 0)
            for c in range(4):
                gated_input(c)
            lo2(21, 1)
            for c in range(4, 8):
                gated_input(c)
            turned_lo_copy(8, mixT)
            roots = headsT[:, 0:8, :].rearrange("p (a b) c -> p a (b c)", a=2)
            gx = z[:, :, 0:D]
            lo2(22, 0)
            merge(21)
            eng.tensor_scalar(mix[:, :, :], roots, 1.0, None, ALU.add).then_inc(u_read, 1)
            lo2(22, 1)
            eng.wait_ge(u_read, 1)
            dve(eng.reciprocal(mix[:, :, :], mix[:, :, :]))
            dve.wait(eng)
            lo2(23, 0)
            eng.wait_ge(gx_done, 8)
            dve(eng.tensor_tensor(gx, gx, mix[:, :, :], ALU.mult))
            dve.wait(eng)
            lo2(23, 1)
            eng.wait_ge(root_ready, 1)
            dve(eng.tensor_tensor(gx, gx, roots, ALU.mult))
            dve(eng.tensor_scalar(mix[:, :, :], mix[:, :, :], 2.0, 1.0, ALU.mult, ALU.subtract))
            dve.wait(eng)
            lo2(24, 0)
            merge(23)
            lo2(24, 1)
            for c in range(8):
                dve(eng.tensor_tensor_scan(headsT[:, c, :], mix[:, c // 4, (c % 4) * SEQ:(c % 4 + 1) * SEQ],
                                           channels(c), 0.0, ALU.mult, ALU.add))
            dve.wait(eng)
            lo2(25, 0)
            eng.tensor_tensor(headsT[:, 0:8, :], headsT[:, 0:8, :], headsT[:, 8:16, :], ALU.mult).then_inc(yc_ready, 1)
            lo2(25, 1)
            eng.wait_ge(yc_hi, 1)
            eng.tensor_tensor(mixT[1][:, :, :], headsT[:, 0:8, :], mixT[0][:, :, :].bitcast(F32), ALU.subtract)\
               .then_inc(yc_lo, 1)
            lo2(26, 0); merge(25); lo2(26, 1)
            lo2(27, 0); lo2(27, 1)
            lo2(28, 0); merge(27); lo2(28, 1)
            eng.wait_ge(merged_done, 12)
            eng.sem_inc(rows_ready, 2)
            turned_lo_copy(9, mixT, 0.5)
            lo2(29, 0); take1(28, mix[:, 1, 0:COLS]); lo2(29, 1)
            lo2(30, 0); take1(29, mix[:, 1, COLS:D]); lo2(30, 1)
            post_add(5, 7, RT)
            norm_rows(6, 8)
            eng.wait_ge(rows_ready, 22)
            eng.sem_inc(gain_free, 1)
            turned_lo_copy(10, hT)
            ffn(B2 + PAIRS2, LAYERS, None)
            post_add(7, 9, 2 * RT)


def rope_tables():
    inv = 1.0 / (np.float32(10000.0) ** (np.arange(0, HD, 2, dtype=np.float32) / HD))
    ang = (np.arange(SEQ, dtype=np.float32)[:, None] * inv[None, :]).astype(np.float32)
    c, s = np.cos(ang).astype(np.float32), np.sin(ang).astype(np.float32)
    by_row = lambda a: np.ascontiguousarray(a.reshape(RT, P, HD).transpose(1, 0, 2))
    return by_row(np.concatenate([c, c], 1)), by_row(np.concatenate([-s, s], 1))


def halves(w):
    n = w.shape[1] // COLS
    return w.reshape(2, KT // 2, P, n, COLS).transpose(3, 0, 2, 1, 4).reshape(n, 2, P, KT // 2 * COLS)


def ffn_layout(gate, up, down):
    k = lambda w: w.reshape(KT, P, FF_STEPS, FF_STEP)
    gu = np.stack([k(gate), k(up)], 3).transpose(2, 1, 0, 3, 4)
    gu = gu.reshape(FF_STEPS, P, KT * COLS)
    dn = down.reshape(FF_STEPS, 2, P, D).transpose(0, 2, 1, 3).reshape(FF_STEPS, P, 4 * UNIT)
    first = gu[0]
    second = np.concatenate([gu[1:, :, 6 * UNIT:], dn[:-1]], 2)
    loop = np.stack([gu[1:, :, :6 * UNIT], second], 1)
    last = dn[-1].reshape(P, 2, 2 * UNIT).transpose(1, 0, 2)
    return first, loop, last


def layout(i):
    t = {}
    t["x"] = i["x"].reshape(SEQ, D)
    w = i["w_in"]
    sizes = [256, 256, 256, 512, 512, 512, 256, 256, 256, 512, 64, 8]
    mq, mk, mv, dq, dk, dv, sq, sk, sv, iq, ik, iw = np.split(w, np.cumsum(sizes)[:-1], axis=2)
    groups = np.concatenate([iq, sq, sk, mv, sv, dq, dk, dv, mq, mk], 2)
    t["w1_groups"] = np.stack([halves(g) for g in groups])
    narrow = np.concatenate([ik, iw], 2)
    t["w1_narrow"] = narrow.reshape(LAYERS, 2, KT // 2, P, NARROW).transpose(0, 1, 3, 2, 4)\
        .reshape(LAYERS, 2, P, KT // 2 * NARROW)
    t["w1_out"] = np.stack([halves(g) for g in i["w_out"]])
    ff = [ffn_layout(i["w_gate"][l], i["w_up"][l], i["w_down"][l]) for l in range(LAYERS)]
    ff.append(ffn_layout(i["w_ffn_in_2"][0][:, :DFF], i["w_ffn_in_2"][0][:, DFF:], i["w_ffn_out_2"][0]))
    for n, name in enumerate(("ff_first", "ff_loop", "ff_last")):
        t[name] = np.stack([f[n] for f in ff])
    again = lambda a: np.concatenate([a, a[-1:]])
    t["attn_norm_g"] = i["attn_norm_g"]
    t["ffn_norm_g"] = i["ffn_norm_g"]
    t["next_norm_g"] = np.concatenate([i["attn_norm_g"][1:], i["g_pre_mix_2"]])
    t["head_gains"] = again(np.concatenate([i["q_norm_g"], i["k_norm_g"]], 1))
    t["diff_lambda"] = again(i["diff_lambda"])
    t["diff_subln_g"] = again(i["diff_subln_g"])
    first = [0.8 - 0.6 * np.exp(-0.3 * l) for l in range(LAYERS + 1)]
    t["lam_init"] = np.array([[v, 1.0 - v] for v in first], np.float32)
    t["rope_c"], t["rope_s"] = rope_tables()
    w2 = i["w_in_2"][0]
    widths = [1024, 1024, 1024, 256, 256, 256, 256, 256, 256, GATES, 1024, 1024, 1024, 1024, 1024]
    u, v, q, kc, vc, ks, vs, kw, vw, ng, xr, rg, ma, mb, mc = np.split(w2, np.cumsum(widths)[:-1], axis=1)
    half = lambda a, n: a[:, n * COLS:(n + 1) * COLS]
    cols = [kc, vc, q, ks, vs, kw, vw, v, u]

    def branch(gate, w):
        return [half(gate, 0), half(w, 0), half(gate, 1), half(w, 1)]

    a, b, c = i["w_br_a_2"][0], i["w_br_b_2"][0], i["w_br_c_2"][0]
    cols += branch(ma, a) + [xr, rg] + branch(mb, b) + branch(mc, c) + [i["w_o_2"][0]]
    t["w2_groups"] = halves(np.concatenate(cols, 1))
    t["w2_narrow"] = ng.reshape(2, KT // 2, P, GATES).transpose(0, 2, 1, 3).reshape(2, P, KT // 2 * GATES)
    comp = np.stack([i["nsa_wk1_2"][0].reshape(COMP_K, P, SEQ), i["nsa_wv1_2"][0].reshape(COMP_K, P, SEQ)], 2)
    t["w2_comp"] = comp.reshape(2, 2, 4, P, COLS).transpose(0, 1, 3, 2, 4).reshape(2, 2, P, 4 * COLS)
    wk2 = i["nsa_wk2_2"][0].reshape(2, P, HD).transpose(1, 0, 2)
    wk2 = np.concatenate([wk2, wk2], 2).reshape(P, 256)
    wv2 = i["nsa_wv2_2"][0].reshape(2, P, HD).transpose(1, 0, 2).reshape(P, 128)
    pos = lambda e: e.reshape(COMP_K, P).T
    t["small2"] = np.concatenate([wk2, wv2, pos(i["nsa_pe_k_2"][0]), pos(i["nsa_pe_v_2"][0])], 1)
    ch = lambda e: e[0].reshape(KT, P).T
    cw = i["rnn_conv_w_2"][0].reshape(4, KT, P).transpose(2, 1, 0).reshape(P, 4 * KT)
    t["channel2"] = np.concatenate([i["gmlp_bs_2"][0].T, cw, ch(i["rnn_conv_b_2"]), ch(i["rnn_ba_2"]),
                                    ch(i["rnn_bx_2"]), ch(i["rnn_lam_2"])], 1)
    t["w_s"] = i["gmlp_ws_2"][0].transpose(2, 0, 1)
    g = lambda w: w[0].reshape(KT, P, HD).transpose(1, 0, 2).reshape(P, KT * HD)
    t["w_gates"] = np.stack([g(i["rnn_wa_2"]), g(i["rnn_wx_2"])])
    t["rows2"] = np.concatenate([i["gmlp_ln_g_2"], i["gmlp_ln_b_2"], i["g_post_mix_2"], i["g_pre_ffn_2"],
                                 i["g_post_ffn_2"]])
    return {k: np.ascontiguousarray(v) for k, v in t.items()}


def kernel(**inputs):
    import concourse.bacc as bacc
    from concourse.bass_utils import run_bass_kernel_spmd

    nc = bacc.Bacc("TRN2", target_bir_lowering=False, num_devices=1)
    arrays = layout({k: np.asarray(v) for k, v in inputs.items()})
    t = {k: nc.dram_tensor(f"in_{k}", v.shape, mybir.dt.from_np(v.dtype), kind="ExternalInput").ap()
         for k, v in arrays.items()}
    t["out"] = nc.dram_tensor("out_x", (SEQ, D), F32, kind="ExternalOutput").ap()
    block_one_and_two(nc, t)
    r = run_bass_kernel_spmd(nc, [{f"in_{k}": v for k, v in arrays.items()}], core_ids=[0])
    return r.results[0]["out_x"].reshape(1, SEQ, D)
```

```python
from contextlib import ExitStack

import numpy as np

import concourse.bass as bass
from concourse import mybir

F32 = mybir.dt.float32
F32R = mybir.dt.float32r
ALU = mybir.AluOpType
ACT = mybir.ActivationFunctionType
AX = mybir.AxisListType

P = 128
SEQ = 256
RT = SEQ // P
D = 1024
KT = D // P
LAYERS = 2
HD = 64
EPS = 1e-6
NEG = -1e30
TAKEN = -3e38
DFF = 2816
COLS = 512
UNIT = COLS
SLOT = 6 * UNIT
TOPK = 64
IDX_HEADS = 8
FF_STEP = 256
FF_STEPS = DFF // FF_STEP

IQ, IK, IW, DQ, DK, DV, MQ, MK, SQ, SK, MV, SV = (
    0, 512, 576, 584, 1096, 1608, 2120, 2376, 2632, 2888, 3144, 3400)
HEAD_SETS = (DQ, DK, MQ, SQ)
Z_COLS = 3656
LN_EXP = "natural_log_exp_and_others"
NARROW = 72
T_IQ, T_SQ, T_SK, T_DQ, T_DK, T_MQ, T_MK, T_IK = 0, 4, 6, 8, 12, 16, 18, 20
PAIRS1 = 22
HALVES = 10
Q2, KC2, VC2, KS2, VS2, KW2, VW2, G2, U2 = 0, 1024, 1280, 1536, 1792, 2048, 2304, 2560, 2608
GATES = 48
CMP = 15
KV_GROUPS = 4
COMP = 2 * KV_GROUPS * CMP
COMP_K = 16
B2 = 2 * PAIRS1
PAIRS2 = 30
T2_KS, T2_KW, T2_KC, T2_V = 8, 12, 16, 17
F_CK, F_CV, F_Q, F_SK, F_WK, F_HT, F_KC, F_VC, F_MIX, F_GATE = 1, 3, 5, 9, 11, 13, 14, 15, 16, 20
NGRP = 4


class Progress:

    def __init__(self, sem):
        self.sem, self.n = sem, 0

    def __call__(self, instruction):
        instruction.then_inc(self.sem, 1)
        self.n += 1

    def wait(self, eng):
        eng.wait_ge(self.sem, self.n)

    def restart(self, eng):
        if self.n:
            eng.wait_ge(self.sem, self.n)
            eng.sem_clear(self.sem)
            self.n = 0


def AP_of(base, offset, pattern):
    return bass.AP(base.tensor, base.offset + offset, [list(base.ap[0])] + pattern)


def block_one_and_two(nc, t):
    ctx = ExitStack()
    with ctx:
        def sb(name, shape, dt=F32):
            return ctx.enter_context(nc.sbuf_tensor(name, shape, dt))

        def sem(name):
            return ctx.enter_context(nc.semaphore(name))

        raw = [sb(f"raw{j}", [P, SLOT]) for j in range(2)]
        whi = [sb(f"whi{j}", [P, SLOT], F32R) for j in range(2)]
        wlo = [sb(f"wlo{j}", [P, SLOT], F32R) for j in range(2)]
        x = sb("x", [P, RT, D])
        hT = [sb(f"hT_{s}", [P, KT, SEQ], F32R) for s in ("hi", "lo")]
        mixT = [sb(f"mixT_{s}", [P, KT, SEQ], F32R) for s in ("hi", "lo")]
        ffT = [sb(f"ffT_{s}", [P, 2, SEQ], F32R) for s in ("hi", "lo")]
        mix = sb("mix", [P, RT, D])
        z = sb("z", [P, RT, Z_COLS])
        headsT = sb("headsT", [P, 21, SEQ])
        probs = sb("probs", [P, 3, COLS])
        probsT = sb("probsT", [P, 3, COLS])
        scr = sb("scr", [P, 2, COLS])
        sqr = sb("sqr", [P, COLS])
        gain = sb("gain", [P, D])
        ident = sb("ident", [P, P])
        causal = sb("causal", [P, 3 * P])
        index = sb("index", [P, 3 * P])
        chosen = index
        rope_c = sb("rope_c", [P, RT, HD])
        rope_s = sb("rope_s", [P, RT, HD])
        gain_c = sb("gain_c", [P, RT, 6, HD])
        gain_s = sb("gain_s", [P, RT, 6, HD])
        hgain = headsT[:, T_MK:T_IK, :].rearrange("p a b -> p (a b)")[:, 0:6 * HD].rearrange("p (n d) -> p n d", d=HD)
        lamp = headsT[:, T_IK, :].rearrange("p (n d) -> p n d", d=HD)
        sub_g = sb("sub_g", [P, 2 * HD])
        flat = [m[:, :, :].rearrange("p k c -> p (k c)")[:, 0:COMP_K * COMP]
                .rearrange("p (j m) -> p j m", m=COMP) for m in mixT]
        flat_f = mix[:, :, :].rearrange("p r c -> p (r c)")[:, 0:COMP_K * COMP]
        small = gain_s[:, :, :, :].rearrange("p a b c -> p (a b c)")
        wk2 = small[:, 0:256].rearrange("p (k c) -> p k c", k=2)
        wv2 = small[:, 256:384].rearrange("p (k c) -> p k c", k=2)
        pe_kv = small[:, 384:416].rearrange("p (v j) -> p v j", v=2)
        par = small[:, 416:416 + 68]
        par_bs, par_cw, par_cb, par_ba, par_bx, par_lam = (
            par[:, a:b] for a, b in ((0, 4), (4, 36), (36, 44), (44, 52), (52, 60), (60, 68)))
        cmask = index[:, 0:2 * CMP].rearrange("p (r n) -> p r n", r=2)
        any_ok = index[:, 32:33]
        cstat = index[:, 64:96]
        ccoef = index[:, 96:128]
        w_s = gain_c[:, :, :, :].rearrange("p a b c -> p (a b c)")[:, 0:4 * P].rearrange("p (g t) -> p g t", g=4)
        hidT = probsT[:, 2, 0:4 * COMP]
        ffn_gain = headsT[:, 16:20, :].rearrange("p a b -> p (a b)")
        bn = rope_c[:, :, :].rearrange("p r d -> p (r d)")
        sp = rope_s[:, :, :].rearrange("p r d -> p (r d)")
        lam_c = sb("lam_c", [P, 2])
        lam = sb("lam", [P, 4])
        eps = sb("eps", [P, 1])
        ssq = sb("ssq", [P, 16])
        nmax = sb("nmax", [P, 8])
        sums = sb("sums", [P, 2, 8])
        inv = sb("inv", [P, 8])
        hss = sb("hss", [P, RT, 8])
        hrs = sb("hrs", [P, RT, 8])
        top8 = sb("top8", [P, 2, 8])
        dstat = sb("dstat", [P, 8])
        bank = [ctx.enter_context(nc.psum_tensor(f"bank{i}", [P, COLS], F32)) for i in range(8)]

        raw_loaded = [sem(f"raw_loaded{j}") for j in range(2)]
        hi_ready = [sem(f"hi_ready{j}") for j in range(2)]
        lo_ready = [sem(f"lo_ready{j}") for j in range(2)]
        used = [sem(f"used{j}") for j in range(2)]
        half_ready = sem("half_ready")
        z_act = sem("z_act")
        z_dve = sem("z_dve")
        out_added = sem("out_added")
        const_ready = sem("const_ready")
        x_loaded = sem("x_loaded")
        gain_loaded = sem("gain_loaded")
        gain_free = sem("gain_free")
        rope_loaded = sem("rope_loaded")
        par_loaded = sem("par_loaded")
        sq_ready = sem("sq_ready")
        rs_ready = sem("rs_ready")
        rows_ready = sem("rows_ready")
        turned = sem("turned")
        turned_hi = sem("turned_hi")
        turned_lo = sem("turned_lo")
        squares = sem("squares")
        ssq_ready = sem("ssq_ready")
        hrs_ready = sem("hrs_ready")
        prep = sem("prep")
        tables_ready = sem("tables_ready")
        heads_turned = sem("heads_turned")
        heads_act = sem("heads_act")
        heads_dve = sem("heads_dve")
        idx_ready = sem("idx_ready")
        idx_relu = sem("idx_relu")
        idx_acc = sem("idx_acc")
        scores = sem("scores")
        masked = sem("masked")
        exped = sem("exped")
        pT_ready = sem("pT_ready")
        pT_act = sem("pT_act")
        pT_dve = sem("pT_dve")
        pv_ready = sem("pv_ready")
        o_done = sem("o_done")
        lam_sum = sem("lam_sum")
        lam_exp = sem("lam_exp")
        dsq = sem("dsq")
        drs = sem("drs")
        gu_ready = sem("gu_ready")
        silu_ready = sem("silu_ready")
        gu_free = sem("gu_free")
        ff_turned = sem("ff_turned")
        ff_hi = sem("ff_hi")
        ff_lo = sem("ff_lo")
        down_ready = sem("down_ready")
        down_added = sem("down_added")
        out_sem = sem("out_sem")
        free = [sem(f"free{r}") for r in range(2)]
        filled = sem("filled")
        read67 = [sem(f"read{b}") for b in (6, 7)]
        small_loaded = sem("small_loaded")
        ws_loaded = sem("ws_loaded")
        ws_ready = sem("ws_ready")
        rg_loaded = sem("rg_loaded")
        ffn_gain_loaded = sem("ffn_gain_loaded")
        cmask_ready = sem("cmask_ready")
        sp_abs = sem("sp_abs")
        sp_exp = sem("sp_exp")
        sp_one = sem("sp_one")
        sp_ln = sem("sp_ln")
        sp_ready = sem("sp_ready")
        dup_ready = sem("dup_ready")
        flat_done = sem("flat_done")
        flat_hi = sem("flat_hi")
        flat_lo = sem("flat_lo")
        pad_ready = sem("pad_ready")
        cs_ready = sem("cs_ready")
        cm_ready = sem("cm_ready")
        ce_ready = sem("ce_ready")
        cn_ready = sem("cn_ready")
        ct_ready = sem("ct_ready")
        cT_act = sem("cT_act")
        cT_dve = sem("cT_dve")
        cv_ready = sem("cv_ready")
        cv_done = sem("cv_done")
        var_ready = sem("var_ready")
        vrs_ready = sem("vrs_ready")
        vn_ready = sem("vn_ready")
        merged_done = sem("merged_done")
        xc_ready = sem("xc_ready")
        rg_ready = sem("rg_ready")
        u_ready = sem("u_ready")
        gx_done = sem("gx_done")
        u_read = sem("u_read")
        root_ready = sem("root_ready")
        yc_ready = sem("yc_ready")
        yc_hi = sem("yc_hi")
        yc_lo = sem("yc_lo")
        x_added = sem("x_added")
        dve = Progress(sem("dve_own"))
        act = Progress(sem("act_own"))
        pool = Progress(sem("pool_own"))
        pe = Progress(sem("pe_own"))

        block = ctx.enter_context(nc.Block())

        def index_heads(u):
            return [2 * i + u for i in range(4)] if u < 2 else [4 * ((u - 2) // 2) + u % 2 + 2 * i for i in range(2)]

        def product(b):
            return b - (b > 6)

        def half_of(b):
            return LAYERS * HALVES + product(b) + 1

        def channels(c):
            return z[:, c // 4, (c % 4) * SEQ:(c % 4 + 1) * SEQ]

        def merged(r, n):
            return z[:, r, U2 + n * COLS:U2 + (n + 1) * COLS]

        def scr_ik(r):
            return scr[:, r, 0:P]

        def ffn_elements(c, j):
            if c == 0:
                return (6 * UNIT, 2 * UNIT)[j]
            if c == FF_STEPS:
                return 2 * UNIT
            return 6 * UNIT

        @block.sync
        def _(eng):
            def load(p, j, src):
                n = src.shape[1]
                eng.wait_ge(lo_ready[j], p + 1)
                eng.dma_start(raw[j][:, 0:n], src).then_inc(raw_loaded[j], 16)

            eng.dma_start(gain[:, :], t["attn_norm_g"][0, :].partition_broadcast(P)).then_inc(gain_loaded, 16)
            for r in range(RT):
                eng.dma_start(x[:, r, :], t["x"][r * P:(r + 1) * P, :]).then_inc(x_loaded, 16)

            def ffn_loads(p0, l, between):
                for j in range(2):
                    lo_, n = (0, 6 * UNIT) if j == 0 else (6 * UNIT, 2 * UNIT)
                    load(p0, j, t["ff_first"][l, :, lo_:lo_ + n])
                with eng.Fori(1, FF_STEPS) as c:
                    for j in range(2):
                        load(p0 + c, j, t["ff_loop"][l, c - 1, j])
                between()
                for j in range(2):
                    load(p0 + FF_STEPS, j, t["ff_last"][l, j])

            def next_gain(i, src):
                eng.wait_ge(gain_free, i)
                eng.dma_start(gain[:, :], src.partition_broadcast(P)).then_inc(gain_loaded, 16)

            def layer_parameters(l):
                for dst, name in ((hgain, "head_gains"), (lamp, "diff_lambda"), (sub_g[:, :], "diff_subln_g"),
                                  (lam_c[:, :], "lam_init")):
                    eng.dma_start(dst, t[name][l].partition_broadcast(P)).then_inc(par_loaded, 16)

            for j in range(2):
                load(0, j, t["w1_groups"][0, 0, j])
            layer_parameters(0)
            with eng.Fori(0, LAYERS) as l:
                for g in range(1, 8):
                    for j in range(2):
                        if g == 1:
                            load(l * PAIRS1 + g, j, t["w1_narrow"][l, j])
                        else:
                            load(l * PAIRS1 + g, j, t["w1_groups"][l, g - (g > 1), j])
                for g in range(2):
                    for j in range(2):
                        load(l * PAIRS1 + 8 + g, j, t["w1_out"][l, g, j])
                    if g == 0:
                        eng.wait_ge(prep, l * 6 + 6)
                        next_gain(2 * l + 1, t["ffn_norm_g"][l, :])

                def next_parameters():
                    next_gain(2 * l + 2, t["next_norm_g"][l, :])
                    layer_parameters(l + 1)
                ffn_loads(l * PAIRS1 + 10, l, next_parameters)
                for j in range(2):
                    load((l + 1) * PAIRS1, j, t["next_first"][l, j])
            for dst, name in ((small[:, 0:416], "small2"), (par, "channel2")):
                eng.dma_start(dst, t[name]).then_inc(small_loaded, 16)
            eng.dma_start(w_s, t["w_s"]).then_inc(ws_loaded, 16)
            with eng.Fori(1, 4) as g:
                for j in range(2):
                    load(B2 + g, j, t["w2_groups"][g, j])
            for j in range(2):
                load(B2 + 4, j, t["w2_narrow"][j])
            for j in range(2):
                load(B2 + 5, j, t["w2_groups"][4, j])
            next_gain(5, t["rows2"][0, :])
            with eng.Fori(0, 2) as g:
                for j in range(2):
                    load(B2 + 6 + g, j, t["w2_comp"][g, j])
            eng.wait_ge(filled, F_CV + 1)
            eng.dma_start(z[:, 0, KC2:KC2 + 512], t["w_gates"][0]).then_inc(rg_loaded, 16)
            eng.dma_start(z[:, 1, KC2:KC2 + 512], t["w_gates"][1]).then_inc(rg_loaded, 16)
            with eng.Fori(0, 4) as g:
                for j in range(2):
                    load(B2 + 8 + g, j, t["w2_groups"][5 + g, j])
            next_gain(6, t["rows2"][1, :])
            with eng.Fori(0, 18) as g:
                for j in range(2):
                    load(B2 + 12 + g, j, t["w2_groups"][9 + g, j])
            next_gain(7, t["rows2"][2, :])
            eng.wait_ge(cv_done, 2)
            eng.dma_start(ffn_gain, t["rows2"][3, :].partition_broadcast(P)).then_inc(ffn_gain_loaded, 16)
            ffn_loads(B2 + PAIRS2, LAYERS, lambda: next_gain(8, t["rows2"][4, :]))
            for r in range(RT):
                eng.wait_ge(x_added, RT + r + 1)
                eng.dma_start(t["out"][r * P:(r + 1) * P, :], x[:, r, :]).then_inc(out_sem, 16)
            eng.wait_ge(out_sem, 16 * RT)

        @block.gpsimd
        def _(eng):
            eng.memset(eps[:, :], EPS).then_inc(const_ready, 1)
            pool(eng.memset(ident[:, :], 0.0))
            pool(eng.memset(causal[:, :], 0.0))
            pool.wait(eng)
            eng.affine_select(out=ident[:, :], in_=ident[:, :], compare_op=ALU.not_equal, fill=1.0,
                              base=0, pattern=[[-1, P]], channel_multiplier=1).then_inc(const_ready, 1)
            for c in (0, 2):
                part = causal[:, c * P:(c + 1) * P]
                eng.affine_select(out=part, in_=part, compare_op=ALU.is_ge, fill=NEG,
                                  base=0, pattern=[[-1, P]], channel_multiplier=1).then_inc(const_ready, 1)
            eng.dma_start(rope_c[:, :, :], t["rope_c"]).then_inc(rope_loaded, 16)
            eng.dma_start(rope_s[:, :, :], t["rope_s"]).then_inc(rope_loaded, 16)
            eng.wait_ge(rope_loaded, 32)
            pool.restart(eng)
            with eng.Fori(0, LAYERS) as l:
                def projected(i):
                    eng.wait_ge(z_act, l * 8 + i + 1)
                    eng.wait_ge(z_dve, l * 8 + i + 1)

                def rotate(src, ct, st, n, scale=None, last=False):
                    h, m = HD // 2, len(ct)
                    w = n // m
                    a, b = (gain[:, c:c + n * HD].rearrange("p (n d) -> p n d", d=HD) for c in (0, COLS))
                    for i in range(m):
                        hs = slice(i * w, (i + 1) * w)
                        pool(eng.tensor_tensor(a[:, hs, :], src[:, hs, :],
                                               ct[i].unsqueeze(1).to_broadcast([P, w, HD]), ALU.mult))
                        for u, v in ((0, h), (h, 0)):
                            pool(eng.tensor_tensor(b[:, hs, u:u + h], src[:, hs, v:v + h],
                                                   st[i][:, u:u + h].unsqueeze(1).to_broadcast([P, w, h]), ALU.mult))
                    pool.wait(eng)
                    if scale is None:
                        ins = eng.tensor_tensor(src, a, b, ALU.add)
                    else:
                        pool(eng.tensor_tensor(a, a, b, ALU.add))
                        pool.wait(eng)
                        eng.wait_ge(hrs_ready, scale[0])
                        ins = eng.tensor_tensor(src, a, scale[1], ALU.mult)
                    if last:
                        ins.then_inc(prep, 1)
                    else:
                        pool(ins)
                        pool.wait(eng)

                eng.wait_ge(gain_free, 2 * l + 1)
                projected(0)
                for r in range(RT):
                    src = z[:, r, IQ:IQ + COLS].rearrange("p (n d) -> p n d", d=HD)
                    rotate(src, [rope_c[:, r, :]], [rope_s[:, r, :]], 8, last=(r == 1))
                projected(1)
                eng.wait_ge(prep, l * 6 + 1)
                eng.wait_ge(lam_sum, l + 1)
                for r in range(RT):
                    src = z[:, r, IK:IK + HD].rearrange("p (n d) -> p n d", d=HD)
                    rotate(src, [rope_c[:, r, :]], [rope_s[:, r, :]], 1)
                    pool(eng.tensor_scalar(z[:, r, IW:IW + IDX_HEADS], z[:, r, IW:IW + IDX_HEADS],
                                           IDX_HEADS ** -0.5, None, ALU.mult))
                pool.wait(eng)
                for r in range(RT):
                    ins = eng.tensor_copy(scr_ik(r).rearrange("p (a d) -> p a d", a=2),
                                          z[:, r, IK:IK + HD].unsqueeze(1).to_broadcast([P, 2, HD]))
                    if r:
                        ins.then_inc(prep, 1)
                    else:
                        pool(ins)
                eng.wait_ge(tables_ready, l + 1)
                for s, (c0, i, gains) in enumerate(zip(HEAD_SETS, (2, 3, 5, 6), ((1,), (4,), (0, 3), (2, 5)))):
                    projected(i)
                    for r in range(RT):
                        src = z[:, r, c0:c0 + COLS].rearrange("p (n d) -> p n d", d=HD)
                        rotate(src, [gain_c[:, r, g, :] for g in gains], [gain_s[:, r, g, :] for g in gains], 8,
                               scale=(l * 8 + 2 * s + r + 1, hrs[:, r, :].unsqueeze(2).to_broadcast([P, 8, HD])),
                               last=(r == 1))
                    if s < 3:
                        eng.wait_ge(prep, l * 6 + 3 + s)
                pool.restart(eng)


            eng.wait_ge(gain_free, 4)
            pool(eng.memset(index[:, 0:48], 0.0))
            pool.wait(eng)
            for r in range(RT):
                pool(eng.affine_select(out=cmask[:, r, :], in_=cmask[:, r, :], compare_op=ALU.is_ge, fill=NEG,
                                       base=r * P - 31, pattern=[[-16, CMP]], channel_multiplier=1))
            eng.affine_select(out=any_ok, in_=any_ok, compare_op=ALU.is_ge, fill=1.0, base=30,
                              pattern=[[0, 1]], channel_multiplier=-1).then_inc(cmask_ready, 1)
            pool.wait(eng)
            eng.wait_ge(ws_loaded, 16)
            eng.affine_select(out=w_s, in_=w_s, compare_op=ALU.is_ge, fill=0.0, base=0,
                              pattern=[[0, 4], [1, P]], channel_multiplier=-1).then_inc(ws_ready, 1)

        @block.tensor
        def _(eng):
            def three(out, a, a_cols, j, w, start, stop, first=True, n=COLS):
                wh, wl = whi[j][:, w:w + n], wlo[j][:, w:w + n]
                hi, lo = (s[:, a, a_cols] for s in three.act)
                eng.matmul(out, lhsT=hi, rhs=wh, start=start, stop=False)
                eng.matmul(out, lhsT=hi, rhs=wl, start=False, stop=False)
                return eng.matmul(out, lhsT=lo, rhs=wh, start=False, stop=stop)

            def chunk(p, j, n=COLS, bank_read=None, between=None):
                eng.wait_ge(lo_ready[j], p + 2)
                for r in range(RT):
                    if j == 0 and bank_read:
                        bank_read(r)
                    for k in range(4):
                        mm = three(bank[r][:, 0:n], 4 * j + k, slice(r * P, (r + 1) * P), j, k * n,
                                   start=(j == 0 and k == 0), stop=(j == 1 and k == 3), n=n)
                    if j == 1 and r == 0:
                        mm.then_inc(half_ready, 1)
                    if between and r == 0:
                        between()
                mm.then_inc(used[j], 1)

            rows_before = 0

            def turn_half(i, h, src=mix):
                for r in range(RT):
                    n = i * 4 + 2 * h + r
                    eng.wait_ge(rows_ready, n + 1 + rows_before)
                    if h:
                        eng.wait_ge(turned_lo, n - 1)
                    for k in range(4):
                        c = (4 * h + k) * P
                        mm = eng.transpose(bank[6 + r][:, k * P:(k + 1) * P], src[:, r, c:c + P], ident[:, :])
                    mm.then_inc(turned, 1)

            def turn_rows(i, src=mix):
                turn_half(i, 0, src)
                turn_half(i, 1, src)
                eng.wait_ge(turned_lo, i * 4 + 4)

            def turn_heads(l, s, src, pairs):
                eng.wait_ge(prep, l * 6 + s + 1)
                if s > 0:
                    eng.wait_ge(heads_act, l * 6 + s)
                    eng.wait_ge(heads_dve, l * 5 + (1 if s < 3 else s - 1))
                for i in range(0, pairs, 2):
                    for q in range(min(2, pairs - i)):
                        for r in range(RT):
                            mm = eng.transpose(bank[6 + i // 2][:, (q * RT + r) * P:(q * RT + r + 1) * P],
                                               src(i + q, r), ident[:, :])
                    mm.then_inc(heads_turned, 1)

            def index_scores(l, u):
                if u == 0:
                    eng.wait_ge(heads_act, l * 6 + 2)
                    eng.wait_ge(heads_dve, l * 5 + 1)
                if u >= 3:
                    eng.wait_ge(idx_relu, l * 6 + u - 2)
                b = bank[2 + u % 3]
                keys = P if u < 2 else SEQ
                for i, h in enumerate(index_heads(u)):
                    half = slice(HD * (h % 2), HD * (h % 2) + HD)
                    rows = slice(0, P) if u < 2 else slice(P, SEQ)
                    mm = eng.matmul(b[:, i * keys:(i + 1) * keys], lhsT=headsT[half, T_IQ + h // 2, rows],
                                    rhs=headsT[half, T_IK, 0:keys], start=True, stop=True)
                mm.then_inc(idx_ready, 1)

            def attend_scores(A, q, k):
                eng.wait_ge(pT_act, 2 * A + 2)
                eng.wait_ge(pT_dve, A + 1)
                for odd in range(2):
                    for u in (0, 1 + odd):
                        keys, rows = (P, slice(0, P)) if u == 0 else (SEQ, slice(P, SEQ))
                        if odd and u == 0:
                            pe.wait(eng)
                        for h in (odd, 2 + odd):
                            half = slice(HD * odd, HD * odd + HD)
                            c = h * P if u == 0 else (h // 2) * SEQ
                            mm = eng.matmul(bank[2 + u][:, c:c + keys],
                                            lhsT=headsT[half, q(h), rows], rhs=headsT[half, k(h), 0:keys],
                                            start=True, stop=True)
                        if odd:
                            mm.then_inc(scores, 2 if u == 0 else 1)
                        elif u == 0:
                            pe(mm)

            def attend_turn(A):
                for u in range(3):
                    eng.wait_ge(exped, 3 * A + (1 if u == 0 else 3))
                    for h in range(4):
                        if u == 0:
                            src = probs[:, 0, h * P:(h + 1) * P]
                        else:
                            c = (h // 2) * SEQ + (u - 1) * P
                            src = probs[:, 1 + h % 2, c:c + P]
                        mm = eng.transpose(bank[2 + u][:, h * P:(h + 1) * P], src, ident[:, :])
                    mm.then_inc(pT_ready, 1)

            def attend_values(A, v, dv):
                eng.wait_ge(pT_act, 2 * A + 4)
                eng.wait_ge(pT_dve, A + 2)
                eng.wait_ge(o_done, A + 2)
                for r in range(RT):
                    for h in range(4):
                        out = bank[5][:, (4 * r + h) * dv:(4 * r + h + 1) * dv] if dv == HD else \
                            bank[5 + r][:, h * dv:(h + 1) * dv]
                        for kt in range(r + 1):
                            mm = eng.matmul(out, lhsT=probsT[:, r + kt, h * P:(h + 1) * P], rhs=v(kt, h),
                                            start=(kt == 0), stop=(kt == r))
                mm.then_inc(pv_ready, 1)

            def ffn(p0, l, norm, bank_read):
                def gate_up(p, c):
                    eng.wait_ge(lo_ready[0], p + 2)
                    for k0, k1 in ((0, 4), (4, 6)) if c is None else ((0, 6),):
                        if c is None and k0:
                            eng.wait_ge(turned_lo, norm * 4 + 4)
                        for r in range(RT):
                            if c is not None:
                                eng.wait_ge(gu_free, l * 2 * FF_STEPS + 2 * c - 1 + r)
                            elif k0 == 0:
                                bank_read(r)
                            for k in range(k0, k1):
                                mm = three(bank[r][:, :], k, slice(r * P, (r + 1) * P), 0, k * UNIT,
                                           start=(k == 0), stop=False)
                            if c is None and k0 == 0 and r == 0:
                                turn_half(norm, 1)
                    mm.then_inc(used[0], 1)
                    eng.wait_ge(lo_ready[1], p + 2)
                    for r in range(RT):
                        for k in range(6, 8):
                            mm = three(bank[r][:, :], k, slice(r * P, (r + 1) * P), 1, (k - 6) * UNIT,
                                       start=False, stop=(k == 7))
                        mm.then_inc(gu_ready, 1)

                def down(c, first, last):
                    eng.wait_ge(ff_lo, l * 2 * FF_STEPS + 2 * c + 2)
                    three.act = ffT
                    for kk in range(2):
                        j, w0 = (kk, 0) if last else (1, (2 + 2 * kk) * UNIT)
                        if last:
                            eng.wait_ge(lo_ready[j], p0 + FF_STEPS + 2)
                        for n in range(2):
                            for r in range(RT):
                                mm = three(bank[2 + 2 * n + r][:, :], kk, slice(r * P, (r + 1) * P), j,
                                           w0 + n * UNIT, start=(first and kk == 0), stop=(last and kk == 1))
                                if last and kk == 1 and not (r == 1 and n == 1):
                                    mm.then_inc(down_ready, 1)
                        if last or kk == 1:
                            mm.then_inc(used[j], 1)
                    three.act = hT

                def turn(c, frees_slot=False):
                    for r in range(RT):
                        eng.wait_ge(gu_free, l * 2 * FF_STEPS + 2 * c + 1 + r)
                        for k in range(2):
                            mm = eng.transpose(bank[6 + r][:, k * P:(k + 1) * P],
                                               probs[:, r, k * P:(k + 1) * P], ident[:, :])
                            if frees_slot and r == 0 and k == 0:
                                mm.then_inc(used[1], 1)
                        mm.then_inc(ff_turned, 1)

                three.act = hT
                gate_up(p0, None)
                turn(0, frees_slot=True)
                gate_up(p0 + 1, 1)
                down(0, True, False)
                turn(1)
                with eng.Fori(2, FF_STEPS) as c:
                    gate_up(p0 + c, c)
                    down(c - 1, False, False)
                    turn(c)
                down(FF_STEPS - 1, False, True)

            eng.wait_ge(const_ready, 4)
            eng.sem_inc(used[0], 1)
            eng.sem_inc(used[1], 1)
            eng.sem_inc(pv_ready, 1)
            with eng.Fori(0, LAYERS) as l:
                p, A = l * PAIRS1, l * NGRP

                def project(i, jj, between=None):
                    def bank_read(r):
                        eng.wait_ge((z_act, z_dve)[r], l * 8 + i)
                    chunk(p + i, jj, NARROW if i == 1 else COLS, bank_read if i else None, between)

                def zcols(c0):
                    return lambda i, r: z[:, r, c0 + i * P:c0 + (i + 1) * P]

                def heads_read(s):
                    eng.wait_ge(heads_act, l * 6 + s + 1)
                    eng.wait_ge(heads_dve, l * 5 + s + (s == 0))

                turn_half(l * 3, 0)
                eng.wait_ge(turned_lo, l * 12 + 2)
                three.act = hT
                project(0, 0, between=lambda: turn_half(l * 3, 1))
                eng.wait_ge(turned_lo, l * 12 + 4)
                project(0, 1)
                project(1, 0); project(1, 1)
                project(2, 0); project(2, 1)
                turn_heads(l, 0, zcols(IQ), 4)
                project(3, 0)
                turn_heads(l, 1, lambda i, r: scr_ik(r), 1)
                project(3, 1)
                for u in range(3):
                    index_scores(l, u)
                project(4, 0)
                turn_heads(l, 2, zcols(DQ), 4)
                for u in range(3, 6):
                    index_scores(l, u)
                turn_heads(l, 3, zcols(DK), 4)
                project(4, 1)
                heads_read(3)
                eng.wait_ge(idx_relu, l * 6 + 6)
                attend_scores(A, lambda h: T_DQ + h // 2, lambda h: T_DK + h // 2)
                project(5, 0); project(5, 1)
                attend_turn(A)
                project(6, 0)
                attend_scores(A + 1, lambda h: T_DQ + 2 + h // 2, lambda h: T_DK + 2 + h // 2)
                attend_values(A, lambda kt, h: z[:, kt, DV + (h // 2) * 2 * HD:DV + (h // 2 + 1) * 2 * HD], 2 * HD)
                project(6, 1)
                attend_turn(A + 1)
                eng.wait_ge(o_done, A + 3)
                turn_heads(l, 4, zcols(MQ), 4)
                project(7, 0)
                heads_read(4)
                attend_scores(A + 2, lambda h: T_MQ + h // 2, lambda h: T_MK + h // 2)
                attend_values(A + 1, lambda kt, h: z[:, kt, DV + (2 + h // 2) * 2 * HD:DV + (3 + h // 2) * 2 * HD], 2 * HD)
                project(7, 1)
                attend_turn(A + 2)
                eng.wait_ge(o_done, A + 4)
                turn_heads(l, 5, zcols(SQ), 4)
                heads_read(5)
                attend_scores(A + 3, lambda h: T_SQ + h // 2, lambda h: T_SK + h // 2)
                for r in range(RT):
                    eng.wait_ge((z_act, z_dve)[r], l * 8 + 8)
                attend_values(A + 2, lambda kt, h: z[:, kt, MV + h * HD:MV + (h + 1) * HD], HD)
                turn_half(l * 3 + 1, 0)
                attend_turn(A + 3)
                eng.wait_ge(turned_lo, l * 12 + 6)
                three.act = mixT
                chunk(p + 8, 0)
                attend_values(A + 3, lambda kt, h: z[:, kt, SV + h * HD:SV + (h + 1) * HD], HD)
                turn_half(l * 3 + 1, 1)
                eng.wait_ge(turned_lo, l * 12 + 8)
                chunk(p + 8, 1)
                chunk(p + 9, 0, bank_read=lambda r: eng.wait_ge(out_added, l * 4 + 1 + r))
                turn_half(l * 3 + 2, 0)
                chunk(p + 9, 1)
                three.act = hT
                eng.wait_ge(turned_lo, l * 12 + 10)
                ffn(p + 10, l, l * 3 + 2, lambda r: eng.wait_ge(out_added, l * 4 + 3 + r))
                pe.restart(eng)

            p, A = B2, LAYERS * NGRP

            def product_chunk(b, j, n=COLS):
                chunk(p + b, j, n, (lambda r: eng.wait_ge(free[r], product(b))) if b else None)

            def channel_chunk(b, j):
                if j == 0:
                    for r in range(RT):
                        eng.wait_ge(free[r], product(b))
                eng.wait_ge(lo_ready[j], p + b + 2)
                for c in range(4):
                    out = bank[c // 2][:, (c % 2) * SEQ:(c % 2 + 1) * SEQ]
                    for k in range(4):
                        w = slice(k * COLS + c * P, k * COLS + (c + 1) * P)
                        for n, (a, h) in enumerate(((whi, 0), (wlo, 0), (whi, 1))):
                            mm = eng.matmul(out, lhsT=a[j][:, w], rhs=hT[h][:, 4 * j + k, :],
                                            start=(j == 0 and k == 0 and n == 0 and c % 2 == 0),
                                            stop=(j == 1 and k == 3 and n == 2), skip_group_check=True)
                    if j == 1 and c == 1:
                        mm.then_inc(half_ready, 1)
                mm.then_inc(used[j], 1)

            def compress(b, j):
                c = 2 * (b - 6) + j
                if c == 0:
                    for r in range(RT):
                        eng.wait_ge(free[r], product(6))
                    eng.wait_ge(flat_lo, 1)
                eng.wait_ge(lo_ready[j], p + b + 2)
                three.act = flat
                for v in range(2):
                    for k in range(4):
                        mm = three(bank[v][0:COMP, 0:SEQ], 4 * c + k, slice(0, COMP), j, k * COLS + v * SEQ,
                                   start=(c == 0 and k == 0), stop=(c == 3 and k == 3), n=SEQ)
                    if c == 3 and v == 0:
                        mm.then_inc(half_ready, 1)
                mm.then_inc(used[j], 1)
                three.act = hT

            def wait_fill(n, at):
                if at:
                    eng.wait_ge(read67[n], at)

            def turn_four(src, at):
                for n in range(2):
                    wait_fill(n, at)
                    for q in range(2):
                        for r in range(RT):
                            mm = eng.transpose(bank[6 + n][:, (q * RT + r) * P:(q * RT + r + 1) * P],
                                               src(2 * n + q, r), ident[:, :])
                    mm.then_inc(filled, 1)

            def group_scores(i):
                g = i % 4
                attend_scores(A + i, lambda h: 2 * g + h // 2, lambda h: (T2_KS, T2_KW)[i // 4] + g)

            def group_values(i):
                c0 = (VS2, VW2)[i // 4] + (i % 4) * HD
                attend_values(A + i, lambda kt, h: z[:, kt, c0:c0 + HD], HD)

            rows_before = 4
            turn_rows(6)
            three.act = hT
            product_chunk(0, 0); product_chunk(0, 1)
            product_chunk(1, 0); product_chunk(1, 1)
            eng.wait_ge(dup_ready, 1)
            turn_four(lambda g, r: scr[:, r, g * P:(g + 1) * P], 0)
            product_chunk(2, 0)
            eng.wait_ge(dup_ready, 2)
            turn_four(lambda g, r: probs[:, r, g * P:(g + 1) * P], 1)
            product_chunk(2, 1)
            product_chunk(3, 0); product_chunk(3, 1)
            for n in range(2):
                if n == 0:
                    for r in range(RT):
                        eng.wait_ge(free[r], 3)
                turn_four(lambda i, r, n=n: z[:, r, Q2 + (4 * n + i) * P:Q2 + (4 * n + i + 1) * P], 2 + n)
            product_chunk(4, 0, GATES); product_chunk(4, 1, GATES)
            product_chunk(5, 0)
            eng.wait_ge(dup_ready, 3)
            turn_four(lambda g, r: scr[:, r, g * P:(g + 1) * P], 4)
            product_chunk(5, 1)
            compress(6, 0); compress(6, 1)
            eng.wait_ge(dup_ready, 4)
            turn_four(lambda g, r: probs[:, r, g * P:(g + 1) * P], 5)
            compress(7, 0); compress(7, 1)
            product_chunk(8, 0)
            eng.wait_ge(free[0], 7)
            eng.wait_ge(free[1], 7)
            wait_fill(1, 6)
            for i in range(4):
                mm = eng.transpose(bank[7][:, i * COMP:(i + 1) * COMP], sqr[0:COMP, i * P:(i + 1) * P],
                                   ident[0:COMP, 0:COMP])
            mm.then_inc(filled, 1)
            product_chunk(8, 1)
            eng.wait_ge(read67[1], 7)
            wait_fill(0, 6)
            for k in range(2):
                mm = eng.matmul(bank[6][:, 0:COMP // 2], lhsT=wk2[:, k, :], rhs=hidT[:, k * COMP:k * COMP + COMP // 2],
                                start=(k == 0), stop=(k == 1))
            mm.then_inc(filled, 1)
            eng.wait_ge(pad_ready, 1)
            wait_fill(1, 7)
            for g in range(KV_GROUPS):
                for k in range(2):
                    mm = eng.matmul(bank[7][:, g * HD:(g + 1) * HD], lhsT=scr[:, k, g * P:(g + 1) * P],
                                    rhs=wv2[:, k, :], start=(k == 0), stop=(k == 1))
            mm.then_inc(filled, 1)
            product_chunk(9, 0)
            eng.wait_ge(read67[0], 7)
            for odd in range(2):
                half = slice(HD * odd, HD * odd + HD)
                for r in range(RT):
                    for i in range(8):
                        g = i // 2
                        mm = eng.matmul(bank[2 + odd][:, r * P + i * 16:r * P + i * 16 + CMP],
                                        lhsT=headsT[half, i, r * P:(r + 1) * P],
                                        rhs=headsT[half, T2_KC, g * CMP:(g + 1) * CMP], start=True, stop=True)
                mm.then_inc(cs_ready, 1)
            product_chunk(9, 1)
            eng.wait_ge(cn_ready, 1)
            for r in range(RT):
                for g in range(KV_GROUPS):
                    mm = eng.transpose(bank[2 + r][:, g * P:(g + 1) * P], probs[:, r, g * P:(g + 1) * P], ident[:, :])
                mm.then_inc(ct_ready, 1)
            product_chunk(10, 0)
            eng.wait_ge(cT_act, 1)
            eng.wait_ge(cT_dve, 1)
            eng.wait_ge(read67[1], 8)
            for r in range(RT):
                if r:
                    eng.wait_ge(cv_done, 1)
                for g in range(KV_GROUPS):
                    mm = eng.matmul(bank[4 + g // 2][:, (g % 2) * SEQ:(g % 2 + 1) * SEQ],
                                    lhsT=probsT[:, r, g * P:(g + 1) * P], rhs=headsT[:, T2_V + g, :],
                                    start=True, stop=True)
                mm.then_inc(cv_ready, 1)
            product_chunk(10, 1)
            eng.wait_ge(cv_done, 2)
            group_scores(0)
            product_chunk(11, 0)
            attend_turn(A)
            product_chunk(11, 1)
            group_values(0); group_scores(1)
            eng.wait_ge(ws_ready, 1)
            for r in range(RT):
                eng.wait_ge(vn_ready, r + 1)
                for g in range(4):
                    if g % 2 == 0:
                        wait_fill(g // 2, (7, 8)[g // 2] + r)
                    mm = eng.matmul(bank[6 + g // 2][:, (g % 2) * SEQ:(g % 2 + 1) * SEQ], lhsT=w_s[:, g, :],
                                    rhs=z[:, r, g * SEQ:(g + 1) * SEQ], start=True, stop=True)
                    if g % 2:
                        mm.then_inc(filled, 1)
            product_chunk(12, 0)
            attend_turn(A + 1)
            product_chunk(12, 1)
            group_values(1); group_scores(2)
            turn_rows(7, z[:, :, U2:U2 + D])
            three.act = mixT
            product_chunk(13, 0)
            attend_turn(A + 2)
            product_chunk(13, 1)
            three.act = hT
            for b, i in ((14, 2), (15, 3), (16, 4), (17, 5), (18, 6), (19, 7)):
                one = channel_chunk if b >= 16 else product_chunk
                group_values(i); group_scores(i + 1) if i < 7 else None
                if b == 15:
                    three.act = mixT
                one(b, 0)
                if i < 7:
                    attend_turn(A + i + 1)
                one(b, 1)
                three.act = hT
            eng.wait_ge(rg_loaded, 32)

            def gates(c):
                eng.wait_ge(xc_ready, c + 1)
                if c < 2:
                    eng.wait_ge(turned_lo, 32)
                wait_fill(c % 2, (9, 10)[c % 2] + c // 2)
                for v in range(2):
                    for h in range(2):
                        half = slice(HD * h, HD * h + HD)
                        w = z[half, v, KC2 + c * HD:KC2 + (c + 1) * HD]
                        mm = eng.matmul(bank[6 + c % 2][half, v * SEQ:(v + 1) * SEQ], lhsT=w,
                                        rhs=channels(c)[half, :], start=True, stop=True)
                mm.then_inc(filled, 1)

            product_chunk(20, 0)
            for c in range(4):
                gates(c)
            product_chunk(20, 1)
            for c in range(4, 8):
                gates(c)
            eng.wait_ge(read67[0], 13)
            eng.wait_ge(read67[1], 14)
            turn_rows(8)
            for b in range(21, 28):
                three.act = (mixT if b % 2 else hT)
                if b == 25:
                    eng.wait_ge(yc_lo, 1)
                product_chunk(b, 0); product_chunk(b, 1)
            turn_rows(9, z[:, :, U2:U2 + D])
            three.act = mixT
            for b in (28, 29):
                product_chunk(b, 0); product_chunk(b, 1)
            three.act = hT
            turn_half(10, 0)
            eng.wait_ge(turned_lo, 42)
            ffn(p + PAIRS2, LAYERS, 10, lambda r: eng.wait_ge(free[r], product(30)))

        @block.scalar
        def _(eng):
            def split_hi(p, j, n):
                eng.wait_ge(raw_loaded[j], 16 * p + 16)
                eng.wait_ge(used[j], p + 1)
                eng.activation(whi[j][:, 0:n], raw[j][:, 0:n], ACT.Copy).then_inc(hi_ready[j], 1)

            def norm_stats(i):
                for r in range(RT):
                    act(eng.activation(z[:, r, 0:D], x[:, r, :], ACT.Square, accum_out=ssq[:, r:r + 1]))
                act.wait(eng)
                act(eng.activation(ssq[:, 2:4], ssq[:, 0:2], ACT.Ln, bias=eps[:, 0:1], scale=1.0 / D))
                act.wait(eng)
                eng.activation(ssq[:, 4:6], ssq[:, 2:4], ACT.Exp, scale=-0.5).then_inc(rs_ready, 1)

            def turned_hi_copy(i, dst, scale=1.0, halves=(0, 1)):
                for h in halves:
                    for r in range(RT):
                        eng.wait_ge(turned, i * 4 + 2 * h + r + 1)
                        eng.activation(dst[0][:, 4 * h:4 * h + 4, r * P:(r + 1) * P],
                                       bank[6 + r][:, :].rearrange("p (k c) -> p k c", k=4),
                                       ACT.Copy, scale=scale).then_inc(turned_hi, 1)

            def copy_z0(p, l, i, c0, n=COLS):
                eng.wait_ge(half_ready, p)
                eng.activation(z[:, 0, c0:c0 + n], bank[0][:, 0:n], ACT.Copy, scale=ssq[:, 4:5]).then_inc(z_act, 1)

            def head_stats(l, s):
                for r in range(RT):
                    n = 2 * s + r
                    c0 = HEAD_SETS[s]
                    if r == 0:
                        eng.wait_ge(z_dve, l * 8 + (3, 4, 6, 7)[s])
                        eng.wait_ge(z_act, l * 8 + (3, 4, 6, 7)[s])
                        if s:
                            eng.wait_ge(prep, l * 6 + 2 + s)
                    if s or r:
                        eng.wait_ge(ssq_ready, l * 8 + n)
                    eng.activation(sqr[:, :], z[:, r, c0:c0 + COLS], ACT.Square).then_inc(squares, 1)
                    eng.wait_ge(ssq_ready, l * 8 + n + 1)
                    act(eng.activation(ssq[:, 8:16], hss[:, r, :], ACT.Ln, bias=eps[:, 0:1], scale=1.0 / HD))
                    act.wait(eng)
                    eng.activation(hrs[:, r, :], ssq[:, 8:16], ACT.Exp, scale=-0.5).then_inc(hrs_ready, 1)

            def heads_copy(l, s):
                n = (0, 2, 3, 5, 7, 9)[s]
                eng.wait_ge(heads_turned, l * 11 + n + 1)
                t0 = (T_IQ, T_IK, T_DQ, T_DK, T_MQ, T_SQ)[s]
                m = 1 if s == 1 else 2
                eng.activation(headsT[:, t0:t0 + m, :], bank[6][:, 0:m * SEQ].rearrange("p (m c) -> p m c", m=m),
                               ACT.Copy).then_inc(heads_act, 1)

            def index_relu(l, u):
                eng.wait_ge(idx_ready, l * 6 + u + 1)
                if u >= 3:
                    eng.wait_ge(idx_acc, l * 6 + u - 2)
                eng.activation(probs[:, u % 3, :], bank[2 + u % 3][:, :], ACT.Relu, scale=HD ** -0.5)\
                   .then_inc(idx_relu, 1)

            def attend_exp(A, par):
                eng.wait_ge(o_done, A + 1)
                for u in range(3):
                    eng.wait_ge(masked, 3 * A + u + 1)
                    heads = range(4) if u == 0 else range(2)
                    keys = P if u == 0 else SEQ
                    for h in heads:
                        c = h if u == 0 else 4 + 2 * h + u - 1
                        part = probs[:, u, h * keys:(h + 1) * keys]
                        ins = eng.activation(part, part, ACT.Exp, bias=nmax[:, c:c + 1],
                                             accum_out=sums[:, par, c:c + 1])
                        if h == heads[-1]:
                            ins.then_inc(exped, 1)
                        else:
                            act(ins)

            def attend_copy(A):
                for u in range(2):
                    eng.wait_ge(pT_ready, 3 * A + u + 1)
                    eng.wait_ge(pv_ready, A + 1)
                    eng.activation(probsT[:, u, :], bank[2 + u][:, :], ACT.Copy).then_inc(pT_act, 1)

            def diff_stats(l, i):
                eng.wait_ge(dsq, l * 2 + i + 1)
                act(eng.activation(ssq[:, 6:10], dstat[:, 0:4], ACT.Ln, bias=eps[:, 0:1], scale=1.0 / (2 * HD)))
                act.wait(eng)
                eng.activation(dstat[:, 4:8], ssq[:, 6:10], ACT.Exp, scale=-0.5).then_inc(drs, 1)

            def ffn(p0, l, norm, after_n):
                def step(c, n0, n1):
                    split_hi(p0 + c + 1, 0, n0)
                    for r in range(RT):
                        n = l * 2 * FF_STEPS + 2 * c + r
                        if r == 0:
                            eng.wait_ge(rs_ready, norm + 1)
                        eng.wait_ge(gu_ready, n + 1)
                        eng.activation(sqr[:, r * FF_STEP:(r + 1) * FF_STEP], bank[r][:, 0:FF_STEP],
                                       ACT.Silu, scale=ssq[:, 4 + r:5 + r]).then_inc(silu_ready, 1)
                    split_hi(p0 + c + 1, 1, n1)
                    for r in range(RT):
                        n = l * 2 * FF_STEPS + 2 * c + r
                        eng.wait_ge(ff_turned, n + 1)
                        eng.activation(ffT[0][:, :, r * P:(r + 1) * P],
                                       bank[6 + r][:, 0:2 * P].rearrange("p (k c) -> p k c", k=2),
                                       ACT.Copy).then_inc(ff_hi, 1)

                eng.preload_act_table(ACT.Silu)
                with eng.Fori(0, FF_STEPS - 1) as c:
                    step(c, ffn_elements(1, 0), ffn_elements(1, 1))
                step(FF_STEPS - 1, 2 * UNIT, 2 * UNIT)
                eng.preload_act_table_set(LN_EXP)
                if after_n is not None:
                    for j in range(2):
                        after_n(p0 + FF_STEPS + 1, j)

            eng.wait_ge(const_ready, 4)
            eng.wait_ge(x_loaded, 16 * RT)
            eng.sem_inc(pT_act, 2)
            for j in range(2):
                split_hi(0, j, 4 * UNIT)
            act.restart(eng)
            eng.preload_act_table_set(LN_EXP)
            with eng.Fori(0, LAYERS) as l:
                p, A = l * PAIRS1, l * NGRP
                hi = lambda i, j: split_hi(p + i, j, 4 * (NARROW if i == 1 else COLS))
                hr = lambda i: l * HALVES + i + 1
                turned_hi_copy(l * 3, hT)
                norm_stats(2 * l)
                hi(1, 0)
                eng.wait_ge(rs_ready, 2 * l + 1)
                copy_z0(hr(0), l, 0, IQ); hi(1, 1)
                hi(2, 0); copy_z0(hr(1), l, 1, IK, NARROW); hi(2, 1)
                eng.wait_ge(lam_sum, l + 1)
                eng.activation(lam[:, 2:4], lam[:, 0:2], ACT.Exp).then_inc(lam_exp, 1)
                hi(3, 0); copy_z0(hr(2), l, 2, DQ); hi(3, 1); heads_copy(l, 0)
                head_stats(l, 0)
                hi(4, 0); heads_copy(l, 1); copy_z0(hr(3), l, 3, DK); hi(4, 1)
                head_stats(l, 1)
                for u in range(3):
                    index_relu(l, u)
                hi(5, 0); heads_copy(l, 2)
                for u in range(3, 6):
                    index_relu(l, u)
                heads_copy(l, 3); copy_z0(hr(4), l, 4, DV); hi(5, 1)
                attend_exp(A, 0)
                hi(6, 0); copy_z0(hr(5), l, 5, MQ); hi(6, 1)
                attend_copy(A)
                head_stats(l, 2)
                hi(7, 0)
                attend_exp(A + 1, 1)
                diff_stats(l, 0)
                copy_z0(hr(6), l, 6, SQ); hi(7, 1)
                attend_copy(A + 1)
                heads_copy(l, 4)
                head_stats(l, 3)
                hi(8, 0)
                attend_exp(A + 2, 0)
                copy_z0(hr(7), l, 7, MV)
                attend_copy(A + 2)
                heads_copy(l, 5)
                diff_stats(l, 1)
                hi(8, 1)
                attend_exp(A + 3, 1)
                turned_hi_copy(l * 3 + 1, mixT, halves=(0,))
                attend_copy(A + 3)
                hi(9, 0)
                turned_hi_copy(l * 3 + 1, mixT, halves=(1,))
                hi(9, 1)
                split_hi(p + 10, 0, ffn_elements(0, 0))
                turned_hi_copy(l * 3 + 2, hT, halves=(0,))
                split_hi(p + 10, 1, ffn_elements(0, 1))
                turned_hi_copy(l * 3 + 2, hT, halves=(1,))
                norm_stats(2 * l + 1)

                def after(pp, j):
                    split_hi(pp, j, 4 * UNIT)
                ffn(p + 10, l, 2 * l + 1, after)
                act.restart(eng)
                eng.wait_ge(down_added, l * 4 + 4)

            A = LAYERS * NGRP

            def hi2(b, j):
                n = ffn_elements(0, j) if b == PAIRS2 else 4 * (GATES if b == 4 else COLS)
                split_hi(B2 + b, j, n)

            def whole(b, r):
                if r == 0:
                    eng.wait_ge(half_ready, half_of(b))
                else:
                    eng.wait_ge(used[1], B2 + b + 2)

            def take(b, r, dst, func, n=COLS, scale=1.0):
                whole(b, r)
                eng.activation(dst, bank[r][:, 0:n], func, scale=scale).then_inc(free[r], 1)

            def fill_copy(n, count, t0):
                eng.wait_ge(filled, count)
                eng.activation(headsT[:, t0:t0 + 2, :], bank[6][:, :].rearrange("p (m c) -> p m c", m=2),
                               ACT.Copy).then_inc(read67[0], 1)

            def branch_gate(b, r):
                n = {12: 0, 14: 1, 20: 2, 22: 3, 24: 4, 26: 5}[b]
                if n:
                    eng.wait_ge(merged_done, 2 * n)
                take(b, r, scr[:, r, :], ACT.Tanh, scale=0.5)

            def gates(c):
                eng.wait_ge(filled, F_GATE + c)
                if c >= 2:
                    eng.wait_ge(gx_done, c - 1)
                b, buf = bank[6 + c % 2], probs[:, c % 2, :]
                act(eng.activation(buf[:, 0:SEQ], b[:, 0:SEQ], ACT.Tanh, scale=0.5, bias=sp[:, 88 + c:89 + c]))
                eng.activation(buf[:, SEQ:2 * SEQ], b[:, SEQ:2 * SEQ], ACT.Tanh, scale=0.5,
                               bias=sp[:, 96 + c:97 + c]).then_inc(read67[c % 2], 1)
                act.wait(eng)
                eng.activation(headsT[:, c, :], buf[:, 0:SEQ], ACT.Tanh, scale=sp[:, 80 + c:81 + c],
                               bias=sp[:, 80 + c:81 + c]).then_inc(u_ready, 1)

            def row_stats(i, src, junk):
                eng.preload_act_table_set(LN_EXP)
                for r in range(RT):
                    act(eng.activation(junk[:, r, 0:D], src[:, r, 0:D], ACT.Square, accum_out=ssq[:, r:r + 1]))
                act.wait(eng)
                act(eng.activation(ssq[:, 2:4], ssq[:, 0:2], ACT.Ln, bias=eps[:, 0:1], scale=1.0 / D))
                act.wait(eng)
                eng.activation(ssq[:, 4:6], ssq[:, 2:4], ACT.Exp, scale=-0.5).then_inc(rs_ready, 1)

            norm_stats(4)
            eng.wait_ge(sp_abs, 1)
            eng.activation(sp[:, 8:16], sp[:, 0:8], ACT.Exp).then_inc(sp_exp, 1)
            eng.wait_ge(sp_one, 1)
            eng.activation(sp[:, 24:32], sp[:, 16:24], ACT.Ln).then_inc(sp_ln, 1)
            turned_hi_copy(6, hT)
            hi2(1, 0); take(0, 0, z[:, 0, KC2:KC2 + COLS], ACT.Copy); hi2(1, 1)
            hi2(2, 0); take(1, 0, z[:, 0, Q2:Q2 + COLS], ACT.Copy, scale=HD ** -0.5); hi2(2, 1)
            hi2(3, 0); take(2, 0, z[:, 0, Q2 + COLS:Q2 + D], ACT.Copy, scale=HD ** -0.5); hi2(3, 1)
            hi2(4, 0); take(3, 0, z[:, 0, KS2:KS2 + COLS], ACT.Copy); hi2(4, 1)
            fill_copy(0, F_Q, 0)
            fill_copy(0, F_Q + 2, 4)
            hi2(5, 0)
            take(4, 0, z[:, 0, G2:G2 + GATES], ACT.Tanh, GATES, 0.5)
            take(4, 1, z[:, 1, G2:G2 + GATES], ACT.Tanh, GATES, 0.5)
            hi2(5, 1)
            eng.wait_ge(flat_done, 1)
            eng.activation(flat[0].rearrange("p j m -> p (j m)"), flat_f, ACT.Copy).then_inc(flat_hi, 1)
            hi2(6, 0); fill_copy(0, F_SK, T2_KS); take(5, 0, z[:, 0, KW2:KW2 + COLS], ACT.Copy); hi2(6, 1)
            hi2(7, 0); fill_copy(0, F_WK, T2_KW); hi2(7, 1)
            hi2(8, 0)
            for v in range(2):
                whole(7, v)
                eng.activation(sqr[0:COMP, v * SEQ:(v + 1) * SEQ], bank[v][0:COMP, 0:SEQ],
                               ACT.Gelu_apprx_tanh).then_inc(free[v], 1)
            hi2(8, 1)
            hi2(9, 0)
            eng.wait_ge(filled, F_HT)
            eng.activation(hidT, bank[7][:, 0:4 * COMP], ACT.Copy).then_inc(read67[1], 1)
            eng.wait_ge(filled, F_Q + 3)
            take(8, 0, z[:, 0, 0:COLS], ACT.Gelu_apprx_tanh)
            take(8, 1, z[:, 1, 0:COLS], ACT.Gelu_apprx_tanh)
            hi2(9, 1)
            eng.wait_ge(filled, F_KC)
            eng.activation(headsT[:, T2_KC, 0:COMP // 2], bank[6][:, 0:COMP // 2], ACT.Copy).then_inc(read67[0], 1)
            eng.wait_ge(cm_ready, 1)
            wide = probs[:, 0:2, :].rearrange("p r (h n) -> p (r h) n", n=32)[:, :, 0:CMP]
            eng.activation(wide, wide, ACT.Exp).then_inc(ce_ready, 1)
            hi2(10, 0)
            take(9, 0, z[:, 0, COLS:D], ACT.Gelu_apprx_tanh)
            take(9, 1, z[:, 1, COLS:D], ACT.Gelu_apprx_tanh)
            hi2(10, 1)
            eng.wait_ge(ct_ready, 1)
            eng.activation(probsT[:, 0, :], bank[2][:, :], ACT.Copy).then_inc(cT_act, 1)
            eng.preload_act_table_set(LN_EXP)
            eng.wait_ge(var_ready, 1)
            act(eng.activation(bn[:, 30:32], bn[:, 24:28].rearrange("p (r s) -> p r s", s=2)[:, :, 1], ACT.Ln,
                               bias=eps[:, 0:1]))
            act.wait(eng)
            eng.activation(bn[:, 28:30], bn[:, 30:32], ACT.Exp, scale=-0.5).then_inc(vrs_ready, 1)
            hi2(11, 0)
            take(10, 0, z[:, 0, U2:U2 + COLS], ACT.Gelu_apprx_tanh)
            take(10, 1, z[:, 1, U2:U2 + COLS], ACT.Gelu_apprx_tanh)
            hi2(11, 1)
            attend_exp(A, 0)
            hi2(12, 0); attend_copy(A)
            take(11, 0, z[:, 0, U2 + COLS:U2 + D], ACT.Gelu_apprx_tanh)
            take(11, 1, z[:, 1, U2 + COLS:U2 + D], ACT.Gelu_apprx_tanh)
            hi2(12, 1)
            for b in range(12, 19):
                i = b - 11
                attend_exp(A + i, i % 2)
                hi2(b + 1, 0)
                attend_copy(A + i)
                if b in (12, 14):
                    branch_gate(b, 0); branch_gate(b, 1)
                if b == 18:
                    for r in range(2):
                        take(b, r, headsT[:, 8 + 2 * r:10 + 2 * r, :].rearrange("p a c -> p (a c)"), ACT.Gelu_apprx_tanh)
                hi2(b + 1, 1)
                if b == 12:
                    turned_hi_copy(7, mixT)
            hi2(20, 0)
            for r in range(2):
                take(19, r, headsT[:, 12 + 2 * r:14 + 2 * r, :].rearrange("p a c -> p (a c)"), ACT.Gelu_apprx_tanh)
            hi2(20, 1)
            hi2(21, 0)
            for c in range(4):
                gates(c)
            branch_gate(20, 0); branch_gate(20, 1)
            hi2(21, 1)
            for c in range(4, 8):
                gates(c)
            turned_hi_copy(8, mixT)
            hi2(22, 0); hi2(22, 1)
            eng.wait_ge(u_read, 1)
            eng.activation(headsT[:, 0:8, :], headsT[:, 0:8, :], ACT.Sqrt).then_inc(root_ready, 1)
            hi2(23, 0); branch_gate(22, 0); branch_gate(22, 1); hi2(23, 1)
            hi2(24, 0); hi2(24, 1)
            hi2(25, 0); branch_gate(24, 0); branch_gate(24, 1); hi2(25, 1)
            eng.wait_ge(yc_ready, 1)
            eng.wait_ge(used[1], B2 + 23 + 2)
            eng.activation(mixT[0][:, :, :], headsT[:, 0:8, :], ACT.Copy).then_inc(yc_hi, 1)
            hi2(26, 0); hi2(26, 1)
            hi2(27, 0); branch_gate(26, 0); branch_gate(26, 1); hi2(27, 1)
            hi2(28, 0); hi2(28, 1)
            turned_hi_copy(9, mixT, scale=0.5)
            hi2(29, 0); take(28, 0, mix[:, 0, 0:COLS], ACT.Copy); hi2(29, 1)
            hi2(30, 0); take(29, 0, mix[:, 0, COLS:D], ACT.Copy); hi2(30, 1)
            for r in range(RT):
                eng.wait_ge(free[r], product(30))
            row_stats(5, mix, z)
            turned_hi_copy(10, hT)
            eng.wait_ge(x_added, RT)
            row_stats(6, x, z)
            ffn(B2 + PAIRS2, LAYERS, 6, None)
            eng.wait_ge(down_added, 4 * LAYERS + 4)
            row_stats(7, mix, z)

        @block.vector
        def _(eng):
            def split_lo(p, j, n):
                eng.wait_ge(hi_ready[j], p + 1)
                eng.tensor_tensor(wlo[j][:, 0:n], raw[j][:, 0:n], whi[j][:, 0:n].bitcast(F32),
                                  ALU.subtract).then_inc(lo_ready[j], 1)

            def gain_rows(r, h, g=gain):
                cols = slice(h * COLS, (h + 1) * COLS)
                eng.tensor_tensor(mix[:, r, cols], x[:, r, cols], g[:, cols], ALU.mult).then_inc(rows_ready, 1)

            def turned_lo_copy(i, dst, scale=None, halves=(0, 1)):
                for h in halves:
                    for r in range(RT):
                        n = i * 4 + 2 * h + r
                        eng.wait_ge(turned_hi, n + 1)
                        cols = slice(r * P, (r + 1) * P)
                        high = dst[0][:, 4 * h:4 * h + 4, cols].bitcast(F32)
                        low = dst[1][:, 4 * h:4 * h + 4, cols]
                        src = bank[6 + r][:, :].rearrange("p (k c) -> p k c", k=4)
                        if scale is None:
                            ins = eng.tensor_tensor(low, src, high, ALU.subtract)
                        else:
                            ins = eng.scalar_tensor_tensor(out=low, in0=src, scalar=scale, in1=high,
                                                           op0=ALU.mult, op1=ALU.subtract)
                        ins.then_inc(turned_lo, 1)

            def copy_z1(p, c0, n=COLS):
                eng.wait_ge(used[1], p + 2)
                eng.tensor_scalar(z[:, 1, c0:c0 + n], bank[1][:, 0:n], ssq[:, 5:6], None, ALU.mult)\
                   .then_inc(z_dve, 1)

            def tables(l):
                eng.wait_ge(par_loaded, 64 * l + 64)
                dve(eng.tensor_scalar(hgain[:, 0:3, :], hgain[:, 0:3, :], HD ** -0.5, None, ALU.mult))
                dve.wait(eng)
                h = HD // 2
                for r in range(RT):
                    dve(eng.tensor_tensor(gain_c[:, r], hgain[:, :, :],
                                          rope_c[:, r, :].unsqueeze(1).to_broadcast([P, 6, HD]), ALU.mult))
                    for a, b in ((0, h), (h, 0)):
                        dve(eng.tensor_tensor(gain_s[:, r, :, a:a + h], hgain[:, :, b:b + h],
                                              rope_s[:, r, a:a + h].unsqueeze(1).to_broadcast([P, 6, h]), ALU.mult))
                dve(eng.tensor_tensor(scr[:, 0, 0:HD], lamp[:, 0, :], lamp[:, 1, :], ALU.mult))
                dve(eng.tensor_tensor(scr[:, 0, HD:2 * HD], lamp[:, 2, :], lamp[:, 3, :], ALU.mult))
                dve.wait(eng)
                eng.sem_inc(tables_ready, 1)
                eng.tensor_reduce(lam[:, 0:2], scr[:, 0, 0:2 * HD].rearrange("p (a d) -> p a d", a=2), AX.X,
                                  ALU.add).then_inc(lam_sum, 1)

            def lambda_value(l):
                eng.wait_ge(lam_exp, l + 1)
                dve(eng.tensor_tensor(lam[:, 0:1], lam[:, 2:3], lam[:, 3:4], ALU.subtract))
                dve.wait(eng)
                dve(eng.tensor_tensor(lam[:, 0:1], lam[:, 0:1], lam_c[:, 0:1], ALU.add))
                dve(eng.tensor_scalar(sub_g[:, :], sub_g[:, :], lam_c[:, 1:2], None, ALU.mult))
                dve.wait(eng)

            def head_sums(l, s):
                for r in range(RT):
                    eng.wait_ge(squares, l * 8 + 2 * s + r + 1)
                    eng.tensor_reduce(hss[:, r, :], sqr[:, :].rearrange("p (n d) -> p n d", d=HD), AX.X,
                                      ALU.add).then_inc(ssq_ready, 1)

            def heads_copy(l, s):
                n = (0, None, 3, 5, 7, 9)[s]
                eng.wait_ge(heads_turned, l * 11 + n + 2)
                t0 = (T_IQ, None, T_DQ, T_DK, T_MQ, T_SQ)[s] + 2
                eng.tensor_copy(headsT[:, t0:t0 + 2, :], bank[7][:, :].rearrange("p (m c) -> p m c", m=2))\
                   .then_inc(heads_dve, 1)

            def index_sum(l, u):
                eng.wait_ge(idx_relu, l * 6 + u + 1)
                r, keys = (0, P) if u < 2 else (1, SEQ)
                acc = index[:, 0:P] if u < 2 else index[:, P:3 * P]
                for i, h in enumerate(index_heads(u)):
                    part, w = probs[:, u % 3, i * keys:(i + 1) * keys], z[:, r, IW + h:IW + h + 1]
                    if h == 0:
                        ins = eng.tensor_scalar(acc, part, w, None, ALU.mult)
                    else:
                        ins = eng.scalar_tensor_tensor(out=acc, in0=part, scalar=w, in1=acc, op0=ALU.mult,
                                                       op1=ALU.add)
                    if i == (3 if u < 2 else 1):
                        ins.then_inc(idx_acc, 1)
                        eng.wait_ge(idx_acc, l * 6 + u + 1)
                    else:
                        dve(ins)
                        dve.wait(eng)

            def topk_rounds(a, b):
                if a == 0:
                    dve(eng.tensor_tensor(index[:, :], index[:, :], causal[:, :], ALU.add))
                    dve.wait(eng)
                for _ in range(a, b):
                    for r, part in enumerate((index[:, 0:P], index[:, P:3 * P])):
                        dve(eng.max(top8[:, r, :], part))
                    dve.wait(eng)
                    for r, part in enumerate((index[:, 0:P], index[:, P:3 * P])):
                        dve(eng.match_replace(part, top8[:, r, :], part, TAKEN))
                    dve.wait(eng)

            def topk_mask():
                dve(eng.tensor_scalar(chosen[:, :], index[:, :], TAKEN / 2, NEG, ALU.is_gt, ALU.mult))
                dve.wait(eng)
                dve(eng.tensor_tensor(chosen[:, :], chosen[:, :], causal[:, :], ALU.add))
                dve.wait(eng)

            def attend_mask(A, mask):
                for u in range(3):
                    eng.wait_ge(scores, 3 * A + u + 1)
                    n, keys = (4, P) if u == 0 else (2, SEQ)
                    m = mask[:, 0:P] if u == 0 else mask[:, P:3 * P]
                    part = probs[:, u, :].rearrange("p (n k) -> p n k", n=n)
                    dve(eng.tensor_tensor(part, bank[2 + u][:, :].rearrange("p (n k) -> p n k", n=n),
                                          m.unsqueeze(1).to_broadcast([P, n, keys]), ALU.add))
                    dve.wait(eng)
                    top = nmax[:, 0:4] if u == 0 else \
                        nmax[:, 4:8].rearrange("p (n two) -> p n two", two=2)[:, :, u - 1]
                    eng.tensor_reduce(top, part, AX.X, ALU.max, negate=True).then_inc(masked, 1)

            def attend_copy(A):
                eng.wait_ge(pT_ready, 3 * A + 3)
                eng.wait_ge(pv_ready, A + 1)
                eng.tensor_copy(probsT[:, 2, :], bank[4][:, :]).then_inc(pT_dve, 1)

            def attend_out(A, par, dst):
                eng.wait_ge(pv_ready, A + 2)
                dve(eng.reciprocal(inv[:, :], sums[:, par, :]))
                dve.wait(eng)
                for r in range(RT):
                    ins = eng.tensor_tensor(dst(r), bank[5][:, r * SEQ:(r + 1) * SEQ].rearrange("p (n d) -> p n d", d=HD),
                                            inv[:, 4 * r:4 * r + 4].unsqueeze(2).to_broadcast([P, 4, HD]), ALU.mult)
                    if r:
                        ins.then_inc(o_done, 1)
                    else:
                        dve(ins)

            def diff_out(A, par):
                eng.wait_ge(pv_ready, A + 2)
                dve(eng.reciprocal(inv[:, :], sums[:, par, :]))
                dve.wait(eng)
                odd = inv[:, :].rearrange("p (n two) -> p n two", two=2)[:, :, 1:2]
                dve(eng.tensor_scalar(odd, odd, lam[:, 0:1], None, ALU.mult))
                dve.wait(eng)
                W = 2 * HD
                for r in range(RT):
                    o = bank[5 + r][:, :].rearrange("p (n two d) -> p n two d", two=2, d=W)
                    c = inv[:, 4 * r:4 * r + 4].rearrange("p (n two) -> p n two", two=2)
                    for w in range(2):
                        ins = eng.tensor_tensor(scr[:, w, r * 2 * W:(r + 1) * 2 * W].rearrange("p (n d) -> p n d", d=W),
                                                o[:, :, w, :], c[:, :, w:w + 1].to_broadcast([P, 2, W]), ALU.mult)
                        if r and w:
                            ins.then_inc(o_done, 1)
                            eng.wait_ge(o_done, A + 3)
                        else:
                            dve(ins)
                dve.wait(eng)
                dve(eng.tensor_tensor(scr[:, 0, :], scr[:, 0, :], scr[:, 1, :], ALU.subtract))
                dve.wait(eng)
                dve(eng.tensor_tensor(scr[:, 1, :], scr[:, 0, :], scr[:, 0, :], ALU.mult))
                dve.wait(eng)
                eng.tensor_reduce(dstat[:, 0:4], scr[:, 1, :].rearrange("p (n d) -> p n d", d=W), AX.X, ALU.add)\
                   .then_inc(dsq, 1)

            def diff_norm(l, i):
                W = 2 * HD
                a4 = scr[:, 0, :].rearrange("p (n d) -> p n d", d=W)
                dve(eng.tensor_tensor(a4, a4, sub_g[:, :].unsqueeze(1).to_broadcast([P, 4, W]), ALU.mult))
                dve.wait(eng)
                eng.wait_ge(drs, l * 2 + i + 1)
                dve(eng.tensor_tensor(mix[:, :, SEQ + 2 * i * W:SEQ + 2 * (i + 1) * W].rearrange("p r (n d) -> p r n d", d=W),
                                      scr[:, 0, :].rearrange("p (r n d) -> p r n d", r=2, d=W),
                                      dstat[:, 4:8].rearrange("p (r n) -> p r n", r=2).unsqueeze(3).to_broadcast([P, 2, 2, W]),
                                      ALU.mult))
                dve.wait(eng)

            def ffn(p0, l, norm, after):
                def step(c, n0, n1):
                    split_lo(p0 + c + 1, 0, n0)
                    for r in range(RT):
                        n = l * 2 * FF_STEPS + 2 * c + r
                        if r == 0:
                            eng.wait_ge(rs_ready, norm + 1)
                        eng.wait_ge(silu_ready, n + 1)
                        eng.scalar_tensor_tensor(out=probs[:, r, 0:FF_STEP], in0=bank[r][:, FF_STEP:2 * FF_STEP],
                                                 scalar=ssq[:, 4 + r:5 + r], in1=sqr[:, r * FF_STEP:(r + 1) * FF_STEP],
                                                 op0=ALU.mult, op1=ALU.mult).then_inc(gu_free, 1)
                    split_lo(p0 + c + 1, 1, n1)
                    for r in range(RT):
                        n = l * 2 * FF_STEPS + 2 * c + r
                        eng.wait_ge(ff_hi, n + 1)
                        eng.tensor_tensor(ffT[1][:, :, r * P:(r + 1) * P],
                                          bank[6 + r][:, 0:2 * P].rearrange("p (k c) -> p k c", k=2),
                                          ffT[0][:, :, r * P:(r + 1) * P].bitcast(F32), ALU.subtract)\
                           .then_inc(ff_lo, 1)

                with eng.Fori(0, FF_STEPS - 1) as c:
                    step(c, ffn_elements(1, 0), ffn_elements(1, 1))
                step(FF_STEPS - 1, 2 * UNIT, 2 * UNIT)
                for n in range(2):
                    for r in range(RT):
                        i = 2 * n + r
                        if i < 3:
                            eng.wait_ge(down_ready, l * 3 + i + 1)
                        else:
                            eng.wait_ge(used[1], p0 + FF_STEPS + 2)
                        part = x[:, r, n * COLS:(n + 1) * COLS]
                        if after is None:
                            eng.tensor_copy(mix[:, r, n * COLS:(n + 1) * COLS], bank[2 + i][:, :])\
                               .then_inc(down_added, 1)
                        else:
                            eng.tensor_tensor(part, part, bank[2 + i][:, :], ALU.add).then_inc(down_added, 1)
                            after(n, r)

            eng.wait_ge(const_ready, 4)
            for j in range(2):
                eng.sem_inc(lo_ready[j], 1)
            eng.sem_inc(pT_dve, 1)
            eng.sem_inc(o_done, 2)
            eng.wait_ge(x_loaded, 16 * RT)
            eng.wait_ge(gain_loaded, 16)
            for h in range(2):
                for r in range(RT):
                    gain_rows(r, h)
            eng.wait_ge(rows_ready, 4)
            eng.sem_inc(gain_free, 1)
            for j in range(2):
                split_lo(0, j, 4 * UNIT)
            eng.wait_ge(rope_loaded, 32)
            dve.restart(eng)
            with eng.Fori(0, LAYERS) as l:
                p, A = l * PAIRS1, l * NGRP
                lo = lambda i, j: split_lo(p + i, j, 4 * (NARROW if i == 1 else COLS))

                def take(c0, n, width):
                    return lambda r: mix[:, r, c0:c0 + n * width].rearrange("p (n d) -> p n d", d=width)

                turned_lo_copy(l * 3, hT)
                tables(l)
                lo(1, 0)
                eng.wait_ge(rs_ready, 2 * l + 1)
                copy_z1(p, IQ); lo(1, 1)
                lo(2, 0); copy_z1(p + 1, IK, NARROW); lo(2, 1)
                lambda_value(l)
                lo(3, 0); copy_z1(p + 2, DQ); lo(3, 1); heads_copy(l, 0)
                head_sums(l, 0)
                lo(4, 0); copy_z1(p + 3, DK); lo(4, 1)
                head_sums(l, 1)
                for u in range(3):
                    index_sum(l, u)
                lo(5, 0); heads_copy(l, 2)
                for u in range(3, 6):
                    index_sum(l, u)
                heads_copy(l, 3)
                topk_rounds(0, 3)
                copy_z1(p + 4, DV); lo(5, 1)
                attend_mask(A, causal)
                topk_rounds(3, 4)
                lo(6, 0); copy_z1(p + 5, MQ); lo(6, 1)
                attend_copy(A)
                head_sums(l, 2)
                topk_rounds(4, 5)
                attend_mask(A + 1, causal)
                lo(7, 0)
                diff_out(A, 0); diff_norm(l, 0)
                copy_z1(p + 6, SQ); lo(7, 1)
                attend_copy(A + 1)
                heads_copy(l, 4)
                head_sums(l, 3)
                topk_rounds(5, 7)
                attend_mask(A + 2, causal)
                diff_out(A + 1, 1)
                copy_z1(p + 7, MV)
                attend_copy(A + 2)
                heads_copy(l, 5)
                diff_norm(l, 1)
                topk_rounds(7, 8); topk_mask()
                attend_mask(A + 3, chosen)
                attend_out(A + 2, 0, take(0, 4, HD))
                eng.wait_ge(o_done, A + 5)
                dve.wait(eng)
                eng.sem_inc(rows_ready, 2)
                lo(8, 0)
                turned_lo_copy(l * 3 + 1, mixT, halves=(0,))
                attend_copy(A + 3)
                lo(8, 1)
                attend_out(A + 3, 1, take(768, 4, HD))
                eng.wait_ge(o_done, A + 6)
                dve.wait(eng)
                eng.sem_inc(rows_ready, 2)
                turned_lo_copy(l * 3 + 1, mixT, halves=(1,))
                lo(9, 0)

                def add_out(i, r):
                    if r == 0:
                        eng.wait_ge(half_ready, l * HALVES + 8 + i + 1)
                    else:
                        eng.wait_ge(used[1], p + 8 + i + 2)
                    part = x[:, r, i * COLS:(i + 1) * COLS]
                    eng.tensor_tensor(part, part, bank[r][:, :], ALU.add).then_inc(out_added, 1)
                    eng.wait_ge(out_added, l * 4 + 2 * i + r + 1)
                    gain_rows(r, i)

                eng.wait_ge(gain_loaded, 16 * (2 * l + 1) + 16)
                add_out(0, 0); add_out(0, 1)
                lo(9, 1)
                split_lo(p + 10, 0, ffn_elements(0, 0))
                turned_lo_copy(l * 3 + 2, hT, halves=(0,))
                add_out(1, 0); add_out(1, 1)
                turned_lo_copy(l * 3 + 2, hT, halves=(1,))
                split_lo(p + 10, 1, ffn_elements(0, 1))
                eng.wait_ge(rows_ready, 12 * l + 12)
                eng.sem_inc(gain_free, 1)

                def after(n, r):
                    eng.wait_ge(down_added, l * 4 + 2 * n + r + 1)
                    if n == 0 and r == 0:
                        eng.wait_ge(gain_loaded, 16 * (2 * l + 2) + 16)
                    gain_rows(r, n)
                    if n == 0 and r == 1:
                        split_lo(p + PAIRS1, 0, 4 * UNIT)
                    if n == 1 and r == 1:
                        split_lo(p + PAIRS1, 1, 4 * UNIT)
                ffn(p + 10, l, 2 * l + 1, after)
                eng.wait_ge(rows_ready, 12 * l + 16)
                eng.sem_inc(gain_free, 1)
                dve.restart(eng)
                eng.wait_ge(down_added, l * 4 + 4)

            A = LAYERS * NGRP

            def lo2(b, j):
                n = ffn_elements(0, j) if b == PAIRS2 else 4 * (GATES if b == 4 else COLS)
                split_lo(B2 + b, j, n)

            def whole(b, r):
                if r == 0:
                    eng.wait_ge(half_ready, half_of(b))
                else:
                    eng.wait_ge(used[1], B2 + b + 2)

            def take1(b, dst, scale=None):
                whole(b, 1)
                if scale is None:
                    ins = eng.tensor_copy(dst, bank[1][:, :])
                else:
                    ins = eng.tensor_scalar(dst, bank[1][:, :], scale, None, ALU.mult)
                ins.then_inc(free[1], 1)

            def twice(dst, c0, count):
                for r in range(RT):
                    ins = eng.tensor_copy(dst[:, r, :].rearrange("p (g a d) -> p g a d", g=KV_GROUPS, a=2),
                                          z[:, r, c0:c0 + KV_GROUPS * HD].rearrange("p (g d) -> p g d", d=HD)
                                          .unsqueeze(2).to_broadcast([P, KV_GROUPS, 2, HD]))
                    if r:
                        ins.then_inc(dup_ready, 1)
                    else:
                        dve(ins)

            def blocks(v, first):
                dst = flat_f.rearrange("p (j v g n) -> p j v g n", v=2, g=KV_GROUPS, n=CMP)
                for g in range(KV_GROUPS):
                    b = bank[6 + g // 2]
                    if g % 2 == 0:
                        eng.wait_ge(filled, first + g // 2)
                    for h in range(2):
                        half = slice(HD * h, HD * h + HD)
                        src = AP_of(b[half, :], (g % 2) * SEQ + h, [[2, COMP_K], [16, CMP]])
                        ins = eng.tensor_tensor(dst[half, :, v, g, :], src,
                                                pe_kv[half, v, :].unsqueeze(2).to_broadcast([HD, COMP_K, CMP]),
                                                ALU.add)
                        if g % 2 and h:
                            ins.then_inc(read67[g // 2], 1)
                        else:
                            dve(ins)

            def fill_copy(count, t0):
                eng.wait_ge(filled, count)
                eng.tensor_copy(headsT[:, t0:t0 + 2, :], bank[7][:, :].rearrange("p (m c) -> p m c", m=2))\
                   .then_inc(read67[1], 1)

            def gate_of(r, g, branch):
                a = G2 + 12 * g
                return z[:, r, a:a + 12].rearrange("p (h b) -> p h b", b=3)[:, :, branch]

            def group_out(i):
                g, branch = i % 4, 1 + i // 4
                eng.wait_ge(pv_ready, A + i + 2)
                dve(eng.reciprocal(inv[:, :], sums[:, i % 2, :]))
                dve.wait(eng)
                for r in range(RT):
                    dve(eng.tensor_tensor(inv[:, 4 * r:4 * r + 4], inv[:, 4 * r:4 * r + 4], gate_of(r, g, branch),
                                          ALU.mult))
                dve.wait(eng)
                eng.tensor_tensor(sqr[:, :].rearrange("p (n d) -> p n d", d=HD),
                                  bank[5][:, :].rearrange("p (n d) -> p n d", d=HD),
                                  inv[:, :].unsqueeze(2).to_broadcast([P, 8, HD]), ALU.mult).then_inc(o_done, 1)
                eng.wait_ge(o_done, A + i + 3)
                part = mix[:, :, g * SEQ:(g + 1) * SEQ]
                dve(eng.tensor_tensor(part, part, sqr[:, :].rearrange("p (r c) -> p r c", r=2), ALU.add))
                dve.wait(eng)

            def merge(b):
                n = (b // 2) % 2
                first = b < 16
                for r in range(RT):
                    whole(b, r)
                    eng.wait_ge(free[r], product(b))
                    dst = merged(r, n) if first else scr[:, r, :]
                    eng.scalar_tensor_tensor(out=dst, in0=scr[:, r, :], scalar=1.0, in1=bank[r][:, :],
                                             op0=ALU.add, op1=ALU.mult).then_inc(free[r], 1)
                    eng.wait_ge(free[r], product(b) + 1)
                    if first:
                        eng.sem_inc(merged_done, 1)
                    else:
                        eng.tensor_tensor(merged(r, n), merged(r, n), scr[:, r, :], ALU.add).then_inc(merged_done, 1)

            def convolve(b):
                for q in range(4):
                    c = 4 * (b - 16) + q
                    if q % 2 == 0:
                        whole(b, q // 2)
                    src, dst = bank[q // 2][:, (q % 2) * SEQ:(q % 2 + 1) * SEQ], channels(c)
                    cw = lambda j: par_cw[:, 4 * c + j:4 * c + j + 1]
                    dve(eng.tensor_scalar(dst, src, cw(3), par_cb[:, c:c + 1], ALU.mult, ALU.add))
                    dve.wait(eng)
                    for back in (1, 2, 3):
                        ins = eng.scalar_tensor_tensor(out=dst[:, back:], in0=src[:, 0:SEQ - back],
                                                       scalar=cw(3 - back), in1=dst[:, back:],
                                                       op0=ALU.mult, op1=ALU.add)
                        if back == 3 and q % 2:
                            ins.then_inc(free[q // 2], 1)
                            eng.wait_ge(free[q // 2], product(b) + 1)
                            eng.sem_inc(xc_ready, 2)
                        else:
                            dve(ins)
                            dve.wait(eng)

            def gated_input(c):
                eng.wait_ge(read67[c % 2], (10, 11)[c % 2] + c // 2)
                eng.wait_ge(u_ready, c + 1)
                eng.scalar_tensor_tensor(out=channels(c), in0=probs[:, c % 2, SEQ:2 * SEQ], scalar=1.0,
                                         in1=channels(c), op0=ALU.add, op1=ALU.mult).then_inc(gx_done, 1)

            def post_add(i, gain_i, last_of):
                eng.wait_ge(rs_ready, i + 1)
                eng.wait_ge(gain_loaded, 16 * gain_i + 16)
                for r in range(RT):
                    dve(eng.scalar_tensor_tensor(out=z[:, r, 0:D], in0=mix[:, r, :], scalar=ssq[:, 4 + r:5 + r],
                                                 in1=gain[:, :], op0=ALU.mult, op1=ALU.mult))
                dve.wait(eng)
                eng.sem_inc(gain_free, 1)
                for r in range(RT):
                    eng.tensor_tensor(x[:, r, :], x[:, r, :], z[:, r, 0:D], ALU.add).then_inc(x_added, 1)
                eng.wait_ge(x_added, last_of)

            eng.wait_ge(rs_ready, 5)
            for h in range(2):
                for r in range(RT):
                    part = mix[:, r, h * COLS:(h + 1) * COLS]
                    eng.tensor_scalar(part, part, ssq[:, 4 + r:5 + r], None, ALU.mult).then_inc(rows_ready, 1)
            eng.wait_ge(small_loaded, 32)
            dve(eng.tensor_scalar(sp[:, 0:8], par_lam, -1.0, None, ALU.mult))
            dve(eng.tensor_scalar(sp[:, 32:40], par_lam, -1.0, 0.0, ALU.mult, ALU.max))
            dve.wait(eng)
            eng.tensor_tensor(sp[:, 0:8], sp[:, 0:8], par_lam, ALU.min).then_inc(sp_abs, 1)
            dve(eng.tensor_scalar(sp[:, 88:96], par_ba, 0.5, None, ALU.mult))
            dve(eng.tensor_scalar(sp[:, 96:104], par_bx, 0.5, None, ALU.mult))
            eng.wait_ge(sp_exp, 1)
            eng.tensor_scalar(sp[:, 16:24], sp[:, 8:16], 1.0, None, ALU.add).then_inc(sp_one, 1)
            eng.wait_ge(sp_one, 1)
            dve(eng.tensor_scalar(sp[:, 40:48], sp[:, 16:24], 1.0, None, ALU.subtract))
            dve.wait(eng)
            dve(eng.tensor_scalar(sp[:, 48:56], sp[:, 40:48], 1e-30, None, ALU.max))
            dve(eng.tensor_scalar(sp[:, 56:64], sp[:, 40:48], 0.0, None, ALU.is_equal))
            dve.wait(eng)
            dve(eng.reciprocal(sp[:, 64:72], sp[:, 48:56]))
            dve(eng.tensor_tensor(sp[:, 56:64], sp[:, 56:64], sp[:, 8:16], ALU.mult))
            dve.wait(eng)
            dve(eng.tensor_tensor(sp[:, 64:72], sp[:, 64:72], sp[:, 8:16], ALU.mult))
            dve(eng.tensor_tensor(sp[:, 32:40], sp[:, 32:40], sp[:, 56:64], ALU.add))
            dve.wait(eng)
            eng.wait_ge(sp_ln, 1)
            dve(eng.tensor_tensor(sp[:, 64:72], sp[:, 64:72], sp[:, 24:32], ALU.mult))
            dve.wait(eng)
            dve(eng.tensor_tensor(sp[:, 72:80], sp[:, 64:72], sp[:, 32:40], ALU.add))
            dve.wait(eng)
            dve(eng.tensor_scalar(sp[:, 80:88], sp[:, 72:80], 2.0, None, ALU.mult))
            turned_lo_copy(6, hT)
            lo2(1, 0); take1(0, z[:, 1, KC2:KC2 + COLS]); lo2(1, 1)
            for r in range(RT):
                eng.wait_ge(free[r], 1)
            twice(scr, KC2, 1)
            twice(probs, VC2, 2)
            lo2(2, 0); take1(1, z[:, 1, Q2:Q2 + COLS], HD ** -0.5); lo2(2, 1)
            blocks(0, F_CK)
            lo2(3, 0)
            blocks(1, F_CV)
            dve.wait(eng)
            eng.wait_ge(read67[0], 2)
            eng.wait_ge(read67[1], 2)
            eng.sem_inc(flat_done, 1)
            take1(2, z[:, 1, Q2 + COLS:Q2 + D], HD ** -0.5); lo2(3, 1)
            lo2(4, 0); take1(3, z[:, 1, KS2:KS2 + COLS]); lo2(4, 1)
            for r in range(RT):
                eng.wait_ge(free[r], 4)
            twice(scr, KS2, 3)
            fill_copy(F_Q + 1, 2)
            fill_copy(F_Q + 3, 6)
            lo2(5, 0)
            eng.wait_ge(flat_hi, 1)
            eng.tensor_tensor(flat[1].rearrange("p j m -> p (j m)"), flat_f,
                              flat[0].rearrange("p j m -> p (j m)").bitcast(F32), ALU.subtract).then_inc(flat_lo, 1)
            lo2(5, 1)
            for r in range(RT):
                eng.wait_ge(free[r], 5)
                dve(eng.tensor_scalar(z[:, r, G2:G2 + GATES], z[:, r, G2:G2 + GATES], 0.5, 0.5, ALU.mult, ALU.add))
            lo2(6, 0); fill_copy(F_SK + 1, T2_KS + 2); take1(5, z[:, 1, KW2:KW2 + COLS])
            for r in range(RT):
                eng.wait_ge(free[r], 6)
            eng.wait_ge(filled, F_CV + 1)
            twice(probs, KW2, 4)
            lo2(6, 1)
            lo2(7, 0); fill_copy(F_WK + 1, T2_KW + 2); lo2(7, 1)
            eng.wait_ge(par_loaded, 64 * (LAYERS + 1))
            dve(eng.memset(scr[:, :, :], 0.0))
            dve(eng.memset(headsT[:, T2_V:T2_V + 4, :], 0.0))
            dve(eng.memset(probs[:, 0:2, :], 0.0))
            dve.wait(eng)
            lo2(8, 0); lo2(8, 1)
            lo2(9, 0)
            eng.wait_ge(read67[1], 7)
            for k in range(2):
                ins = eng.tensor_copy(scr[:, k, :].rearrange("p (g h n) -> p g h n", g=4, h=4)[:, :, :, 0:CMP],
                                      hidT[:, (2 + k) * COMP + COMP // 2:(3 + k) * COMP]
                                      .rearrange("p (g n) -> p g n", n=CMP).unsqueeze(2).to_broadcast([P, 4, 4, CMP]))
                if k:
                    ins.then_inc(pad_ready, 1)
                else:
                    dve(ins)
            lo2(9, 1)
            eng.wait_ge(filled, F_VC)
            for h in range(4):
                part = slice(32 * h, 32 * h + 32)
                ins = eng.tensor_copy(headsT[part, T2_V:T2_V + 4, h * HD:(h + 1) * HD],
                                      bank[7][part, 0:4 * HD].rearrange("p (g d) -> p g d", d=HD))
                if h == 3:
                    ins.then_inc(read67[1], 1)
                else:
                    dve(ins)
            wide = probs[:, 0:2, :].rearrange("p r (h n) -> p (r h) n", n=32)[:, :, 0:CMP]
            eng.wait_ge(cmask_ready, 1)
            for odd in range(2):
                eng.wait_ge(cs_ready, odd + 1)
                for r in range(RT):
                    dve(eng.tensor_tensor(probs[:, r, :].rearrange("p (h o n) -> p h o n", o=2, n=32)[:, :, odd, 0:CMP],
                                          bank[2 + odd][:, r * P:(r + 1) * P].rearrange("p (h n) -> p h n", n=16)[:, :, 0:CMP],
                                          cmask[:, r, :].unsqueeze(1).to_broadcast([P, 8, CMP]), ALU.add))
            dve.wait(eng)
            dve(eng.tensor_reduce(cstat, wide, AX.X, ALU.max))
            dve.wait(eng)
            eng.tensor_tensor(wide, wide, cstat.unsqueeze(2).to_broadcast([P, 32, CMP]), ALU.subtract)\
               .then_inc(cm_ready, 1)
            lo2(10, 0)
            eng.wait_ge(ce_ready, 1)
            dve(eng.tensor_reduce(cstat, wide, AX.X, ALU.add))
            dve.wait(eng)
            dve(eng.reciprocal(ccoef, cstat))
            dve.wait(eng)
            for r in range(RT):
                c = ccoef[:, 16 * r:16 * r + 16]
                dve(eng.tensor_tensor(c, c, z[:, r, G2:G2 + GATES].rearrange("p (h b) -> p h b", b=3)[:, :, 0], ALU.mult))
            dve.wait(eng)
            dve(eng.tensor_scalar(ccoef[:, 0:16], ccoef[:, 0:16], any_ok, None, ALU.mult))
            dve.wait(eng)
            eng.tensor_tensor(wide, wide, ccoef.unsqueeze(2).to_broadcast([P, 32, CMP]), ALU.mult)\
               .then_inc(cn_ready, 1)
            for r in range(RT):
                eng.wait_ge(free[r], 9)
            lo2(10, 1)
            eng.wait_ge(ct_ready, 2)
            eng.tensor_copy(probsT[:, 1, :], bank[3][:, :]).then_inc(cT_dve, 1)
            for r in range(RT):
                for n in range(2):
                    dve(eng.bn_stats(bn[:, 12 * r + 6 * n:12 * r + 6 * n + 6], z[:, r, n * COLS:(n + 1) * COLS]))
            dve.wait(eng)
            for r in range(RT):
                ins = eng.bn_aggr(bn[:, 24 + 2 * r:26 + 2 * r], bn[:, 12 * r:12 * r + 12])
                if r:
                    ins.then_inc(var_ready, 1)
                else:
                    dve(ins)
            lo2(11, 0)
            for r in range(RT):
                eng.wait_ge(cv_ready, r + 1)
                dve(eng.tensor_copy(mix[:, r, 0:COLS], bank[4][:, :]))
                eng.tensor_copy(mix[:, r, COLS:D], bank[5][:, :]).then_inc(cv_done, 1)
            dve.wait(eng)
            eng.wait_ge(vrs_ready, 1)
            eng.wait_ge(gain_loaded, 96)
            for r in range(RT):
                v = z[:, r, 0:D]
                dve(eng.tensor_scalar(v, v, bn[:, 24 + 2 * r:25 + 2 * r], bn[:, 28 + r:29 + r], ALU.subtract, ALU.mult))
            lo2(11, 1)
            attend_mask(A, causal)
            dve.wait(eng)
            for r in range(RT):
                dve(eng.tensor_tensor(z[:, r, 0:D], z[:, r, 0:D], gain[:, :], ALU.mult))
            dve.wait(eng)
            eng.sem_inc(gain_free, 1)
            lo2(12, 0)
            attend_copy(A)
            lo2(12, 1)
            eng.wait_ge(gain_loaded, 112)
            for r in range(RT):
                eng.tensor_tensor(z[:, r, 0:D], z[:, r, 0:D], gain[:, :], ALU.add).then_inc(vn_ready, 1)
            eng.wait_ge(vn_ready, 2)
            eng.sem_inc(gain_free, 1)
            group_out(0)
            attend_mask(A + 1, causal)
            eng.wait_ge(free[0], product(12))
            eng.wait_ge(free[1], product(12))
            for r in range(RT):
                for g in range(4):
                    if g % 2 == 0:
                        eng.wait_ge(filled, F_MIX + 2 * r + g // 2)
                    u = z[:, r, U2 + g * SEQ:U2 + (g + 1) * SEQ]
                    ins = eng.scalar_tensor_tensor(out=u, in0=bank[6 + g // 2][:, (g % 2) * SEQ:(g % 2 + 1) * SEQ],
                                                   scalar=par_bs[:, g:g + 1], in1=u, op0=ALU.add, op1=ALU.mult)
                    if g % 2:
                        ins.then_inc(read67[g // 2], 1)
                    else:
                        dve(ins)
            dve.wait(eng)
            eng.wait_ge(read67[0], 9)
            eng.wait_ge(read67[1], 10)
            eng.sem_inc(rows_ready, 4)
            for b in range(12, 19):
                i = b - 11
                if b > 12:
                    group_out(i - 1)
                    attend_mask(A + i, causal)
                lo2(b + 1, 0)
                attend_copy(A + i)
                if b in (13, 15):
                    merge(b)
                if b in (16, 17):
                    convolve(b)
                lo2(b + 1, 1)
                if b == 12:
                    turned_lo_copy(7, mixT)
            group_out(7)
            eng.sem_inc(rows_ready, 4)
            lo2(20, 0); lo2(20, 1)
            lo2(21, 0)
            for c in range(4):
                gated_input(c)
            lo2(21, 1)
            for c in range(4, 8):
                gated_input(c)
            turned_lo_copy(8, mixT)
            roots = headsT[:, 0:8, :].rearrange("p (a b) c -> p a (b c)", a=2)
            gx = z[:, :, 0:D]
            lo2(22, 0)
            merge(21)
            eng.tensor_scalar(mix[:, :, :], roots, 1.0, None, ALU.add).then_inc(u_read, 1)
            lo2(22, 1)
            eng.wait_ge(u_read, 1)
            dve(eng.reciprocal(mix[:, :, :], mix[:, :, :]))
            dve.wait(eng)
            lo2(23, 0)
            eng.wait_ge(gx_done, 8)
            dve(eng.tensor_tensor(gx, gx, mix[:, :, :], ALU.mult))
            dve.wait(eng)
            lo2(23, 1)
            eng.wait_ge(root_ready, 1)
            dve(eng.tensor_tensor(gx, gx, roots, ALU.mult))
            dve(eng.tensor_scalar(mix[:, :, :], mix[:, :, :], 2.0, 1.0, ALU.mult, ALU.subtract))
            dve.wait(eng)
            lo2(24, 0)
            merge(23)
            lo2(24, 1)
            for c in range(8):
                dve(eng.tensor_tensor_scan(headsT[:, c, :], mix[:, c // 4, (c % 4) * SEQ:(c % 4 + 1) * SEQ],
                                           channels(c), 0.0, ALU.mult, ALU.add))
            dve.wait(eng)
            lo2(25, 0)
            eng.tensor_tensor(headsT[:, 0:8, :], headsT[:, 0:8, :], headsT[:, 8:16, :], ALU.mult).then_inc(yc_ready, 1)
            lo2(25, 1)
            eng.wait_ge(yc_hi, 1)
            eng.tensor_tensor(mixT[1][:, :, :], headsT[:, 0:8, :], mixT[0][:, :, :].bitcast(F32), ALU.subtract)\
               .then_inc(yc_lo, 1)
            lo2(26, 0); merge(25); lo2(26, 1)
            lo2(27, 0); lo2(27, 1)
            lo2(28, 0); merge(27); lo2(28, 1)
            eng.wait_ge(merged_done, 12)
            eng.sem_inc(rows_ready, 4)
            turned_lo_copy(9, mixT, 0.5)
            lo2(29, 0); take1(28, mix[:, 1, 0:COLS]); lo2(29, 1)
            lo2(30, 0); take1(29, mix[:, 1, COLS:D]); lo2(30, 1)
            post_add(5, 7, RT)
            eng.wait_ge(ffn_gain_loaded, 16)
            for h in range(2):
                for r in range(RT):
                    gain_rows(r, h, ffn_gain)
            turned_lo_copy(10, hT)
            ffn(B2 + PAIRS2, LAYERS, 6, None)
            post_add(7, 8, 2 * RT)


def rope_tables():
    inv = 1.0 / (np.float32(10000.0) ** (np.arange(0, HD, 2, dtype=np.float32) / HD))
    ang = (np.arange(SEQ, dtype=np.float32)[:, None] * inv[None, :]).astype(np.float32)
    c, s = np.cos(ang).astype(np.float32), np.sin(ang).astype(np.float32)
    by_row = lambda a: np.ascontiguousarray(a.reshape(RT, P, HD).transpose(1, 0, 2))
    return by_row(np.concatenate([c, c], 1)), by_row(np.concatenate([-s, s], 1))


def halves(w):
    n = w.shape[1] // COLS
    return w.reshape(2, KT // 2, P, n, COLS).transpose(3, 0, 2, 1, 4).reshape(n, 2, P, KT // 2 * COLS)


def ffn_layout(gate, up, down):
    k = lambda w: w.reshape(KT, P, FF_STEPS, FF_STEP)
    gu = np.stack([k(gate), k(up)], 3).transpose(2, 1, 0, 3, 4)
    gu = gu.reshape(FF_STEPS, P, KT * COLS)
    dn = down.reshape(FF_STEPS, 2, P, D).transpose(0, 2, 1, 3).reshape(FF_STEPS, P, 4 * UNIT)
    first = gu[0]
    second = np.concatenate([gu[1:, :, 6 * UNIT:], dn[:-1]], 2)
    loop = np.stack([gu[1:, :, :6 * UNIT], second], 1)
    last = dn[-1].reshape(P, 2, 2 * UNIT).transpose(1, 0, 2)
    return first, loop, last


def layout(i):
    t = {}
    t["x"] = i["x"].reshape(SEQ, D)
    w = i["w_in"]
    sizes = [256, 256, 256, 512, 512, 512, 256, 256, 256, 512, 64, 8]
    mq, mk, mv, dq, dk, dv, sq, sk, sv, iq, ik, iw = np.split(w, np.cumsum(sizes)[:-1], axis=2)
    groups = np.concatenate([iq, dq, dk, dv, mq, mk, sq, sk, mv, sv], 2)
    t["w1_groups"] = np.stack([halves(g) for g in groups])
    kv = np.concatenate([i["w_in_2"][0][:, 3072:3584]], 1)
    t["next_first"] = np.stack([t["w1_groups"][1, 0], halves(kv)[0]])
    narrow = np.concatenate([ik, iw], 2)
    t["w1_narrow"] = narrow.reshape(LAYERS, 2, KT // 2, P, NARROW).transpose(0, 1, 3, 2, 4)\
        .reshape(LAYERS, 2, P, KT // 2 * NARROW)
    t["w1_out"] = np.stack([halves(g) for g in i["w_out"]])
    ff = [ffn_layout(i["w_gate"][l], i["w_up"][l], i["w_down"][l]) for l in range(LAYERS)]
    ff.append(ffn_layout(i["w_ffn_in_2"][0][:, :DFF], i["w_ffn_in_2"][0][:, DFF:], i["w_ffn_out_2"][0]))
    for n, name in enumerate(("ff_first", "ff_loop", "ff_last")):
        t[name] = np.stack([f[n] for f in ff])
    again = lambda a: np.concatenate([a, a[-1:]])
    t["attn_norm_g"] = i["attn_norm_g"]
    t["ffn_norm_g"] = i["ffn_norm_g"]
    t["next_norm_g"] = np.concatenate([i["attn_norm_g"][1:], i["g_pre_mix_2"]])
    t["head_gains"] = again(np.concatenate([i["q_norm_g"], i["k_norm_g"]], 1))
    t["diff_lambda"] = again(i["diff_lambda"])
    t["diff_subln_g"] = again(i["diff_subln_g"])
    first = [0.8 - 0.6 * np.exp(-0.3 * l) for l in range(LAYERS + 1)]
    t["lam_init"] = np.array([[v, 1.0 - v] for v in first], np.float32)
    t["rope_c"], t["rope_s"] = rope_tables()
    w2 = i["w_in_2"][0]
    widths = [1024, 1024, 1024, 256, 256, 256, 256, 256, 256, GATES, 1024, 1024, 1024, 1024, 1024]
    u, v, q, kc, vc, ks, vs, kw, vw, ng, xr, rg, ma, mb, mc = np.split(w2, np.cumsum(widths)[:-1], axis=1)
    half = lambda a, n: a[:, n * COLS:(n + 1) * COLS]
    cols = [kc, vc, q, ks, vs, kw, vw, v, u]

    def branch(gate, w):
        return [half(gate, 0), half(w, 0), half(gate, 1), half(w, 1)]

    a, b, c = i["w_br_a_2"][0], i["w_br_b_2"][0], i["w_br_c_2"][0]
    cols += branch(ma, a) + [xr, rg] + branch(mb, b) + branch(mc, c) + [i["w_o_2"][0]]
    t["w2_groups"] = halves(np.concatenate(cols, 1))
    t["w2_narrow"] = ng.reshape(2, KT // 2, P, GATES).transpose(0, 2, 1, 3).reshape(2, P, KT // 2 * GATES)
    comp = np.stack([i["nsa_wk1_2"][0].reshape(COMP_K, P, SEQ), i["nsa_wv1_2"][0].reshape(COMP_K, P, SEQ)], 2)
    t["w2_comp"] = comp.reshape(2, 2, 4, P, COLS).transpose(0, 1, 3, 2, 4).reshape(2, 2, P, 4 * COLS)
    wk2 = i["nsa_wk2_2"][0].reshape(2, P, HD).transpose(1, 0, 2)
    wk2 = np.concatenate([wk2, wk2], 2).reshape(P, 256)
    wv2 = i["nsa_wv2_2"][0].reshape(2, P, HD).transpose(1, 0, 2).reshape(P, 128)
    pos = lambda e: e.reshape(COMP_K, P).T
    t["small2"] = np.concatenate([wk2, wv2, pos(i["nsa_pe_k_2"][0]), pos(i["nsa_pe_v_2"][0])], 1)
    ch = lambda e: e[0].reshape(KT, P).T
    cw = i["rnn_conv_w_2"][0].reshape(4, KT, P).transpose(2, 1, 0).reshape(P, 4 * KT)
    t["channel2"] = np.concatenate([i["gmlp_bs_2"][0].T, cw, ch(i["rnn_conv_b_2"]), ch(i["rnn_ba_2"]),
                                    ch(i["rnn_bx_2"]), ch(i["rnn_lam_2"])], 1)
    t["w_s"] = i["gmlp_ws_2"][0].transpose(2, 0, 1)
    g = lambda w: w[0].reshape(KT, P, HD).transpose(1, 0, 2).reshape(P, KT * HD)
    t["w_gates"] = np.stack([g(i["rnn_wa_2"]), g(i["rnn_wx_2"])])
    t["rows2"] = np.concatenate([i["gmlp_ln_g_2"], i["gmlp_ln_b_2"], i["g_post_mix_2"], i["g_pre_ffn_2"],
                                 i["g_post_ffn_2"]])
    return {k: np.ascontiguousarray(v) for k, v in t.items()}


def kernel(**inputs):
    import concourse.bacc as bacc
    from concourse.bass_utils import run_bass_kernel_spmd

    nc = bacc.Bacc("TRN2", target_bir_lowering=False, num_devices=1)
    arrays = layout({k: np.asarray(v) for k, v in inputs.items()})
    t = {k: nc.dram_tensor(f"in_{k}", v.shape, mybir.dt.from_np(v.dtype), kind="ExternalInput").ap()
         for k, v in arrays.items()}
    t["out"] = nc.dram_tensor("out_x", (SEQ, D), F32, kind="ExternalOutput").ap()
    block_one_and_two(nc, t)
    r = run_bass_kernel_spmd(nc, [{f"in_{k}": v for k, v in arrays.items()}], core_ids=[0])
    return r.results[0]["out_x"].reshape(1, SEQ, D)
```

```python
from contextlib import ExitStack

import numpy as np

import concourse.bass as bass
from concourse import mybir

F32 = mybir.dt.float32
F32R = mybir.dt.float32r
ALU = mybir.AluOpType
ACT = mybir.ActivationFunctionType
AX = mybir.AxisListType

P = 128
SEQ = 256
RT = SEQ // P
D = 1024
KT = D // P
LAYERS = 2
HD = 64
EPS = 1e-6
NEG = -1e30
TAKEN = -3e38
DFF = 2816
COLS = 512
UNIT = COLS
SLOT = 6 * UNIT
TOPK = 64
IDX_HEADS = 8
FF_STEP = 256
FF_STEPS = DFF // FF_STEP

IQ, IK, IW, DQ, DK, DV, MQ, MK, SQ, SK, MV, SV = (
    0, 512, 576, 584, 1096, 1608, 2120, 2376, 2632, 2888, 3144, 3400)
HEAD_SETS = (DQ, DK, MQ, SQ)
Z_COLS = 3656
LN_EXP = "natural_log_exp_and_others"
EXP_TANH = "exp_and_others"
NARROW = 72
T_IQ, T_SQ, T_SK, T_DQ, T_DK, T_MQ, T_MK, T_IK = 0, 4, 6, 8, 12, 16, 18, 20
PAIRS1 = 22
HALVES = 10
Q2, KC2, VC2, KS2, VS2, KW2, VW2, G2, U2 = 0, 1024, 1280, 1536, 1792, 2048, 2304, 2560, 2608
GATES = 48
CMP = 15
KV_GROUPS = 4
COMP = 2 * KV_GROUPS * CMP
COMP_K = 16
B2 = 2 * PAIRS1
PAIRS2 = 30
T2_KS, T2_KW, T2_KC, T2_V = 8, 12, 16, 17
F_CK, F_CV, F_Q, F_SK, F_WK, F_HT, F_KC, F_VC, F_MIX, F_GATE = 1, 3, 5, 9, 11, 13, 14, 15, 16, 20
NGRP = 4


class Progress:

    def __init__(self, sem):
        self.sem, self.n = sem, 0

    def __call__(self, instruction):
        instruction.then_inc(self.sem, 1)
        self.n += 1

    def wait(self, eng):
        eng.wait_ge(self.sem, self.n)

    def restart(self, eng):
        if self.n:
            eng.wait_ge(self.sem, self.n)
            eng.sem_clear(self.sem)
            self.n = 0


def AP_of(base, offset, pattern):
    return bass.AP(base.tensor, base.offset + offset, [list(base.ap[0])] + pattern)


def block_one_and_two(nc, t):
    ctx = ExitStack()
    with ctx:
        def sb(name, shape, dt=F32):
            return ctx.enter_context(nc.sbuf_tensor(name, shape, dt))

        def sem(name):
            return ctx.enter_context(nc.semaphore(name))

        raw = [sb(f"raw{j}", [P, SLOT]) for j in range(2)]
        whi = [sb(f"whi{j}", [P, SLOT], F32R) for j in range(2)]
        wlo = [sb(f"wlo{j}", [P, SLOT], F32R) for j in range(2)]
        x = sb("x", [P, RT, D])
        hT = [sb(f"hT_{s}", [P, KT, SEQ], F32R) for s in ("hi", "lo")]
        mixT = [sb(f"mixT_{s}", [P, KT, SEQ], F32R) for s in ("hi", "lo")]
        ffT = [sb(f"ffT_{s}", [P, 2, SEQ], F32R) for s in ("hi", "lo")]
        mix = sb("mix", [P, RT, D])
        z = sb("z", [P, RT, Z_COLS])
        headsT = sb("headsT", [P, 21, SEQ])
        probs = sb("probs", [P, 3, COLS])
        probsT = sb("probsT", [P, 3, COLS])
        scr = sb("scr", [P, 2, COLS])
        sqr = sb("sqr", [P, COLS])
        gain = sb("gain", [P, D])
        ident = sb("ident", [P, P])
        causal = sb("causal", [P, 3 * P])
        index = sb("index", [P, 3 * P])
        chosen = index
        rope_c = sb("rope_c", [P, RT, HD])
        rope_s = sb("rope_s", [P, RT, HD])
        gain_c = sb("gain_c", [P, RT, 6, HD])
        gain_s = sb("gain_s", [P, RT, 6, HD])
        hgain = headsT[:, T_MK:T_IK, :].rearrange("p a b -> p (a b)")[:, 0:6 * HD].rearrange("p (n d) -> p n d", d=HD)
        lamp = headsT[:, T_IK, :].rearrange("p (n d) -> p n d", d=HD)
        sub_g = sb("sub_g", [P, 2 * HD])
        flat = [m[:, :, :].rearrange("p k c -> p (k c)")[:, 0:COMP_K * COMP]
                .rearrange("p (j m) -> p j m", m=COMP) for m in mixT]
        flat_f = mix[:, :, :].rearrange("p r c -> p (r c)")[:, 0:COMP_K * COMP]
        small = gain_s[:, :, :, :].rearrange("p a b c -> p (a b c)")
        wk2 = small[:, 0:256].rearrange("p (k c) -> p k c", k=2)
        wv2 = small[:, 256:384].rearrange("p (k c) -> p k c", k=2)
        pe_kv = small[:, 384:416].rearrange("p (v j) -> p v j", v=2)
        par = small[:, 416:416 + 68]
        par_bs, par_cw, par_cb, par_ba, par_bx, par_lam = (
            par[:, a:b] for a, b in ((0, 4), (4, 36), (36, 44), (44, 52), (52, 60), (60, 68)))
        cmask = index[:, 0:2 * CMP].rearrange("p (r n) -> p r n", r=2)
        any_ok = index[:, 32:33]
        cstat = index[:, 64:96]
        ccoef = index[:, 96:128]
        w_s = gain_c[:, :, :, :].rearrange("p a b c -> p (a b c)")[:, 0:4 * P].rearrange("p (g t) -> p g t", g=4)
        hidT = probsT[:, 2, 0:4 * COMP]
        ffn_gain = headsT[:, 16:20, :].rearrange("p a b -> p (a b)")
        bn = rope_c[:, :, :].rearrange("p r d -> p (r d)")
        sp = rope_s[:, :, :].rearrange("p r d -> p (r d)")
        lam_c = sb("lam_c", [P, 2])
        lam = sb("lam", [P, 4])
        eps = sb("eps", [P, 1])
        ssq = sb("ssq", [P, 16])
        nmax = sb("nmax", [P, 8])
        sums = sb("sums", [P, 2, 8])
        inv = sb("inv", [P, 8])
        hss = sb("hss", [P, RT, 8])
        hrs = sb("hrs", [P, RT, 8])
        top8 = sb("top8", [P, 2, 8])
        dstat = sb("dstat", [P, 8])
        bank = [ctx.enter_context(nc.psum_tensor(f"bank{i}", [P, COLS], F32)) for i in range(8)]

        raw_loaded = [sem(f"raw_loaded{j}") for j in range(2)]
        hi_ready = [sem(f"hi_ready{j}") for j in range(2)]
        lo_ready = [sem(f"lo_ready{j}") for j in range(2)]
        used = [sem(f"used{j}") for j in range(2)]
        half_ready = sem("half_ready")
        z_act = sem("z_act")
        z_dve = sem("z_dve")
        out_added = sem("out_added")
        const_ready = sem("const_ready")
        x_loaded = sem("x_loaded")
        gain_loaded = sem("gain_loaded")
        gain_free = sem("gain_free")
        rope_loaded = sem("rope_loaded")
        par_loaded = sem("par_loaded")
        sq_ready = sem("sq_ready")
        rs_ready = sem("rs_ready")
        rows_ready = sem("rows_ready")
        turned = sem("turned")
        turned_hi = sem("turned_hi")
        turned_lo = sem("turned_lo")
        squares = sem("squares")
        ssq_ready = sem("ssq_ready")
        hrs_ready = sem("hrs_ready")
        prep = sem("prep")
        tables_ready = sem("tables_ready")
        heads_turned = sem("heads_turned")
        heads_act = sem("heads_act")
        heads_dve = sem("heads_dve")
        idx_ready = sem("idx_ready")
        idx_relu = sem("idx_relu")
        idx_acc = sem("idx_acc")
        scores = sem("scores")
        masked = sem("masked")
        exped = sem("exped")
        pT_ready = sem("pT_ready")
        pT_act = sem("pT_act")
        pT_dve = sem("pT_dve")
        pv_ready = sem("pv_ready")
        o_done = sem("o_done")
        lam_sum = sem("lam_sum")
        lam_exp = sem("lam_exp")
        dsq = sem("dsq")
        drs = sem("drs")
        gu_ready = sem("gu_ready")
        silu_ready = sem("silu_ready")
        gu_free = sem("gu_free")
        ff_turned = sem("ff_turned")
        ff_hi = sem("ff_hi")
        ff_lo = sem("ff_lo")
        down_ready = sem("down_ready")
        down_added = sem("down_added")
        out_sem = sem("out_sem")
        free = [sem(f"free{r}") for r in range(2)]
        filled = sem("filled")
        read67 = [sem(f"read{b}") for b in (6, 7)]
        small_loaded = sem("small_loaded")
        ws_loaded = sem("ws_loaded")
        ws_ready = sem("ws_ready")
        rg_loaded = sem("rg_loaded")
        ffn_gain_loaded = sem("ffn_gain_loaded")
        cmask_ready = sem("cmask_ready")
        sp_abs = sem("sp_abs")
        sp_exp = sem("sp_exp")
        sp_one = sem("sp_one")
        sp_ln = sem("sp_ln")
        sp_ready = sem("sp_ready")
        dup_ready = sem("dup_ready")
        flat_done = sem("flat_done")
        flat_hi = sem("flat_hi")
        flat_lo = sem("flat_lo")
        pad_ready = sem("pad_ready")
        cs_ready = sem("cs_ready")
        cm_ready = sem("cm_ready")
        ce_ready = sem("ce_ready")
        cn_ready = sem("cn_ready")
        ct_ready = sem("ct_ready")
        cT_act = sem("cT_act")
        cT_dve = sem("cT_dve")
        cv_ready = sem("cv_ready")
        cv_done = sem("cv_done")
        var_ready = sem("var_ready")
        vrs_ready = sem("vrs_ready")
        vn_ready = sem("vn_ready")
        merged_done = sem("merged_done")
        xc_ready = sem("xc_ready")
        rg_ready = sem("rg_ready")
        u_ready = sem("u_ready")
        gx_done = sem("gx_done")
        root_ready = sem("root_ready")
        yc_ready = sem("yc_ready")
        yc_hi = sem("yc_hi")
        yc_lo = sem("yc_lo")
        x_added = sem("x_added")
        squared = sem("squared")
        dve = Progress(sem("dve_own"))
        act = Progress(sem("act_own"))
        pool = Progress(sem("pool_own"))
        pe = Progress(sem("pe_own"))

        block = ctx.enter_context(nc.Block())

        def index_heads(u):
            return [2 * i + u for i in range(4)] if u < 2 else [4 * ((u - 2) // 2) + u % 2 + 2 * i for i in range(2)]

        def product(b):
            return b - (b > 6)

        def half_of(b):
            return LAYERS * HALVES + product(b) + 1

        def channels(c):
            return z[:, c // 4, (c % 4) * SEQ:(c % 4 + 1) * SEQ]

        def stage(r):
            return headsT[:, 16 + 2 * r:18 + 2 * r, :].rearrange("p a c -> p (a c)")

        def gate_buffer(b):
            return probs if b == 25 else scr

        def merged(r, n):
            return z[:, r, U2 + n * COLS:U2 + (n + 1) * COLS]

        def scr_ik(r):
            return scr[:, r, 0:P]

        def ffn_elements(c, j):
            if c == 0:
                return 4 * UNIT
            if c == FF_STEPS:
                return 2 * UNIT
            return 6 * UNIT

        @block.sync
        def _(eng):
            def load(p, j, src):
                n = src.shape[1]
                eng.wait_ge(lo_ready[j], p + 1)
                eng.dma_start(raw[j][:, 0:n], src).then_inc(raw_loaded[j], 16)

            eng.dma_start(gain[:, :], t["attn_norm_g"][0, :].partition_broadcast(P)).then_inc(gain_loaded, 16)
            for r in range(RT):
                eng.dma_start(x[:, r, :], t["x"][r * P:(r + 1) * P, :]).then_inc(x_loaded, 16)

            def ffn_loads(p0, l, between):
                for j in range(2):
                    n = 4 * UNIT
                    load(p0, j, t["ff_first"][l, :, j * n:(j + 1) * n])
                with eng.Fori(1, FF_STEPS) as c:
                    for j in range(2):
                        load(p0 + c, j, t["ff_loop"][l, c - 1, j])
                between()
                for j in range(2):
                    load(p0 + FF_STEPS, j, t["ff_last"][l, j])

            def next_gain(i, src):
                eng.wait_ge(gain_free, i)
                eng.dma_start(gain[:, :], src.partition_broadcast(P)).then_inc(gain_loaded, 16)

            def layer_parameters(l):
                for dst, name in ((hgain, "head_gains"), (lamp, "diff_lambda"), (sub_g[:, :], "diff_subln_g"),
                                  (lam_c[:, :], "lam_init")):
                    eng.dma_start(dst, t[name][l].partition_broadcast(P)).then_inc(par_loaded, 16)

            for j in range(2):
                load(0, j, t["w1_groups"][0, 0, j])
            layer_parameters(0)
            with eng.Fori(0, LAYERS) as l:
                for g in range(1, 8):
                    for j in range(2):
                        if g == 1:
                            load(l * PAIRS1 + g, j, t["w1_narrow"][l, j])
                        else:
                            load(l * PAIRS1 + g, j, t["w1_groups"][l, g - (g > 1), j])
                for g in range(2):
                    for j in range(2):
                        load(l * PAIRS1 + 8 + g, j, t["w1_out"][l, g, j])
                    if g == 0:
                        eng.wait_ge(prep, l * 6 + 6)
                        next_gain(2 * l + 1, t["ffn_norm_g"][l, :])

                def next_parameters():
                    next_gain(2 * l + 2, t["next_norm_g"][l, :])
                    layer_parameters(l + 1)
                ffn_loads(l * PAIRS1 + 10, l, next_parameters)
                for j in range(2):
                    load((l + 1) * PAIRS1, j, t["next_first"][l, j])
            for dst, name in ((small[:, 0:416], "small2"), (par, "channel2")):
                eng.dma_start(dst, t[name]).then_inc(small_loaded, 16)
            eng.dma_start(w_s, t["w_s"]).then_inc(ws_loaded, 16)
            with eng.Fori(1, 4) as g:
                for j in range(2):
                    load(B2 + g, j, t["w2_groups"][g, j])
            for j in range(2):
                load(B2 + 4, j, t["w2_narrow"][j])
            for j in range(2):
                load(B2 + 5, j, t["w2_groups"][4, j])
            next_gain(5, t["rows2"][0, :])
            with eng.Fori(0, 2) as g:
                for j in range(2):
                    load(B2 + 6 + g, j, t["w2_comp"][g, j])
            eng.wait_ge(filled, F_CV + 1)
            eng.dma_start(z[:, 0, KC2:KC2 + 512], t["w_gates"][0]).then_inc(rg_loaded, 16)
            eng.dma_start(z[:, 1, KC2:KC2 + 512], t["w_gates"][1]).then_inc(rg_loaded, 16)
            with eng.Fori(0, 4) as g:
                for j in range(2):
                    load(B2 + 8 + g, j, t["w2_groups"][5 + g, j])
            for j in range(2):
                load(B2 + 12, j, t["w2_groups"][9, j])
            next_gain(6, t["rows2"][1, :])
            with eng.Fori(1, 4) as g:
                for j in range(2):
                    load(B2 + 12 + g, j, t["w2_groups"][9 + g, j])
            next_gain(7, t["rows2"][2, :])
            with eng.Fori(4, 18) as g:
                for j in range(2):
                    load(B2 + 12 + g, j, t["w2_groups"][9 + g, j])
            eng.wait_ge(xc_ready, 8)
            eng.dma_start(ffn_gain, t["rows2"][3, :].partition_broadcast(P)).then_inc(ffn_gain_loaded, 16)
            ffn_loads(B2 + PAIRS2, LAYERS, lambda: next_gain(8, t["rows2"][4, :]))
            for r in range(RT):
                eng.wait_ge(x_added, 4 + 2 * (r + 1))
                eng.dma_start(t["out"][r * P:(r + 1) * P, :], x[:, r, :]).then_inc(out_sem, 16)
            eng.wait_ge(out_sem, 16 * RT)

        @block.gpsimd
        def _(eng):
            eng.memset(eps[:, :], EPS).then_inc(const_ready, 1)
            pool(eng.memset(ident[:, :], 0.0))
            pool(eng.memset(causal[:, :], 0.0))
            pool.wait(eng)
            eng.affine_select(out=ident[:, :], in_=ident[:, :], compare_op=ALU.not_equal, fill=1.0,
                              base=0, pattern=[[-1, P]], channel_multiplier=1).then_inc(const_ready, 1)
            for c in (0, 2):
                part = causal[:, c * P:(c + 1) * P]
                eng.affine_select(out=part, in_=part, compare_op=ALU.is_ge, fill=NEG,
                                  base=0, pattern=[[-1, P]], channel_multiplier=1).then_inc(const_ready, 1)
            eng.dma_start(rope_c[:, :, :], t["rope_c"]).then_inc(rope_loaded, 16)
            eng.dma_start(rope_s[:, :, :], t["rope_s"]).then_inc(rope_loaded, 16)
            eng.wait_ge(rope_loaded, 32)
            pool.restart(eng)
            with eng.Fori(0, LAYERS) as l:
                def projected(i):
                    eng.wait_ge(z_act, l * 8 + i + 1)
                    eng.wait_ge(z_dve, l * 8 + i + 1)

                def rotate(src, ct, st, n, scale=None, last=False):
                    h, m = HD // 2, len(ct)
                    w = n // m
                    a, b = (gain[:, c:c + n * HD].rearrange("p (n d) -> p n d", d=HD) for c in (0, COLS))
                    for i in range(m):
                        hs = slice(i * w, (i + 1) * w)
                        pool(eng.tensor_tensor(a[:, hs, :], src[:, hs, :],
                                               ct[i].unsqueeze(1).to_broadcast([P, w, HD]), ALU.mult))
                        for u, v in ((0, h), (h, 0)):
                            pool(eng.tensor_tensor(b[:, hs, u:u + h], src[:, hs, v:v + h],
                                                   st[i][:, u:u + h].unsqueeze(1).to_broadcast([P, w, h]), ALU.mult))
                    pool.wait(eng)
                    if scale is None:
                        ins = eng.tensor_tensor(src, a, b, ALU.add)
                    else:
                        pool(eng.tensor_tensor(a, a, b, ALU.add))
                        pool.wait(eng)
                        eng.wait_ge(hrs_ready, scale[0])
                        ins = eng.tensor_tensor(src, a, scale[1], ALU.mult)
                    if last:
                        ins.then_inc(prep, 1)
                    else:
                        pool(ins)
                        pool.wait(eng)

                eng.wait_ge(gain_free, 2 * l + 1)
                projected(0)
                for r in range(RT):
                    src = z[:, r, IQ:IQ + COLS].rearrange("p (n d) -> p n d", d=HD)
                    rotate(src, [rope_c[:, r, :]], [rope_s[:, r, :]], 8, last=(r == 1))
                projected(1)
                eng.wait_ge(prep, l * 6 + 1)
                eng.wait_ge(lam_sum, l + 1)
                for r in range(RT):
                    src = z[:, r, IK:IK + HD].rearrange("p (n d) -> p n d", d=HD)
                    rotate(src, [rope_c[:, r, :]], [rope_s[:, r, :]], 1)
                    pool(eng.tensor_scalar(z[:, r, IW:IW + IDX_HEADS], z[:, r, IW:IW + IDX_HEADS],
                                           IDX_HEADS ** -0.5, None, ALU.mult))
                pool.wait(eng)
                for r in range(RT):
                    ins = eng.tensor_copy(scr_ik(r).rearrange("p (a d) -> p a d", a=2),
                                          z[:, r, IK:IK + HD].unsqueeze(1).to_broadcast([P, 2, HD]))
                    if r:
                        ins.then_inc(prep, 1)
                    else:
                        pool(ins)
                eng.wait_ge(tables_ready, l + 1)
                for s, (c0, i, gains) in enumerate(zip(HEAD_SETS, (2, 3, 5, 6), ((1,), (4,), (0, 3), (2, 5)))):
                    projected(i)
                    for r in range(RT):
                        src = z[:, r, c0:c0 + COLS].rearrange("p (n d) -> p n d", d=HD)
                        rotate(src, [gain_c[:, r, g, :] for g in gains], [gain_s[:, r, g, :] for g in gains], 8,
                               scale=(l * 8 + 2 * s + r + 1, hrs[:, r, :].unsqueeze(2).to_broadcast([P, 8, HD])),
                               last=(r == 1))
                    if s < 3:
                        eng.wait_ge(prep, l * 6 + 3 + s)
                pool.restart(eng)

            eng.wait_ge(gain_free, 4)
            pool(eng.memset(index[:, 0:48], 0.0))
            pool.wait(eng)
            for r in range(RT):
                pool(eng.affine_select(out=cmask[:, r, :], in_=cmask[:, r, :], compare_op=ALU.is_ge, fill=NEG,
                                       base=r * P - 31, pattern=[[-16, CMP]], channel_multiplier=1))
            eng.affine_select(out=any_ok, in_=any_ok, compare_op=ALU.is_ge, fill=1.0, base=30,
                              pattern=[[0, 1]], channel_multiplier=-1).then_inc(cmask_ready, 1)
            pool.wait(eng)
            eng.wait_ge(ws_loaded, 16)
            eng.affine_select(out=w_s, in_=w_s, compare_op=ALU.is_ge, fill=0.0, base=0,
                              pattern=[[0, 4], [1, P]], channel_multiplier=-1).then_inc(ws_ready, 1)

        @block.tensor
        def _(eng):
            def three(out, a, a_cols, j, w, start, stop, first=True, n=COLS):
                wh, wl = whi[j][:, w:w + n], wlo[j][:, w:w + n]
                hi, lo = (s[:, a, a_cols] for s in three.act)
                eng.matmul(out, lhsT=hi, rhs=wh, start=start, stop=False)
                eng.matmul(out, lhsT=hi, rhs=wl, start=False, stop=False)
                return eng.matmul(out, lhsT=lo, rhs=wh, start=False, stop=stop)

            def chunk(p, j, n=COLS, bank_read=None, between=None):
                eng.wait_ge(lo_ready[j], p + 2)
                for r in range(RT):
                    if j == 0 and bank_read:
                        bank_read(r)
                    for k in range(4):
                        mm = three(bank[r][:, 0:n], 4 * j + k, slice(r * P, (r + 1) * P), j, k * n,
                                   start=(j == 0 and k == 0), stop=(j == 1 and k == 3), n=n)
                    if j == 1 and r == 0:
                        mm.then_inc(half_ready, 1)
                    if between and r == 0:
                        between()
                mm.then_inc(used[j], 1)

            rows_before = 0

            def turn_half(i, h, src=mix):
                for r in range(RT):
                    n = i * 4 + 2 * h + r
                    eng.wait_ge(rows_ready, n + 1 + rows_before)
                    if h:
                        eng.wait_ge(turned_lo, n - 1)
                    for k in range(4):
                        c = (4 * h + k) * P
                        mm = eng.transpose(bank[6 + r][:, k * P:(k + 1) * P], src[:, r, c:c + P], ident[:, :])
                    mm.then_inc(turned, 1)

            def turn_rows(i, src=mix):
                turn_half(i, 0, src)
                turn_half(i, 1, src)
                eng.wait_ge(turned_lo, i * 4 + 4)

            def turn_heads(l, s, src, pairs):
                eng.wait_ge(prep, l * 6 + s + 1)
                if s > 0:
                    eng.wait_ge(heads_act, l * 6 + s)
                    eng.wait_ge(heads_dve, l * 5 + (1 if s < 3 else s - 1))
                for i in range(0, pairs, 2):
                    for q in range(min(2, pairs - i)):
                        for r in range(RT):
                            mm = eng.transpose(bank[6 + i // 2][:, (q * RT + r) * P:(q * RT + r + 1) * P],
                                               src(i + q, r), ident[:, :])
                    mm.then_inc(heads_turned, 1)

            def index_scores(l, u):
                if u == 0:
                    eng.wait_ge(heads_act, l * 6 + 2)
                    eng.wait_ge(heads_dve, l * 5 + 1)
                if u >= 3:
                    eng.wait_ge(idx_relu, l * 6 + u - 2)
                b = bank[2 + u % 3]
                keys = P if u < 2 else SEQ
                for i, h in enumerate(index_heads(u)):
                    half = slice(HD * (h % 2), HD * (h % 2) + HD)
                    rows = slice(0, P) if u < 2 else slice(P, SEQ)
                    mm = eng.matmul(b[:, i * keys:(i + 1) * keys], lhsT=headsT[half, T_IQ + h // 2, rows],
                                    rhs=headsT[half, T_IK, 0:keys], start=True, stop=True)
                mm.then_inc(idx_ready, 1)

            def attend_scores(A, q, k):
                eng.wait_ge(pT_act, 2 * A + 2)
                eng.wait_ge(pT_dve, A + 1)
                for odd in range(2):
                    for u in (0, 1 + odd):
                        keys, rows = (P, slice(0, P)) if u == 0 else (SEQ, slice(P, SEQ))
                        if odd and u == 0:
                            pe.wait(eng)
                        for h in (odd, 2 + odd):
                            half = slice(HD * odd, HD * odd + HD)
                            c = h * P if u == 0 else (h // 2) * SEQ
                            mm = eng.matmul(bank[2 + u][:, c:c + keys],
                                            lhsT=headsT[half, q(h), rows], rhs=headsT[half, k(h), 0:keys],
                                            start=True, stop=True)
                        if odd:
                            mm.then_inc(scores, 2 if u == 0 else 1)
                        elif u == 0:
                            pe(mm)

            def attend_turn(A):
                for u in range(3):
                    eng.wait_ge(exped, 3 * A + (1 if u == 0 else 3))
                    for h in range(4):
                        if u == 0:
                            src = probs[:, 0, h * P:(h + 1) * P]
                        else:
                            c = (h // 2) * SEQ + (u - 1) * P
                            src = probs[:, 1 + h % 2, c:c + P]
                        mm = eng.transpose(bank[2 + u][:, h * P:(h + 1) * P], src, ident[:, :])
                    mm.then_inc(pT_ready, 1)

            def attend_values(A, v, dv):
                eng.wait_ge(pT_act, 2 * A + 4)
                eng.wait_ge(pT_dve, A + 2)
                eng.wait_ge(o_done, A + 2)
                for r in range(RT):
                    for h in range(4):
                        out = bank[5][:, (4 * r + h) * dv:(4 * r + h + 1) * dv] if dv == HD else \
                            bank[5 + r][:, h * dv:(h + 1) * dv]
                        for kt in range(r + 1):
                            mm = eng.matmul(out, lhsT=probsT[:, r + kt, h * P:(h + 1) * P], rhs=v(kt, h),
                                            start=(kt == 0), stop=(kt == r))
                mm.then_inc(pv_ready, 1)

            def ffn(p0, l, norm, bank_read):
                def gate_up(p, c):
                    is_first, is_second = (isinstance(c, int) and c == n for n in (0, 1))
                    out = bank[4:6] if is_first else bank[0:2]

                    def tile(r, k0, k1, j, back):
                        for k in range(k0, k1):
                            mm = three(out[r][:, :], k, slice(r * P, (r + 1) * P), j, (k - back) * UNIT,
                                       start=(k == 0), stop=(k == 7))
                            if is_second and r == 0 and k == 0:
                                mm.then_inc(used[1], 1)
                        return mm

                    eng.wait_ge(lo_ready[0], p + 2)
                    if is_first:
                        tile(0, 0, 4, 0, 0)
                        turn_half(norm, 1)
                        tile(1, 0, 4, 0, 0).then_inc(used[0], 1)
                        eng.wait_ge(turned_lo, norm * 4 + 4)
                        eng.wait_ge(lo_ready[1], p + 2)
                        for r in range(RT):
                            tile(r, 4, 8, 1, 4).then_inc(gu_ready, 1)
                        return
                    for r in range(RT):
                        if is_second:
                            bank_read(r)
                        else:
                            eng.wait_ge(gu_free, l * 2 * FF_STEPS + 2 * c - 1 + r)
                        mm = tile(r, 0, 6, 0, 0)
                    mm.then_inc(used[0], 1)
                    if is_second:
                        turn(0)
                    eng.wait_ge(lo_ready[1], p + 2)
                    for r in range(RT):
                        tile(r, 6, 8, 1, 6).then_inc(gu_ready, 1)

                def down(c, first, last, between=None):
                    eng.wait_ge(ff_lo, l * 2 * FF_STEPS + 2 * c + 2)
                    three.act = hT if last else ffT
                    for kk in range(2):
                        if between and kk == 1:
                            between()
                        j, w0 = (kk, 0) if last else (1, (2 + 2 * kk) * UNIT)
                        if last:
                            eng.wait_ge(lo_ready[j], p0 + FF_STEPS + 2)
                        for n in range(2):
                            for r in range(RT):
                                mm = three(bank[2 + 2 * n + r][:, :], kk, slice(r * P, (r + 1) * P), j,
                                           w0 + n * UNIT, start=(first and kk == 0), stop=(last and kk == 1))
                                if last and kk == 1 and not (r == 1 and n == 1):
                                    mm.then_inc(down_ready, 1)
                        if last or kk == 1:
                            mm.then_inc(used[j], 1)
                    three.act = hT

                def turn(c):
                    for r in range(RT):
                        eng.wait_ge(gu_free, l * 2 * FF_STEPS + 2 * c + 1 + r)
                        for k in range(2):
                            mm = eng.transpose(bank[6 + r][:, k * P:(k + 1) * P],
                                               probs[:, r, k * P:(k + 1) * P], ident[:, :])
                        mm.then_inc(ff_turned, 1)

                three.act = hT
                gate_up(p0, 0)
                gate_up(p0 + 1, 1)
                down(0, True, False)
                turn(1)
                with eng.Fori(2, FF_STEPS - 1) as c:
                    gate_up(p0 + c, c)
                    down(c - 1, False, False)
                    turn(c)
                last = FF_STEPS - 1
                gate_up(p0 + last, last)
                down(last - 1, False, False, between=lambda: turn(last))
                down(last, False, True)

            eng.wait_ge(const_ready, 4)
            eng.sem_inc(used[0], 1)
            eng.sem_inc(used[1], 1)
            eng.sem_inc(pv_ready, 1)
            with eng.Fori(0, LAYERS) as l:
                p, A = l * PAIRS1, l * NGRP

                def project(i, jj, between=None):
                    def bank_read(r):
                        eng.wait_ge((z_act, z_dve)[r], l * 8 + i)
                    chunk(p + i, jj, NARROW if i == 1 else COLS, bank_read if i else None, between)

                def zcols(c0):
                    return lambda i, r: z[:, r, c0 + i * P:c0 + (i + 1) * P]

                def heads_read(s):
                    eng.wait_ge(heads_act, l * 6 + s + 1)
                    eng.wait_ge(heads_dve, l * 5 + s + (s == 0))

                turn_half(l * 3, 0)
                eng.wait_ge(turned_lo, l * 12 + 2)
                three.act = hT
                project(0, 0, between=lambda: turn_half(l * 3, 1))
                eng.wait_ge(turned_lo, l * 12 + 4)
                project(0, 1)
                project(1, 0); project(1, 1)
                project(2, 0); project(2, 1)
                turn_heads(l, 0, zcols(IQ), 4)
                project(3, 0)
                turn_heads(l, 1, lambda i, r: scr_ik(r), 1)
                project(3, 1)
                for u in range(3):
                    index_scores(l, u)
                project(4, 0)
                turn_heads(l, 2, zcols(DQ), 4)
                for u in range(3, 6):
                    index_scores(l, u)
                turn_heads(l, 3, zcols(DK), 4)
                project(4, 1)
                heads_read(3)
                eng.wait_ge(idx_relu, l * 6 + 6)
                attend_scores(A, lambda h: T_DQ + h // 2, lambda h: T_DK + h // 2)
                project(5, 0); project(5, 1)
                attend_turn(A)
                project(6, 0)
                attend_scores(A + 1, lambda h: T_DQ + 2 + h // 2, lambda h: T_DK + 2 + h // 2)
                attend_values(A, lambda kt, h: z[:, kt, DV + (h // 2) * 2 * HD:DV + (h // 2 + 1) * 2 * HD], 2 * HD)
                project(6, 1)
                attend_turn(A + 1)
                eng.wait_ge(o_done, A + 3)
                turn_heads(l, 4, zcols(MQ), 4)
                project(7, 0)
                heads_read(4)
                attend_scores(A + 2, lambda h: T_MQ + h // 2, lambda h: T_MK + h // 2)
                attend_values(A + 1, lambda kt, h: z[:, kt, DV + (2 + h // 2) * 2 * HD:DV + (3 + h // 2) * 2 * HD], 2 * HD)
                project(7, 1)
                attend_turn(A + 2)
                eng.wait_ge(o_done, A + 4)
                turn_heads(l, 5, zcols(SQ), 4)
                heads_read(5)
                attend_scores(A + 3, lambda h: T_SQ + h // 2, lambda h: T_SK + h // 2)
                for r in range(RT):
                    eng.wait_ge((z_act, z_dve)[r], l * 8 + 8)
                attend_values(A + 2, lambda kt, h: z[:, kt, MV + h * HD:MV + (h + 1) * HD], HD)
                turn_half(l * 3 + 1, 0)
                attend_turn(A + 3)
                eng.wait_ge(turned_lo, l * 12 + 6)
                three.act = mixT
                chunk(p + 8, 0, between=lambda: attend_values(
                    A + 3, lambda kt, h: z[:, kt, SV + h * HD:SV + (h + 1) * HD], HD))
                turn_half(l * 3 + 1, 1)
                eng.wait_ge(turned_lo, l * 12 + 8)
                chunk(p + 8, 1)
                chunk(p + 9, 0, bank_read=lambda r: eng.wait_ge(out_added, l * 4 + 1 + r))
                turn_half(l * 3 + 2, 0)
                chunk(p + 9, 1)
                three.act = hT
                eng.wait_ge(turned_lo, l * 12 + 10)
                ffn(p + 10, l, l * 3 + 2, lambda r: eng.wait_ge(out_added, l * 4 + 3 + r))
                pe.restart(eng)

            p, A = B2, LAYERS * NGRP

            def product_chunk(b, j, n=COLS):
                chunk(p + b, j, n, (lambda r: eng.wait_ge(free[r], product(b))) if b else None)

            def channel_chunk(b, j):
                if j == 0:
                    for r in range(RT):
                        eng.wait_ge(free[r], product(b))
                eng.wait_ge(lo_ready[j], p + b + 2)
                for c in range(4):
                    out = bank[c // 2][:, (c % 2) * SEQ:(c % 2 + 1) * SEQ]
                    for k in range(4):
                        w = slice(k * COLS + c * P, k * COLS + (c + 1) * P)
                        for n, (a, h) in enumerate(((whi, 0), (wlo, 0), (whi, 1))):
                            mm = eng.matmul(out, lhsT=a[j][:, w], rhs=hT[h][:, 4 * j + k, :],
                                            start=(j == 0 and k == 0 and n == 0 and c % 2 == 0),
                                            stop=(j == 1 and k == 3 and n == 2), skip_group_check=True)
                    if j == 1 and c == 1:
                        mm.then_inc(half_ready, 1)
                mm.then_inc(used[j], 1)

            def compress(b, j):
                c = 2 * (b - 6) + j
                if c == 0:
                    for r in range(RT):
                        eng.wait_ge(free[r], product(6))
                    eng.wait_ge(flat_lo, 1)
                eng.wait_ge(lo_ready[j], p + b + 2)
                three.act = flat
                for v in range(2):
                    for k in range(4):
                        mm = three(bank[v][0:COMP, 0:SEQ], 4 * c + k, slice(0, COMP), j, k * COLS + v * SEQ,
                                   start=(c == 0 and k == 0), stop=(c == 3 and k == 3), n=SEQ)
                    if c == 3 and v == 0:
                        mm.then_inc(half_ready, 1)
                mm.then_inc(used[j], 1)
                three.act = hT

            def wait_fill(n, at):
                if at:
                    eng.wait_ge(read67[n], at)

            def turn_four(src, at):
                for n in range(2):
                    wait_fill(n, at)
                    for q in range(2):
                        for r in range(RT):
                            mm = eng.transpose(bank[6 + n][:, (q * RT + r) * P:(q * RT + r + 1) * P],
                                               src(2 * n + q, r), ident[:, :])
                    mm.then_inc(filled, 1)

            def group_scores(i):
                g = i % 4
                attend_scores(A + i, lambda h: 2 * g + h // 2, lambda h: (T2_KS, T2_KW)[i // 4] + g)

            def group_values(i):
                c0 = (VS2, VW2)[i // 4] + (i % 4) * HD
                attend_values(A + i, lambda kt, h: z[:, kt, c0:c0 + HD], HD)

            rows_before = 4
            turn_rows(6)
            three.act = hT
            product_chunk(0, 0); product_chunk(0, 1)
            product_chunk(1, 0); product_chunk(1, 1)
            eng.wait_ge(dup_ready, 1)
            turn_four(lambda g, r: scr[:, r, g * P:(g + 1) * P], 0)
            product_chunk(2, 0)
            eng.wait_ge(dup_ready, 2)
            turn_four(lambda g, r: probs[:, r, g * P:(g + 1) * P], 1)
            product_chunk(2, 1)
            product_chunk(3, 0); product_chunk(3, 1)
            for n in range(2):
                if n == 0:
                    for r in range(RT):
                        eng.wait_ge(free[r], 3)
                turn_four(lambda i, r, n=n: z[:, r, Q2 + (4 * n + i) * P:Q2 + (4 * n + i + 1) * P], 2 + n)
            product_chunk(4, 0, GATES); product_chunk(4, 1, GATES)
            product_chunk(5, 0)
            eng.wait_ge(dup_ready, 3)
            turn_four(lambda g, r: scr[:, r, g * P:(g + 1) * P], 4)
            product_chunk(5, 1)
            compress(6, 0); compress(6, 1)
            eng.wait_ge(dup_ready, 4)
            turn_four(lambda g, r: probs[:, r, g * P:(g + 1) * P], 5)
            compress(7, 0); compress(7, 1)
            product_chunk(8, 0)
            eng.wait_ge(free[0], 7)
            eng.wait_ge(free[1], 7)
            wait_fill(1, 6)
            for i in range(4):
                mm = eng.transpose(bank[7][:, i * COMP:(i + 1) * COMP], sqr[0:COMP, i * P:(i + 1) * P],
                                   ident[0:COMP, 0:COMP])
            mm.then_inc(filled, 1)
            product_chunk(8, 1)
            eng.wait_ge(read67[1], 7)
            wait_fill(0, 6)
            for k in range(2):
                mm = eng.matmul(bank[6][:, 0:COMP // 2], lhsT=wk2[:, k, :], rhs=hidT[:, k * COMP:k * COMP + COMP // 2],
                                start=(k == 0), stop=(k == 1))
            mm.then_inc(filled, 1)
            eng.wait_ge(pad_ready, 1)
            wait_fill(1, 7)
            for g in range(KV_GROUPS):
                for k in range(2):
                    mm = eng.matmul(bank[7][:, g * HD:(g + 1) * HD], lhsT=scr[:, k, g * P:(g + 1) * P],
                                    rhs=wv2[:, k, :], start=(k == 0), stop=(k == 1))
            mm.then_inc(filled, 1)
            product_chunk(9, 0)
            eng.wait_ge(read67[0], 7)
            for odd in range(2):
                half = slice(HD * odd, HD * odd + HD)
                for r in range(RT):
                    for i in range(8):
                        g = i // 2
                        mm = eng.matmul(bank[2 + odd][:, r * P + i * 16:r * P + i * 16 + CMP],
                                        lhsT=headsT[half, i, r * P:(r + 1) * P],
                                        rhs=headsT[half, T2_KC, g * CMP:(g + 1) * CMP], start=True, stop=True)
                mm.then_inc(cs_ready, 1)
            product_chunk(9, 1)
            eng.wait_ge(cn_ready, 1)
            for r in range(RT):
                for g in range(KV_GROUPS):
                    mm = eng.transpose(bank[2 + r][:, g * P:(g + 1) * P], probs[:, r, g * P:(g + 1) * P], ident[:, :])
                mm.then_inc(ct_ready, 1)
            product_chunk(10, 0)
            eng.wait_ge(cT_act, 1)
            eng.wait_ge(cT_dve, 1)
            eng.wait_ge(read67[1], 8)
            for r in range(RT):
                for g in range(KV_GROUPS):
                    mm = eng.matmul(bank[4 - 2 * r + g // 2][:, (g % 2) * SEQ:(g % 2 + 1) * SEQ],
                                    lhsT=probsT[:, r, g * P:(g + 1) * P], rhs=headsT[:, T2_V + g, :],
                                    start=True, stop=True)
                mm.then_inc(cv_ready, 1)
            product_chunk(10, 1)
            eng.wait_ge(cv_done, 2)
            group_scores(0)
            product_chunk(11, 0)
            attend_turn(A)
            product_chunk(11, 1)
            group_scores(1); group_values(0)
            def mix_positions(r):
                eng.wait_ge(vn_ready, r + 1)
                for g in range(4):
                    if g % 2 == 0:
                        wait_fill(g // 2, (7, 8)[g // 2] + r)
                    mm = eng.matmul(bank[6 + g // 2][:, (g % 2) * SEQ:(g % 2 + 1) * SEQ], lhsT=w_s[:, g, :],
                                    rhs=z[:, r, g * SEQ:(g + 1) * SEQ], start=True, stop=True)
                    if g % 2:
                        mm.then_inc(filled, 1)

            eng.wait_ge(ws_ready, 1)
            mix_positions(0)
            product_chunk(12, 0)
            attend_turn(A + 1)
            mix_positions(1)
            product_chunk(12, 1)
            group_scores(2); group_values(1)
            turn_rows(7, z[:, :, U2:U2 + D])
            three.act = mixT
            product_chunk(13, 0)
            attend_turn(A + 2)
            product_chunk(13, 1)
            three.act = hT
            for b, i in ((14, 2), (15, 3), (16, 4), (17, 5), (18, 6), (19, 7)):
                one = channel_chunk if b >= 16 else product_chunk
                if i < 7:
                    group_scores(i + 1)
                group_values(i)
                if b == 15:
                    three.act = mixT
                one(b, 0)
                if i < 7:
                    attend_turn(A + i + 1)
                one(b, 1)
                three.act = hT
            eng.wait_ge(rg_loaded, 32)

            def gates(c):
                eng.wait_ge(xc_ready, c + 1)
                wait_fill(c % 2, (9, 10)[c % 2] + c // 2)
                for v in range(2):
                    for h in range(2):
                        half = slice(HD * h, HD * h + HD)
                        w = z[half, v, KC2 + c * HD:KC2 + (c + 1) * HD]
                        mm = eng.matmul(bank[6 + c % 2][half, v * SEQ:(v + 1) * SEQ], lhsT=w,
                                        rhs=channels(c)[half, :], start=True, stop=True)
                mm.then_inc(filled, 1)

            product_chunk(20, 0)
            turn_half(8, 0)
            product_chunk(20, 1)
            eng.wait_ge(turned_lo, 34)
            for b in range(21, 28):
                three.act = (mixT if b in (21, 23, 26, 27) else hT)
                if b == 26:
                    eng.wait_ge(yc_lo, 1)
                for j in range(2):
                    if (b, j) == (21, 0):
                        chunk(p + b, 0, COLS, lambda r: eng.wait_ge(free[r], product(21)),
                              between=lambda: turn_half(8, 1))
                        eng.wait_ge(turned_lo, 36)
                    else:
                        product_chunk(b, j)
                    if (b, j) == (27, 0):
                        turn_half(9, 0, z[:, :, U2:U2 + D])
                    if b in (21, 22):
                        c = 4 * (b - 21) + 2 * j
                        gates(c)
                        gates(c + 1)
            eng.wait_ge(turned_lo, 38)
            chunk(p + 28, 0, COLS, lambda r: eng.wait_ge(free[r], product(28)),
                  between=lambda: turn_half(9, 1, z[:, :, U2:U2 + D]))
            eng.wait_ge(turned_lo, 40)
            product_chunk(28, 1)
            product_chunk(29, 0); product_chunk(29, 1)
            three.act = hT
            turn_half(10, 0)
            eng.wait_ge(turned_lo, 42)
            ffn(p + PAIRS2, LAYERS, 10, lambda r: eng.wait_ge(free[r], product(30)))

        @block.scalar
        def _(eng):
            def split_hi(p, j, n):
                eng.wait_ge(raw_loaded[j], 16 * p + 16)
                eng.wait_ge(used[j], p + 1)
                eng.activation(whi[j][:, 0:n], raw[j][:, 0:n], ACT.Copy).then_inc(hi_ready[j], 1)

            def norm_stats():
                for r in range(RT):
                    act(eng.activation(z[:, r, 0:D], x[:, r, :], ACT.Square, accum_out=ssq[:, r:r + 1]))
                act.wait(eng)
                act(eng.activation(ssq[:, 2:4], ssq[:, 0:2], ACT.Ln, bias=eps[:, 0:1], scale=1.0 / D))
                act.wait(eng)
                eng.activation(ssq[:, 4:6], ssq[:, 2:4], ACT.Exp, scale=-0.5).then_inc(rs_ready, 1)

            def turned_hi_copy(i, dst, scale=1.0, halves=(0, 1)):
                for h in halves:
                    for r in range(RT):
                        eng.wait_ge(turned, i * 4 + 2 * h + r + 1)
                        eng.activation(dst[0][:, 4 * h:4 * h + 4, r * P:(r + 1) * P],
                                       bank[6 + r][:, :].rearrange("p (k c) -> p k c", k=4),
                                       ACT.Copy, scale=scale).then_inc(turned_hi, 1)

            def copy_z0(p, l, i, c0, n=COLS):
                eng.wait_ge(half_ready, p)
                eng.activation(z[:, 0, c0:c0 + n], bank[0][:, 0:n], ACT.Copy, scale=ssq[:, 4:5]).then_inc(z_act, 1)

            def head_stats(l, s):
                for r in range(RT):
                    n = 2 * s + r
                    c0 = HEAD_SETS[s]
                    if r == 0:
                        eng.wait_ge(z_dve, l * 8 + (3, 4, 6, 7)[s])
                        eng.wait_ge(z_act, l * 8 + (3, 4, 6, 7)[s])
                        if s:
                            eng.wait_ge(prep, l * 6 + 2 + s)
                    if s or r:
                        eng.wait_ge(ssq_ready, l * 8 + n)
                    eng.activation(sqr[:, :], z[:, r, c0:c0 + COLS], ACT.Square).then_inc(squares, 1)
                    eng.wait_ge(ssq_ready, l * 8 + n + 1)
                    act(eng.activation(ssq[:, 8:16], hss[:, r, :], ACT.Ln, bias=eps[:, 0:1], scale=1.0 / HD))
                    act.wait(eng)
                    eng.activation(hrs[:, r, :], ssq[:, 8:16], ACT.Exp, scale=-0.5).then_inc(hrs_ready, 1)

            def heads_copy(l, s):
                n = (0, 2, 3, 5, 7, 9)[s]
                eng.wait_ge(heads_turned, l * 11 + n + 1)
                t0 = (T_IQ, T_IK, T_DQ, T_DK, T_MQ, T_SQ)[s]
                m = 1 if s == 1 else 2
                eng.activation(headsT[:, t0:t0 + m, :], bank[6][:, 0:m * SEQ].rearrange("p (m c) -> p m c", m=m),
                               ACT.Copy).then_inc(heads_act, 1)

            def index_relu(l, u):
                eng.wait_ge(idx_ready, l * 6 + u + 1)
                if u >= 3:
                    eng.wait_ge(idx_acc, l * 6 + u - 2)
                eng.activation(probs[:, u % 3, :], bank[2 + u % 3][:, :], ACT.Relu, scale=HD ** -0.5)\
                   .then_inc(idx_relu, 1)

            def attend_exp(A, par):
                eng.wait_ge(o_done, A + 1)
                for u in range(3):
                    eng.wait_ge(masked, 3 * A + u + 1)
                    heads = range(4) if u == 0 else range(2)
                    keys = P if u == 0 else SEQ
                    for h in heads:
                        c = h if u == 0 else 4 + 2 * h + u - 1
                        part = probs[:, u, h * keys:(h + 1) * keys]
                        ins = eng.activation(part, part, ACT.Exp, bias=nmax[:, c:c + 1],
                                             accum_out=sums[:, par, c:c + 1])
                        if h == heads[-1]:
                            ins.then_inc(exped, 1)
                        else:
                            act(ins)

            def attend_copy(A):
                for u in range(2):
                    eng.wait_ge(pT_ready, 3 * A + u + 1)
                    eng.wait_ge(pv_ready, A + 1)
                    eng.activation(probsT[:, u, :], bank[2 + u][:, :], ACT.Copy).then_inc(pT_act, 1)

            def diff_stats(l, i):
                eng.wait_ge(dsq, l * 2 + i + 1)
                act(eng.activation(ssq[:, 6:10], dstat[:, 0:4], ACT.Ln, bias=eps[:, 0:1], scale=1.0 / (2 * HD)))
                act.wait(eng)
                eng.activation(dstat[:, 4:8], ssq[:, 6:10], ACT.Exp, scale=-0.5).then_inc(drs, 1)

            def ffn(p0, l, norm, stats, after_n):
                def step(c, n0, n1, out=bank, first=False, last=False):
                    dst = hT if last else ffT
                    split_hi(p0 + c + 1, 0, n0)
                    if first:
                        stats()
                        eng.preload_act_table(ACT.Silu)
                    for r in range(RT):
                        n = l * 2 * FF_STEPS + 2 * c + r
                        if r == 0:
                            eng.wait_ge(rs_ready, norm + 1)
                        eng.wait_ge(gu_ready, n + 1)
                        eng.activation(sqr[:, r * FF_STEP:(r + 1) * FF_STEP], out[r][:, 0:FF_STEP],
                                       ACT.Silu, scale=ssq[:, 4 + r:5 + r]).then_inc(silu_ready, 1)
                    if not last:
                        split_hi(p0 + c + 1, 1, n1)
                    for r in range(RT):
                        n = l * 2 * FF_STEPS + 2 * c + r
                        eng.wait_ge(ff_turned, n + 1)
                        eng.activation(dst[0][:, 0:2, r * P:(r + 1) * P],
                                       bank[6 + r][:, 0:2 * P].rearrange("p (k c) -> p k c", k=2),
                                       ACT.Copy).then_inc(ff_hi, 1)
                    if last:
                        split_hi(p0 + c + 1, 1, n1)

                step(0, ffn_elements(1, 0), ffn_elements(1, 1), bank[4:6], first=True)
                with eng.Fori(1, FF_STEPS - 1) as c:
                    step(c, ffn_elements(1, 0), ffn_elements(1, 1))
                step(FF_STEPS - 1, 2 * UNIT, 2 * UNIT, last=True)
                eng.preload_act_table_set(LN_EXP)
                if after_n is not None:
                    after_n(p0 + FF_STEPS + 1, 0)

            eng.wait_ge(const_ready, 4)
            eng.wait_ge(x_loaded, 16 * RT)
            eng.sem_inc(pT_act, 2)
            eng.preload_act_table_set(LN_EXP)
            split_hi(0, 0, 4 * UNIT)
            act.restart(eng)
            with eng.Fori(0, LAYERS) as l:
                p, A = l * PAIRS1, l * NGRP
                hi = lambda i, j: split_hi(p + i, j, 4 * (NARROW if i == 1 else COLS))
                hr = lambda i: l * HALVES + i + 1
                turned_hi_copy(l * 3, hT, halves=(0,))
                split_hi(p, 1, 4 * UNIT)
                turned_hi_copy(l * 3, hT, halves=(1,))
                eng.wait_ge(rows_ready, 12 * l + 4)
                norm_stats()
                hi(1, 0)
                eng.wait_ge(rs_ready, 2 * l + 1)
                copy_z0(hr(0), l, 0, IQ); hi(1, 1)
                hi(2, 0); copy_z0(hr(1), l, 1, IK, NARROW); hi(2, 1)
                eng.wait_ge(lam_sum, l + 1)
                eng.activation(lam[:, 2:4], lam[:, 0:2], ACT.Exp).then_inc(lam_exp, 1)
                hi(3, 0); copy_z0(hr(2), l, 2, DQ); hi(3, 1); heads_copy(l, 0)
                head_stats(l, 0)
                hi(4, 0); heads_copy(l, 1); copy_z0(hr(3), l, 3, DK); hi(4, 1)
                head_stats(l, 1)
                for u in range(3):
                    index_relu(l, u)
                hi(5, 0); heads_copy(l, 2)
                for u in range(3, 6):
                    index_relu(l, u)
                heads_copy(l, 3); copy_z0(hr(4), l, 4, DV); hi(5, 1)
                attend_exp(A, 0)
                hi(6, 0); copy_z0(hr(5), l, 5, MQ); hi(6, 1)
                attend_copy(A)
                head_stats(l, 2)
                hi(7, 0)
                attend_exp(A + 1, 1)
                diff_stats(l, 0)
                copy_z0(hr(6), l, 6, SQ); hi(7, 1)
                attend_copy(A + 1)
                heads_copy(l, 4)
                head_stats(l, 3)
                hi(8, 0)
                attend_exp(A + 2, 0)
                copy_z0(hr(7), l, 7, MV)
                attend_copy(A + 2)
                heads_copy(l, 5)
                diff_stats(l, 1)
                hi(8, 1)
                attend_exp(A + 3, 1)
                turned_hi_copy(l * 3 + 1, mixT, halves=(0,))
                attend_copy(A + 3)
                turned_hi_copy(l * 3 + 1, mixT, halves=(1,))
                hi(9, 0); hi(9, 1)
                split_hi(p + 10, 0, ffn_elements(0, 0))
                turned_hi_copy(l * 3 + 2, hT, halves=(0,))
                split_hi(p + 10, 1, ffn_elements(0, 1))
                turned_hi_copy(l * 3 + 2, hT, halves=(1,))

                def after(pp, j):
                    split_hi(pp, j, 4 * UNIT)
                ffn(p + 10, l, 2 * l + 1, norm_stats, after)
                act.restart(eng)

            A = LAYERS * NGRP

            def hi2(b, j):
                n = ffn_elements(0, j) if b == PAIRS2 else 4 * (GATES if b == 4 else COLS)
                split_hi(B2 + b, j, n)

            def whole(b, r):
                if r == 0:
                    eng.wait_ge(half_ready, half_of(b))
                else:
                    eng.wait_ge(used[1], B2 + b + 2)

            def take(b, r, dst, func, n=COLS, scale=1.0):
                whole(b, r)
                eng.activation(dst, bank[r][:, 0:n], func, scale=scale).then_inc(free[r], 1)

            def fill_copy(n, count, t0):
                eng.wait_ge(filled, count)
                eng.activation(headsT[:, t0:t0 + 2, :], bank[6][:, :].rearrange("p (m c) -> p m c", m=2),
                               ACT.Copy).then_inc(read67[0], 1)

            def branch_gate(b, r):
                n = {12: 0, 14: 1, 20: 2, 22: 3, 24: 4, 25: 4}[b]
                if n:
                    eng.wait_ge(merged_done, 2 * n)
                take(b, r, gate_buffer(b)[:, r, :], ACT.Tanh, scale=0.5)

            def gates(c):
                eng.wait_ge(filled, F_GATE + c)
                if c >= 2:
                    eng.wait_ge(gx_done, c - 1)
                b, buf = bank[6 + c % 2], probs[:, c % 2, :]
                act(eng.activation(buf[:, 0:SEQ], b[:, 0:SEQ], ACT.Tanh, scale=0.5, bias=sp[:, 88 + c:89 + c]))
                eng.activation(buf[:, SEQ:2 * SEQ], b[:, SEQ:2 * SEQ], ACT.Tanh, scale=0.5,
                               bias=sp[:, 96 + c:97 + c]).then_inc(read67[c % 2], 1)
                act.wait(eng)
                act(eng.activation(headsT[:, c, :], buf[:, 0:SEQ], ACT.Tanh, scale=sp[:, 80 + c:81 + c],
                                   bias=sp[:, 80 + c:81 + c]))
                eng.activation(mix[:, c // 4, (c % 4) * SEQ:(c % 4 + 1) * SEQ], buf[:, 0:SEQ], ACT.Exp,
                               scale=sp[:, 104 + c:105 + c], bias=sp[:, 104 + c:105 + c]).then_inc(u_ready, 1)

            def split_channels(b):
                for r in range(RT):
                    whole(b, r)
                    if b == 17:
                        eng.wait_ge(xc_ready, 2 * (r + 1))
                    act(eng.activation(stage(r), bank[r][:, :], ACT.Copy))
                    for q in range(2):
                        c = 4 * (b - 16) + 2 * r + q
                        ins = eng.activation(channels(c), bank[r][:, q * SEQ:(q + 1) * SEQ], ACT.Identity,
                                             scale=par_cw[:, 4 * c + 3:4 * c + 4], bias=par_cb[:, c:c + 1])
                        if q:
                            ins.then_inc(free[r], 1)
                        else:
                            act(ins)

            def post_squares(n, banks, ready):
                for r in range(RT):
                    ready(r)
                    eng.activation(z[:, r, n * COLS:(n + 1) * COLS], banks[r][:, :], ACT.Square,
                                   accum_out=ssq[:, 8 + 2 * n + r:9 + 2 * n + r]).then_inc(squared, 1)
                if n == 0:
                    eng.wait_ge(squared, 2 + 4 * post_squares.calls)
                    act(eng.activation(ssq[:, 12:14], ssq[:, 8:10], ACT.Identity, bias=eps[:, 0:1], scale=1.0 / D))
                    post_squares.calls += 1
            post_squares.calls = 0

            def post_stats():
                eng.wait_ge(squared, 4 * post_squares.calls)
                act.wait(eng)
                for r in range(RT):
                    act(eng.activation(ssq[:, 2 + r:3 + r], ssq[:, 10 + r:11 + r], ACT.Ln, bias=ssq[:, 12 + r:13 + r],
                                       scale=1.0 / D))
                act.wait(eng)
                eng.activation(ssq[:, 4:6], ssq[:, 2:4], ACT.Exp, scale=-0.5).then_inc(rs_ready, 1)

            def row_stats(src, junk):
                for r in range(RT):
                    act(eng.activation(junk[:, r, 0:D], src[:, r, 0:D], ACT.Square, accum_out=ssq[:, r:r + 1]))
                act.wait(eng)
                act(eng.activation(ssq[:, 2:4], ssq[:, 0:2], ACT.Ln, bias=eps[:, 0:1], scale=1.0 / D))
                act.wait(eng)
                eng.activation(ssq[:, 4:6], ssq[:, 2:4], ACT.Exp, scale=-0.5).then_inc(rs_ready, 1)

            eng.wait_ge(down_added, 4 * LAYERS)
            norm_stats()
            hi2(0, 1)
            turned_hi_copy(6, hT)
            eng.wait_ge(sp_abs, 1)
            eng.activation(sp[:, 8:16], sp[:, 0:8], ACT.Exp).then_inc(sp_exp, 1)
            eng.wait_ge(sp_one, 1)
            eng.activation(sp[:, 24:32], sp[:, 16:24], ACT.Ln).then_inc(sp_ln, 1)
            hi2(1, 0); take(0, 0, z[:, 0, KC2:KC2 + COLS], ACT.Copy); hi2(1, 1)
            hi2(2, 0); take(1, 0, z[:, 0, Q2:Q2 + COLS], ACT.Copy, scale=HD ** -0.5); hi2(2, 1)
            hi2(3, 0); take(2, 0, z[:, 0, Q2 + COLS:Q2 + D], ACT.Copy, scale=HD ** -0.5); hi2(3, 1)
            hi2(4, 0); take(3, 0, z[:, 0, KS2:KS2 + COLS], ACT.Copy); hi2(4, 1)
            fill_copy(0, F_Q, 0)
            fill_copy(0, F_Q + 2, 4)
            hi2(5, 0)
            take(4, 0, z[:, 0, G2:G2 + GATES], ACT.Tanh, GATES, 0.5)
            take(4, 1, z[:, 1, G2:G2 + GATES], ACT.Tanh, GATES, 0.5)
            hi2(5, 1)
            eng.wait_ge(flat_done, 1)
            eng.activation(flat[0].rearrange("p j m -> p (j m)"), flat_f, ACT.Copy).then_inc(flat_hi, 1)
            hi2(6, 0); fill_copy(0, F_SK, T2_KS); take(5, 0, z[:, 0, KW2:KW2 + COLS], ACT.Copy); hi2(6, 1)
            hi2(7, 0); fill_copy(0, F_WK, T2_KW); hi2(7, 1)
            hi2(8, 0)
            for v in range(2):
                whole(7, v)
                eng.activation(sqr[0:COMP, v * SEQ:(v + 1) * SEQ], bank[v][0:COMP, 0:SEQ],
                               ACT.Gelu_apprx_tanh).then_inc(free[v], 1)
            hi2(8, 1)
            hi2(9, 0)
            eng.wait_ge(filled, F_HT)
            eng.activation(hidT, bank[7][:, 0:4 * COMP], ACT.Copy).then_inc(read67[1], 1)
            eng.wait_ge(filled, F_Q + 3)
            take(8, 0, z[:, 0, 0:COLS], ACT.Gelu_apprx_tanh)
            take(8, 1, z[:, 1, 0:COLS], ACT.Gelu_apprx_tanh)
            hi2(9, 1)
            eng.wait_ge(filled, F_KC)
            eng.activation(headsT[:, T2_KC, 0:COMP // 2], bank[6][:, 0:COMP // 2], ACT.Copy).then_inc(read67[0], 1)
            eng.wait_ge(cm_ready, 1)
            wide = probs[:, 0:2, :].rearrange("p r (h n) -> p (r h) n", n=32)[:, :, 0:CMP]
            eng.activation(wide, wide, ACT.Exp).then_inc(ce_ready, 1)
            hi2(10, 0)
            take(9, 0, z[:, 0, COLS:D], ACT.Gelu_apprx_tanh)
            take(9, 1, z[:, 1, COLS:D], ACT.Gelu_apprx_tanh)
            hi2(10, 1)
            eng.wait_ge(ct_ready, 1)
            eng.activation(probsT[:, 0, :], bank[2][:, :], ACT.Copy).then_inc(cT_act, 1)
            eng.preload_act_table_set(LN_EXP)
            eng.wait_ge(var_ready, 1)
            act(eng.activation(bn[:, 30:32], bn[:, 24:28].rearrange("p (r s) -> p r s", s=2)[:, :, 1], ACT.Ln,
                               bias=eps[:, 0:1]))
            act.wait(eng)
            eng.activation(bn[:, 28:30], bn[:, 30:32], ACT.Exp, scale=-0.5).then_inc(vrs_ready, 1)
            hi2(11, 0)
            take(10, 0, z[:, 0, U2:U2 + COLS], ACT.Gelu_apprx_tanh)
            take(10, 1, z[:, 1, U2:U2 + COLS], ACT.Gelu_apprx_tanh)
            hi2(11, 1)
            attend_exp(A, 0)
            hi2(12, 0); attend_copy(A)
            take(11, 0, z[:, 0, U2 + COLS:U2 + D], ACT.Gelu_apprx_tanh)
            take(11, 1, z[:, 1, U2 + COLS:U2 + D], ACT.Gelu_apprx_tanh)
            hi2(12, 1)
            for b in range(12, 19):
                i = b - 11
                attend_exp(A + i, i % 2)
                hi2(b + 1, 0)
                attend_copy(A + i)
                if b in (12, 14):
                    branch_gate(b, 0); branch_gate(b, 1)
                if b in (16, 17):
                    split_channels(b)
                if b == 18:
                    for r in range(2):
                        take(b, r, headsT[:, 8 + 2 * r:10 + 2 * r, :].rearrange("p a c -> p (a c)"), ACT.Gelu_apprx_tanh)
                hi2(b + 1, 1)
                if b == 12:
                    turned_hi_copy(7, mixT)
            hi2(20, 0)
            for r in range(2):
                take(19, r, headsT[:, 12 + 2 * r:14 + 2 * r, :].rearrange("p a c -> p (a c)"), ACT.Gelu_apprx_tanh)
            hi2(20, 1)
            eng.preload_act_table_set(EXP_TANH)
            hi2(21, 0)
            turned_hi_copy(8, mixT, halves=(0,))
            branch_gate(20, 0); branch_gate(20, 1)
            turned_hi_copy(8, mixT, halves=(1,))
            hi2(21, 1)
            hi2(22, 0); gates(0); gates(1)
            hi2(22, 1); gates(2); gates(3)
            hi2(23, 0); gates(4); gates(5)
            branch_gate(22, 0); branch_gate(22, 1)
            hi2(23, 1); gates(6); gates(7)
            hi2(24, 0)
            act.wait(eng)
            eng.wait_ge(u_ready, 8)
            eng.activation(headsT[:, 0:8, :], headsT[:, 0:8, :], ACT.Sqrt).then_inc(root_ready, 1)
            eng.preload_act_table_set(EXP_TANH)
            hi2(24, 1)
            hi2(25, 0); branch_gate(24, 0); branch_gate(24, 1); hi2(25, 1)
            eng.wait_ge(yc_ready, 1)
            eng.wait_ge(used[1], B2 + 23 + 2)
            eng.activation(mixT[0][:, :, :], headsT[:, 0:8, :], ACT.Copy).then_inc(yc_hi, 1)
            hi2(26, 0); branch_gate(25, 0); branch_gate(25, 1); hi2(26, 1)
            hi2(27, 0); hi2(27, 1)
            hi2(28, 0)
            turned_hi_copy(9, mixT, scale=0.5, halves=(0,))
            hi2(28, 1)
            turned_hi_copy(9, mixT, scale=0.5, halves=(1,))
            eng.preload_act_table_set(LN_EXP)
            hi2(29, 0); post_squares(0, bank, lambda r: whole(28, r)); hi2(29, 1)
            hi2(30, 0); post_squares(1, bank, lambda r: whole(29, r))
            post_stats()
            hi2(30, 1)
            turned_hi_copy(10, hT)

            def ffn_stats():
                eng.wait_ge(x_added, 4)
                row_stats(x, z)
            ffn(B2 + PAIRS2, LAYERS, 6, ffn_stats, None)
            for n in range(2):
                def down(r, n=n):
                    if 2 * n + r < 3:
                        eng.wait_ge(down_ready, LAYERS * 3 + 2 * n + r + 1)
                    else:
                        eng.wait_ge(used[1], B2 + PAIRS2 + FF_STEPS + 2)
                post_squares(n, bank[2 + 2 * n:], down)
            post_stats()

        @block.vector
        def _(eng):
            def split_lo(p, j, n):
                eng.wait_ge(hi_ready[j], p + 1)
                eng.tensor_tensor(wlo[j][:, 0:n], raw[j][:, 0:n], whi[j][:, 0:n].bitcast(F32),
                                  ALU.subtract).then_inc(lo_ready[j], 1)

            def gain_rows(r, h, g=gain):
                cols = slice(h * COLS, (h + 1) * COLS)
                eng.tensor_tensor(mix[:, r, cols], x[:, r, cols], g[:, cols], ALU.mult).then_inc(rows_ready, 1)

            def post_gain(n, r, b, nth):
                cols = slice(n * COLS, (n + 1) * COLS)
                eng.wait_ge(squared, 4 * nth + 2 * n + r + 1)
                return eng.tensor_tensor(mix[:, r, cols], b[:, :], gain[:, cols], ALU.mult)

            def turned_lo_copy(i, dst, scale=None, halves=(0, 1)):
                for h in halves:
                    for r in range(RT):
                        n = i * 4 + 2 * h + r
                        eng.wait_ge(turned_hi, n + 1)
                        cols = slice(r * P, (r + 1) * P)
                        high = dst[0][:, 4 * h:4 * h + 4, cols].bitcast(F32)
                        low = dst[1][:, 4 * h:4 * h + 4, cols]
                        src = bank[6 + r][:, :].rearrange("p (k c) -> p k c", k=4)
                        if scale is None:
                            ins = eng.tensor_tensor(low, src, high, ALU.subtract)
                        else:
                            ins = eng.scalar_tensor_tensor(out=low, in0=src, scalar=scale, in1=high,
                                                           op0=ALU.mult, op1=ALU.subtract)
                        ins.then_inc(turned_lo, 1)

            def copy_z1(p, c0, n=COLS):
                eng.wait_ge(used[1], p + 2)
                eng.tensor_scalar(z[:, 1, c0:c0 + n], bank[1][:, 0:n], ssq[:, 5:6], None, ALU.mult)\
                   .then_inc(z_dve, 1)

            def tables(l):
                eng.wait_ge(par_loaded, 64 * l + 64)
                dve(eng.tensor_scalar(hgain[:, 0:3, :], hgain[:, 0:3, :], HD ** -0.5, None, ALU.mult))
                dve.wait(eng)
                h = HD // 2
                for r in range(RT):
                    dve(eng.tensor_tensor(gain_c[:, r], hgain[:, :, :],
                                          rope_c[:, r, :].unsqueeze(1).to_broadcast([P, 6, HD]), ALU.mult))
                    for a, b in ((0, h), (h, 0)):
                        dve(eng.tensor_tensor(gain_s[:, r, :, a:a + h], hgain[:, :, b:b + h],
                                              rope_s[:, r, a:a + h].unsqueeze(1).to_broadcast([P, 6, h]), ALU.mult))
                dve(eng.tensor_tensor(scr[:, 0, 0:HD], lamp[:, 0, :], lamp[:, 1, :], ALU.mult))
                dve(eng.tensor_tensor(scr[:, 0, HD:2 * HD], lamp[:, 2, :], lamp[:, 3, :], ALU.mult))
                dve.wait(eng)
                eng.sem_inc(tables_ready, 1)
                eng.tensor_reduce(lam[:, 0:2], scr[:, 0, 0:2 * HD].rearrange("p (a d) -> p a d", a=2), AX.X,
                                  ALU.add).then_inc(lam_sum, 1)

            def lambda_value(l):
                eng.wait_ge(lam_exp, l + 1)
                dve(eng.tensor_tensor(lam[:, 0:1], lam[:, 2:3], lam[:, 3:4], ALU.subtract))
                dve.wait(eng)
                dve(eng.tensor_tensor(lam[:, 0:1], lam[:, 0:1], lam_c[:, 0:1], ALU.add))
                dve(eng.tensor_scalar(sub_g[:, :], sub_g[:, :], lam_c[:, 1:2], None, ALU.mult))
                dve.wait(eng)

            def head_sums(l, s):
                for r in range(RT):
                    eng.wait_ge(squares, l * 8 + 2 * s + r + 1)
                    eng.tensor_reduce(hss[:, r, :], sqr[:, :].rearrange("p (n d) -> p n d", d=HD), AX.X,
                                      ALU.add).then_inc(ssq_ready, 1)

            def heads_copy(l, s):
                n = (0, None, 3, 5, 7, 9)[s]
                eng.wait_ge(heads_turned, l * 11 + n + 2)
                t0 = (T_IQ, None, T_DQ, T_DK, T_MQ, T_SQ)[s] + 2
                eng.tensor_copy(headsT[:, t0:t0 + 2, :], bank[7][:, :].rearrange("p (m c) -> p m c", m=2))\
                   .then_inc(heads_dve, 1)

            def index_sum(l, u):
                eng.wait_ge(idx_relu, l * 6 + u + 1)
                r, keys = (0, P) if u < 2 else (1, SEQ)
                acc = index[:, 0:P] if u < 2 else index[:, P:3 * P]
                for i, h in enumerate(index_heads(u)):
                    part, w = probs[:, u % 3, i * keys:(i + 1) * keys], z[:, r, IW + h:IW + h + 1]
                    if h == 0:
                        ins = eng.tensor_scalar(acc, part, w, None, ALU.mult)
                    else:
                        ins = eng.scalar_tensor_tensor(out=acc, in0=part, scalar=w, in1=acc, op0=ALU.mult,
                                                       op1=ALU.add)
                    if i == (3 if u < 2 else 1):
                        ins.then_inc(idx_acc, 1)
                        eng.wait_ge(idx_acc, l * 6 + u + 1)
                    else:
                        dve(ins)
                        dve.wait(eng)

            def topk_rounds(a, b):
                if a == 0:
                    dve(eng.tensor_tensor(index[:, :], index[:, :], causal[:, :], ALU.add))
                    dve.wait(eng)
                for _ in range(a, b):
                    for r, part in enumerate((index[:, 0:P], index[:, P:3 * P])):
                        dve(eng.max(top8[:, r, :], part))
                    dve.wait(eng)
                    for r, part in enumerate((index[:, 0:P], index[:, P:3 * P])):
                        dve(eng.match_replace(part, top8[:, r, :], part, TAKEN))
                    dve.wait(eng)

            def topk_mask():
                dve(eng.tensor_scalar(chosen[:, :], index[:, :], TAKEN / 2, NEG, ALU.is_gt, ALU.mult))
                dve.wait(eng)
                dve(eng.tensor_tensor(chosen[:, :], chosen[:, :], causal[:, :], ALU.add))
                dve.wait(eng)

            def attend_mask(A, mask):
                for u in range(3):
                    eng.wait_ge(scores, 3 * A + u + 1)
                    n, keys = (4, P) if u == 0 else (2, SEQ)
                    m = mask[:, 0:P] if u == 0 else mask[:, P:3 * P]
                    part = probs[:, u, :].rearrange("p (n k) -> p n k", n=n)
                    dve(eng.tensor_tensor(part, bank[2 + u][:, :].rearrange("p (n k) -> p n k", n=n),
                                          m.unsqueeze(1).to_broadcast([P, n, keys]), ALU.add))
                    dve.wait(eng)
                    top = nmax[:, 0:4] if u == 0 else \
                        nmax[:, 4:8].rearrange("p (n two) -> p n two", two=2)[:, :, u - 1]
                    eng.tensor_reduce(top, part, AX.X, ALU.max, negate=True).then_inc(masked, 1)

            def attend_copy(A):
                eng.wait_ge(pT_ready, 3 * A + 3)
                eng.wait_ge(pv_ready, A + 1)
                eng.tensor_copy(probsT[:, 2, :], bank[4][:, :]).then_inc(pT_dve, 1)

            def attend_out(A, par, dst):
                eng.wait_ge(pv_ready, A + 2)
                dve(eng.reciprocal(inv[:, :], sums[:, par, :]))
                dve.wait(eng)
                for r in range(RT):
                    ins = eng.tensor_tensor(dst(r), bank[5][:, r * SEQ:(r + 1) * SEQ].rearrange("p (n d) -> p n d", d=HD),
                                            inv[:, 4 * r:4 * r + 4].unsqueeze(2).to_broadcast([P, 4, HD]), ALU.mult)
                    if r:
                        ins.then_inc(o_done, 1)
                    else:
                        dve(ins)

            def diff_out(A, par):
                eng.wait_ge(pv_ready, A + 2)
                dve(eng.reciprocal(inv[:, :], sums[:, par, :]))
                dve.wait(eng)
                odd = inv[:, :].rearrange("p (n two) -> p n two", two=2)[:, :, 1:2]
                dve(eng.tensor_scalar(odd, odd, lam[:, 0:1], None, ALU.mult))
                dve.wait(eng)
                W = 2 * HD
                for r in range(RT):
                    o = bank[5 + r][:, :].rearrange("p (n two d) -> p n two d", two=2, d=W)
                    c = inv[:, 4 * r:4 * r + 4].rearrange("p (n two) -> p n two", two=2)
                    for w in range(2):
                        ins = eng.tensor_tensor(scr[:, w, r * 2 * W:(r + 1) * 2 * W].rearrange("p (n d) -> p n d", d=W),
                                                o[:, :, w, :], c[:, :, w:w + 1].to_broadcast([P, 2, W]), ALU.mult)
                        if r and w:
                            ins.then_inc(o_done, 1)
                            eng.wait_ge(o_done, A + 3)
                        else:
                            dve(ins)
                dve.wait(eng)
                dve(eng.tensor_tensor(scr[:, 0, :], scr[:, 0, :], scr[:, 1, :], ALU.subtract))
                dve.wait(eng)
                dve(eng.tensor_tensor(scr[:, 1, :], scr[:, 0, :], scr[:, 0, :], ALU.mult))
                dve.wait(eng)
                eng.tensor_reduce(dstat[:, 0:4], scr[:, 1, :].rearrange("p (n d) -> p n d", d=W), AX.X, ALU.add)\
                   .then_inc(dsq, 1)

            def diff_norm(l, i):
                W = 2 * HD
                a4 = scr[:, 0, :].rearrange("p (n d) -> p n d", d=W)
                dve(eng.tensor_tensor(a4, a4, sub_g[:, :].unsqueeze(1).to_broadcast([P, 4, W]), ALU.mult))
                dve.wait(eng)
                eng.wait_ge(drs, l * 2 + i + 1)
                dve(eng.tensor_tensor(mix[:, :, SEQ + 2 * i * W:SEQ + 2 * (i + 1) * W].rearrange("p r (n d) -> p r n d", d=W),
                                      scr[:, 0, :].rearrange("p (r n d) -> p r n d", r=2, d=W),
                                      dstat[:, 4:8].rearrange("p (r n) -> p r n", r=2).unsqueeze(3).to_broadcast([P, 2, 2, W]),
                                      ALU.mult))
                dve.wait(eng)

            def ffn(p0, l, norm, after):
                def step(c, n0, n1, out=bank, last=False):
                    dst = hT if last else ffT
                    split_lo(p0 + c + 1, 0, n0)
                    for r in range(RT):
                        n = l * 2 * FF_STEPS + 2 * c + r
                        if r == 0:
                            eng.wait_ge(rs_ready, norm + 1)
                        eng.wait_ge(silu_ready, n + 1)
                        eng.scalar_tensor_tensor(out=probs[:, r, 0:FF_STEP], in0=out[r][:, FF_STEP:2 * FF_STEP],
                                                 scalar=ssq[:, 4 + r:5 + r], in1=sqr[:, r * FF_STEP:(r + 1) * FF_STEP],
                                                 op0=ALU.mult, op1=ALU.mult).then_inc(gu_free, 1)
                    if not last:
                        split_lo(p0 + c + 1, 1, n1)
                    for r in range(RT):
                        n = l * 2 * FF_STEPS + 2 * c + r
                        eng.wait_ge(ff_hi, n + 1)
                        eng.tensor_tensor(dst[1][:, 0:2, r * P:(r + 1) * P],
                                          bank[6 + r][:, 0:2 * P].rearrange("p (k c) -> p k c", k=2),
                                          dst[0][:, 0:2, r * P:(r + 1) * P].bitcast(F32), ALU.subtract)\
                           .then_inc(ff_lo, 1)
                    if last:
                        split_lo(p0 + c + 1, 1, n1)

                step(0, ffn_elements(1, 0), ffn_elements(1, 1), bank[4:6])
                with eng.Fori(1, FF_STEPS - 1) as c:
                    step(c, ffn_elements(1, 0), ffn_elements(1, 1))
                step(FF_STEPS - 1, 2 * UNIT, 2 * UNIT, last=True)
                for n in range(2):
                    for r in range(RT):
                        i = 2 * n + r
                        if after is None and i == 0:
                            eng.wait_ge(gain_loaded, 16 * 8 + 16)
                        if i < 3:
                            eng.wait_ge(down_ready, l * 3 + i + 1)
                        else:
                            eng.wait_ge(used[1], p0 + FF_STEPS + 2)
                        part = x[:, r, n * COLS:(n + 1) * COLS]
                        if after is None:
                            post_gain(n, r, bank[2 + i], 1).then_inc(down_added, 1)
                        else:
                            eng.tensor_tensor(part, part, bank[2 + i][:, :], ALU.add).then_inc(down_added, 1)
                            if n == 0:
                                after(0, r)
                if after:
                    after(1, 0)
                    after(1, 1)

            eng.wait_ge(const_ready, 4)
            for j in range(2):
                eng.sem_inc(lo_ready[j], 1)
            eng.sem_inc(pT_dve, 1)
            eng.sem_inc(o_done, 2)
            eng.wait_ge(x_loaded, 16 * RT)
            eng.wait_ge(gain_loaded, 16)
            for h in range(2):
                for r in range(RT):
                    gain_rows(r, h)
            eng.wait_ge(rows_ready, 4)
            eng.sem_inc(gain_free, 1)
            split_lo(0, 0, 4 * UNIT)
            eng.wait_ge(rope_loaded, 32)
            dve.restart(eng)
            with eng.Fori(0, LAYERS) as l:
                p, A = l * PAIRS1, l * NGRP
                lo = lambda i, j: split_lo(p + i, j, 4 * (NARROW if i == 1 else COLS))

                def take(c0, n, width):
                    return lambda r: mix[:, r, c0:c0 + n * width].rearrange("p (n d) -> p n d", d=width)

                turned_lo_copy(l * 3, hT, halves=(0,))
                split_lo(p, 1, 4 * UNIT)
                turned_lo_copy(l * 3, hT, halves=(1,))
                tables(l)
                lo(1, 0)
                eng.wait_ge(rs_ready, 2 * l + 1)
                copy_z1(p, IQ); lo(1, 1)
                lo(2, 0); copy_z1(p + 1, IK, NARROW); lo(2, 1)
                lambda_value(l)
                lo(3, 0); copy_z1(p + 2, DQ); lo(3, 1); heads_copy(l, 0)
                head_sums(l, 0)
                lo(4, 0); copy_z1(p + 3, DK); lo(4, 1)
                head_sums(l, 1)
                for u in range(3):
                    index_sum(l, u)
                heads_copy(l, 2); lo(5, 0)
                for u in range(3, 6):
                    index_sum(l, u)
                heads_copy(l, 3)
                topk_rounds(0, 3)
                copy_z1(p + 4, DV); lo(5, 1)
                attend_mask(A, causal)
                topk_rounds(3, 4)
                lo(6, 0); copy_z1(p + 5, MQ); lo(6, 1)
                attend_copy(A)
                head_sums(l, 2)
                topk_rounds(4, 5)
                attend_mask(A + 1, causal)
                lo(7, 0)
                diff_out(A, 0); diff_norm(l, 0)
                copy_z1(p + 6, SQ); lo(7, 1)
                attend_copy(A + 1)
                heads_copy(l, 4)
                head_sums(l, 3)
                topk_rounds(5, 7)
                attend_mask(A + 2, causal)
                diff_out(A + 1, 1)
                attend_copy(A + 2)
                heads_copy(l, 5)
                copy_z1(p + 7, MV)
                diff_norm(l, 1)
                topk_rounds(7, 8); topk_mask()
                attend_mask(A + 3, chosen)
                attend_out(A + 2, 0, take(0, 4, HD))
                eng.wait_ge(o_done, A + 5)
                dve.wait(eng)
                eng.sem_inc(rows_ready, 2)
                lo(8, 0)
                turned_lo_copy(l * 3 + 1, mixT, halves=(0,))
                attend_copy(A + 3)
                lo(8, 1)
                attend_out(A + 3, 1, take(768, 4, HD))
                eng.wait_ge(o_done, A + 6)
                dve.wait(eng)
                eng.sem_inc(rows_ready, 2)
                turned_lo_copy(l * 3 + 1, mixT, halves=(1,))
                lo(9, 0)

                def add_out(i, r):
                    if r == 0:
                        eng.wait_ge(half_ready, l * HALVES + 8 + i + 1)
                    else:
                        eng.wait_ge(used[1], p + 8 + i + 2)
                    part = x[:, r, i * COLS:(i + 1) * COLS]
                    eng.tensor_tensor(part, part, bank[r][:, :], ALU.add).then_inc(out_added, 1)
                    eng.wait_ge(out_added, l * 4 + 2 * i + r + 1)
                    gain_rows(r, i)

                eng.wait_ge(gain_loaded, 16 * (2 * l + 1) + 16)
                add_out(0, 0); add_out(0, 1)
                lo(9, 1)
                split_lo(p + 10, 0, ffn_elements(0, 0))
                turned_lo_copy(l * 3 + 2, hT, halves=(0,))
                add_out(1, 0); add_out(1, 1)
                split_lo(p + 10, 1, ffn_elements(0, 1))
                turned_lo_copy(l * 3 + 2, hT, halves=(1,))
                eng.wait_ge(rows_ready, 12 * l + 12)
                eng.sem_inc(gain_free, 1)

                def after(n, r):
                    eng.wait_ge(down_added, l * 4 + 2 * n + r + 1)
                    if n == 0 and r == 0:
                        eng.wait_ge(gain_loaded, 16 * (2 * l + 2) + 16)
                    gain_rows(r, n)
                    if n == 1 and r == 1:
                        split_lo(p + PAIRS1, 0, 4 * UNIT)
                ffn(p + 10, l, 2 * l + 1, after)
                eng.wait_ge(rows_ready, 12 * l + 16)
                eng.sem_inc(gain_free, 1)
                dve.restart(eng)

            A = LAYERS * NGRP

            def lo2(b, j):
                n = ffn_elements(0, j) if b == PAIRS2 else 4 * (GATES if b == 4 else COLS)
                split_lo(B2 + b, j, n)

            def whole(b, r):
                if r == 0:
                    eng.wait_ge(half_ready, half_of(b))
                else:
                    eng.wait_ge(used[1], B2 + b + 2)

            def take1(b, dst, scale=None):
                whole(b, 1)
                if scale is None:
                    ins = eng.tensor_copy(dst, bank[1][:, :])
                else:
                    ins = eng.tensor_scalar(dst, bank[1][:, :], scale, None, ALU.mult)
                ins.then_inc(free[1], 1)

            def twice(dst, c0, count):
                for r in range(RT):
                    ins = eng.tensor_copy(dst[:, r, :].rearrange("p (g a d) -> p g a d", g=KV_GROUPS, a=2),
                                          z[:, r, c0:c0 + KV_GROUPS * HD].rearrange("p (g d) -> p g d", d=HD)
                                          .unsqueeze(2).to_broadcast([P, KV_GROUPS, 2, HD]))
                    if r:
                        ins.then_inc(dup_ready, 1)
                    else:
                        dve(ins)

            def blocks(v, first):
                dst = flat_f.rearrange("p (j v g n) -> p j v g n", v=2, g=KV_GROUPS, n=CMP)
                for g in range(KV_GROUPS):
                    b = bank[6 + g // 2]
                    if g % 2 == 0:
                        eng.wait_ge(filled, first + g // 2)
                    for h in range(2):
                        half = slice(HD * h, HD * h + HD)
                        src = AP_of(b[half, :], (g % 2) * SEQ + h, [[2, COMP_K], [16, CMP]])
                        ins = eng.tensor_tensor(dst[half, :, v, g, :], src,
                                                pe_kv[half, v, :].unsqueeze(2).to_broadcast([HD, COMP_K, CMP]),
                                                ALU.add)
                        if g % 2 and h:
                            ins.then_inc(read67[g // 2], 1)
                        else:
                            dve(ins)

            def fill_copy(count, t0):
                eng.wait_ge(filled, count)
                eng.tensor_copy(headsT[:, t0:t0 + 2, :], bank[7][:, :].rearrange("p (m c) -> p m c", m=2))\
                   .then_inc(read67[1], 1)

            def gate_of(r, g, branch):
                a = G2 + 12 * g
                return z[:, r, a:a + 12].rearrange("p (h b) -> p h b", b=3)[:, :, branch]

            def group_out(i):
                g, branch = i % 4, 1 + i // 4
                eng.wait_ge(pv_ready, A + i + 2)
                dve(eng.reciprocal(inv[:, :], sums[:, i % 2, :]))
                dve.wait(eng)
                for r in range(RT):
                    dve(eng.tensor_tensor(inv[:, 4 * r:4 * r + 4], inv[:, 4 * r:4 * r + 4], gate_of(r, g, branch),
                                          ALU.mult))
                dve.wait(eng)
                eng.tensor_tensor(sqr[:, :].rearrange("p (n d) -> p n d", d=HD),
                                  bank[5][:, :].rearrange("p (n d) -> p n d", d=HD),
                                  inv[:, :].unsqueeze(2).to_broadcast([P, 8, HD]), ALU.mult).then_inc(o_done, 1)
                eng.wait_ge(o_done, A + i + 3)
                part = mix[:, :, g * SEQ:(g + 1) * SEQ]
                dve(eng.tensor_tensor(part, part, sqr[:, :].rearrange("p (r c) -> p r c", r=2), ALU.add))
                dve.wait(eng)

            def merge(b):
                n = (b // 2) % 2 if b < 24 else b - 26
                first, gate = b < 16, gate_buffer(b - 1 if b < 26 else b - 2)
                for r in range(RT):
                    whole(b, r)
                    eng.wait_ge(free[r], product(b))
                    dst = merged(r, n) if first else gate[:, r, :]
                    eng.scalar_tensor_tensor(out=dst, in0=gate[:, r, :], scalar=1.0, in1=bank[r][:, :],
                                             op0=ALU.add, op1=ALU.mult).then_inc(free[r], 1)
                    eng.wait_ge(free[r], product(b) + 1)
                    if first:
                        eng.sem_inc(merged_done, 1)
                    else:
                        eng.tensor_tensor(merged(r, n), merged(r, n), gate[:, r, :], ALU.add).then_inc(merged_done, 1)

            def convolve(b):
                for q in range(4):
                    c, r = 4 * (b - 16) + q, q // 2
                    if q % 2 == 0:
                        eng.wait_ge(free[r], product(b) + 1)
                    src, dst = stage(r)[:, (q % 2) * SEQ:(q % 2 + 1) * SEQ], channels(c)
                    for back in (1, 2, 3):
                        ins = eng.scalar_tensor_tensor(out=dst[:, back:], in0=src[:, 0:SEQ - back],
                                                       scalar=par_cw[:, 4 * c + 3 - back:4 * c + 4 - back],
                                                       in1=dst[:, back:], op0=ALU.mult, op1=ALU.add)
                        if back == 3:
                            ins.then_inc(xc_ready, 1)
                        else:
                            dve(ins)
                            dve.wait(eng)

            def gated_input(c):
                eng.wait_ge(u_ready, c + 1)
                eng.scalar_tensor_tensor(out=channels(c), in0=probs[:, c % 2, SEQ:2 * SEQ], scalar=1.0,
                                         in1=channels(c), op0=ALU.add, op1=ALU.mult).then_inc(gx_done, 1)

            def post_add(h, r):
                cols = slice(h * COLS, (h + 1) * COLS)
                eng.scalar_tensor_tensor(out=x[:, r, cols], in0=mix[:, r, cols], scalar=ssq[:, 4 + r:5 + r],
                                         in1=x[:, r, cols], op0=ALU.mult, op1=ALU.add).then_inc(x_added, 1)

            eng.wait_ge(rs_ready, 5)
            for h in range(2):
                for r in range(RT):
                    part = mix[:, r, h * COLS:(h + 1) * COLS]
                    eng.tensor_scalar(part, part, ssq[:, 4 + r:5 + r], None, ALU.mult).then_inc(rows_ready, 1)
            turned_lo_copy(6, hT, halves=(0,))
            lo2(0, 1)
            turned_lo_copy(6, hT, halves=(1,))
            eng.wait_ge(small_loaded, 32)
            dve(eng.tensor_scalar(sp[:, 0:8], par_lam, -1.0, None, ALU.mult))
            dve(eng.tensor_scalar(sp[:, 32:40], par_lam, -1.0, 0.0, ALU.mult, ALU.max))
            dve.wait(eng)
            eng.tensor_tensor(sp[:, 0:8], sp[:, 0:8], par_lam, ALU.min).then_inc(sp_abs, 1)
            dve(eng.tensor_scalar(sp[:, 88:96], par_ba, 0.5, None, ALU.mult))
            dve(eng.tensor_scalar(sp[:, 96:104], par_bx, 0.5, None, ALU.mult))
            eng.wait_ge(sp_exp, 1)
            eng.tensor_scalar(sp[:, 16:24], sp[:, 8:16], 1.0, None, ALU.add).then_inc(sp_one, 1)
            eng.wait_ge(sp_one, 1)
            dve(eng.tensor_scalar(sp[:, 40:48], sp[:, 16:24], 1.0, None, ALU.subtract))
            dve.wait(eng)
            dve(eng.tensor_scalar(sp[:, 48:56], sp[:, 40:48], 1e-30, None, ALU.max))
            dve(eng.tensor_scalar(sp[:, 56:64], sp[:, 40:48], 0.0, None, ALU.is_equal))
            dve.wait(eng)
            dve(eng.reciprocal(sp[:, 64:72], sp[:, 48:56]))
            dve(eng.tensor_tensor(sp[:, 56:64], sp[:, 56:64], sp[:, 8:16], ALU.mult))
            dve.wait(eng)
            dve(eng.tensor_tensor(sp[:, 64:72], sp[:, 64:72], sp[:, 8:16], ALU.mult))
            dve(eng.tensor_tensor(sp[:, 32:40], sp[:, 32:40], sp[:, 56:64], ALU.add))
            dve.wait(eng)
            eng.wait_ge(sp_ln, 1)
            dve(eng.tensor_tensor(sp[:, 64:72], sp[:, 64:72], sp[:, 24:32], ALU.mult))
            dve.wait(eng)
            dve(eng.tensor_tensor(sp[:, 72:80], sp[:, 64:72], sp[:, 32:40], ALU.add))
            dve.wait(eng)
            dve(eng.tensor_scalar(sp[:, 80:88], sp[:, 72:80], 2.0, None, ALU.mult))
            dve(eng.tensor_scalar(sp[:, 104:112], sp[:, 72:80], -4.0, None, ALU.mult))
            lo2(1, 0); take1(0, z[:, 1, KC2:KC2 + COLS]); lo2(1, 1)
            for r in range(RT):
                eng.wait_ge(free[r], 1)
            twice(scr, KC2, 1)
            twice(probs, VC2, 2)
            lo2(2, 0); take1(1, z[:, 1, Q2:Q2 + COLS], HD ** -0.5); lo2(2, 1)
            blocks(0, F_CK)
            lo2(3, 0)
            blocks(1, F_CV)
            dve.wait(eng)
            eng.wait_ge(read67[0], 2)
            eng.wait_ge(read67[1], 2)
            eng.sem_inc(flat_done, 1)
            take1(2, z[:, 1, Q2 + COLS:Q2 + D], HD ** -0.5); lo2(3, 1)
            lo2(4, 0); take1(3, z[:, 1, KS2:KS2 + COLS]); lo2(4, 1)
            for r in range(RT):
                eng.wait_ge(free[r], 4)
            twice(scr, KS2, 3)
            fill_copy(F_Q + 1, 2)
            fill_copy(F_Q + 3, 6)
            lo2(5, 0)
            eng.wait_ge(flat_hi, 1)
            eng.tensor_tensor(flat[1].rearrange("p j m -> p (j m)"), flat_f,
                              flat[0].rearrange("p j m -> p (j m)").bitcast(F32), ALU.subtract).then_inc(flat_lo, 1)
            lo2(5, 1)
            for r in range(RT):
                eng.wait_ge(free[r], 5)
                dve(eng.tensor_scalar(z[:, r, G2:G2 + GATES], z[:, r, G2:G2 + GATES], 0.5, 0.5, ALU.mult, ALU.add))
            lo2(6, 0); fill_copy(F_SK + 1, T2_KS + 2); take1(5, z[:, 1, KW2:KW2 + COLS])
            for r in range(RT):
                eng.wait_ge(free[r], 6)
            eng.wait_ge(filled, F_CV + 1)
            twice(probs, KW2, 4)
            lo2(6, 1)
            lo2(7, 0); fill_copy(F_WK + 1, T2_KW + 2); lo2(7, 1)
            eng.wait_ge(par_loaded, 64 * (LAYERS + 1))
            dve(eng.memset(scr[:, :, :], 0.0))
            dve(eng.memset(headsT[:, T2_V:T2_V + 4, :], 0.0))
            dve(eng.memset(probs[:, 0:2, :], 0.0))
            dve.wait(eng)
            lo2(8, 0); lo2(8, 1)
            lo2(9, 0)
            eng.wait_ge(read67[1], 7)
            for k in range(2):
                ins = eng.tensor_copy(scr[:, k, :].rearrange("p (g h n) -> p g h n", g=4, h=4)[:, :, :, 0:CMP],
                                      hidT[:, (2 + k) * COMP + COMP // 2:(3 + k) * COMP]
                                      .rearrange("p (g n) -> p g n", n=CMP).unsqueeze(2).to_broadcast([P, 4, 4, CMP]))
                if k:
                    ins.then_inc(pad_ready, 1)
                else:
                    dve(ins)
            lo2(9, 1)
            eng.wait_ge(filled, F_VC)
            for h in range(4):
                part = slice(32 * h, 32 * h + 32)
                ins = eng.tensor_copy(headsT[part, T2_V:T2_V + 4, h * HD:(h + 1) * HD],
                                      bank[7][part, 0:4 * HD].rearrange("p (g d) -> p g d", d=HD))
                if h == 3:
                    ins.then_inc(read67[1], 1)
                else:
                    dve(ins)
            wide = probs[:, 0:2, :].rearrange("p r (h n) -> p (r h) n", n=32)[:, :, 0:CMP]
            eng.wait_ge(cmask_ready, 1)
            for odd in range(2):
                eng.wait_ge(cs_ready, odd + 1)
                for r in range(RT):
                    dve(eng.tensor_tensor(probs[:, r, :].rearrange("p (h o n) -> p h o n", o=2, n=32)[:, :, odd, 0:CMP],
                                          bank[2 + odd][:, r * P:(r + 1) * P].rearrange("p (h n) -> p h n", n=16)[:, :, 0:CMP],
                                          cmask[:, r, :].unsqueeze(1).to_broadcast([P, 8, CMP]), ALU.add))
            dve.wait(eng)
            dve(eng.tensor_reduce(cstat, wide, AX.X, ALU.max))
            dve.wait(eng)
            eng.tensor_tensor(wide, wide, cstat.unsqueeze(2).to_broadcast([P, 32, CMP]), ALU.subtract)\
               .then_inc(cm_ready, 1)
            lo2(10, 0)
            eng.wait_ge(ce_ready, 1)
            dve(eng.tensor_reduce(cstat, wide, AX.X, ALU.add))
            dve.wait(eng)
            dve(eng.reciprocal(ccoef, cstat))
            dve.wait(eng)
            for r in range(RT):
                c = ccoef[:, 16 * r:16 * r + 16]
                dve(eng.tensor_tensor(c, c, z[:, r, G2:G2 + GATES].rearrange("p (h b) -> p h b", b=3)[:, :, 0], ALU.mult))
            dve.wait(eng)
            dve(eng.tensor_scalar(ccoef[:, 0:16], ccoef[:, 0:16], any_ok, None, ALU.mult))
            dve.wait(eng)
            eng.tensor_tensor(wide, wide, ccoef.unsqueeze(2).to_broadcast([P, 32, CMP]), ALU.mult)\
               .then_inc(cn_ready, 1)
            for r in range(RT):
                eng.wait_ge(free[r], 9)
            lo2(10, 1)
            eng.wait_ge(ct_ready, 2)
            eng.tensor_copy(probsT[:, 1, :], bank[3][:, :]).then_inc(cT_dve, 1)
            for r in range(RT):
                for n in range(2):
                    dve(eng.bn_stats(bn[:, 12 * r + 6 * n:12 * r + 6 * n + 6], z[:, r, n * COLS:(n + 1) * COLS]))
            dve.wait(eng)
            for r in range(RT):
                ins = eng.bn_aggr(bn[:, 24 + 2 * r:26 + 2 * r], bn[:, 12 * r:12 * r + 12])
                if r:
                    ins.then_inc(var_ready, 1)
                else:
                    dve(ins)
            lo2(11, 0)
            for r in range(RT):
                eng.wait_ge(cv_ready, r + 1)
                dve(eng.tensor_copy(mix[:, r, 0:COLS], bank[4 - 2 * r][:, :]))
                eng.tensor_copy(mix[:, r, COLS:D], bank[5 - 2 * r][:, :]).then_inc(cv_done, 1)
            dve.wait(eng)
            eng.wait_ge(vrs_ready, 1)
            eng.wait_ge(gain_loaded, 96)
            for r in range(RT):
                v = z[:, r, 0:D]
                dve(eng.tensor_scalar(v, v, bn[:, 24 + 2 * r:25 + 2 * r], bn[:, 28 + r:29 + r], ALU.subtract, ALU.mult))
            lo2(11, 1)
            attend_mask(A, causal)
            dve.wait(eng)
            for r in range(RT):
                dve(eng.tensor_tensor(z[:, r, 0:D], z[:, r, 0:D], gain[:, :], ALU.mult))
            dve.wait(eng)
            eng.sem_inc(gain_free, 1)
            lo2(12, 0)
            attend_copy(A)
            lo2(12, 1)
            eng.wait_ge(gain_loaded, 112)
            for r in range(RT):
                eng.tensor_tensor(z[:, r, 0:D], z[:, r, 0:D], gain[:, :], ALU.add).then_inc(vn_ready, 1)
            eng.wait_ge(vn_ready, 2)
            eng.sem_inc(gain_free, 1)
            attend_mask(A + 1, causal)
            group_out(0)
            def gated_rows(r):
                eng.wait_ge(free[r], product(12))
                for g in range(4):
                    if g % 2 == 0:
                        eng.wait_ge(filled, F_MIX + 2 * r + g // 2)
                    u = z[:, r, U2 + g * SEQ:U2 + (g + 1) * SEQ]
                    ins = eng.scalar_tensor_tensor(out=u, in0=bank[6 + g // 2][:, (g % 2) * SEQ:(g % 2 + 1) * SEQ],
                                                   scalar=par_bs[:, g:g + 1], in1=u, op0=ALU.add, op1=ALU.mult)
                    if g % 2:
                        ins.then_inc(read67[g // 2], 1)
                    else:
                        dve(ins)

            gated_rows(0)
            for b in range(12, 19):
                i = b - 11
                if 12 < b < 18:
                    attend_mask(A + i, causal)
                if b > 12:
                    group_out(i - 1)
                lo2(b + 1, 0)
                attend_copy(A + i)
                if b in (17, 18):
                    convolve(b - 1)
                if b == 17:
                    attend_mask(A + 7, causal)
                if b == 12:
                    gated_rows(1)
                    dve.wait(eng)
                    eng.wait_ge(read67[0], 9)
                    eng.wait_ge(read67[1], 10)
                    eng.sem_inc(rows_ready, 4)
                if b in (13, 15):
                    merge(b)
                lo2(b + 1, 1)
                if b == 12:
                    turned_lo_copy(7, mixT)
            group_out(7)
            eng.sem_inc(rows_ready, 4)
            lo2(20, 0); lo2(20, 1)
            lo2(21, 0)
            turned_lo_copy(8, mixT)
            lo2(21, 1)
            lo2(22, 0); gated_input(0); gated_input(1)
            merge(21)
            lo2(22, 1); gated_input(2); gated_input(3)
            lo2(23, 0); gated_input(4); gated_input(5)
            lo2(23, 1); gated_input(6); gated_input(7)
            gx = z[:, :, 0:D]
            eng.wait_ge(gx_done, 8)
            dve(eng.scalar_tensor_tensor(out=gx, in0=mix[:, :, :], scalar=1.0, in1=gx, op0=ALU.add, op1=ALU.mult))
            lo2(24, 0)
            merge(23)
            dve.wait(eng)
            eng.wait_ge(root_ready, 1)
            dve(eng.scalar_tensor_tensor(out=gx, in0=headsT[:, 0:8, :].rearrange("p (a b) c -> p a (b c)", a=2),
                                         scalar=0.5, in1=gx, op0=ALU.mult, op1=ALU.mult))
            dve.wait(eng)
            lo2(24, 1)
            for c in range(8):
                dve(eng.tensor_tensor_scan(headsT[:, c, :], mix[:, c // 4, (c % 4) * SEQ:(c % 4 + 1) * SEQ],
                                           channels(c), 0.0, ALU.mult, ALU.add))
            lo2(25, 0)
            dve.wait(eng)
            eng.tensor_tensor(headsT[:, 0:8, :], headsT[:, 0:8, :], headsT[:, 8:16, :], ALU.mult).then_inc(yc_ready, 1)
            lo2(25, 1)
            eng.wait_ge(yc_hi, 1)
            eng.tensor_tensor(mixT[1][:, :, :], headsT[:, 0:8, :], mixT[0][:, :, :].bitcast(F32), ALU.subtract)\
               .then_inc(yc_lo, 1)
            lo2(26, 0); lo2(26, 1)
            lo2(27, 0)
            merge(26)
            eng.wait_ge(merged_done, 10)
            eng.sem_inc(rows_ready, 2)
            lo2(27, 1)
            lo2(28, 0)
            turned_lo_copy(9, mixT, 0.5, halves=(0,))
            merge(27)
            eng.wait_ge(merged_done, 12)
            eng.sem_inc(rows_ready, 2)
            lo2(28, 1)
            turned_lo_copy(9, mixT, 0.5, halves=(1,))
            eng.wait_ge(gain_loaded, 16 * 7 + 16)
            lo2(29, 0)
            for r in range(RT):
                whole(28, r)
                post_gain(0, r, bank[r], 0).then_inc(free[r], 1)
            lo2(29, 1)
            lo2(30, 0)
            for r in range(RT):
                whole(29, r)
                post_gain(1, r, bank[r], 0).then_inc(free[r], 1)
            eng.wait_ge(free[0], product(30))
            eng.wait_ge(free[1], product(30))
            eng.sem_inc(gain_free, 1)
            eng.wait_ge(rs_ready, 6)
            eng.wait_ge(ffn_gain_loaded, 16)
            for h in range(2):
                for r in range(RT):
                    if h and r:
                        turned_lo_copy(10, hT, halves=(0,))
                    post_add(h, r)
                    eng.wait_ge(x_added, 2 * h + r + 1)
                    gain_rows(r, h, ffn_gain)
            lo2(30, 1)
            turned_lo_copy(10, hT, halves=(1,))
            ffn(B2 + PAIRS2, LAYERS, 6, None)
            eng.wait_ge(rs_ready, 8)
            eng.wait_ge(down_added, 4 * LAYERS + 4)
            for r in range(RT):
                for h in range(2):
                    post_add(h, r)


def rope_tables():
    inv = 1.0 / (np.float32(10000.0) ** (np.arange(0, HD, 2, dtype=np.float32) / HD))
    ang = (np.arange(SEQ, dtype=np.float32)[:, None] * inv[None, :]).astype(np.float32)
    c, s = np.cos(ang).astype(np.float32), np.sin(ang).astype(np.float32)
    by_row = lambda a: np.ascontiguousarray(a.reshape(RT, P, HD).transpose(1, 0, 2))
    return by_row(np.concatenate([c, c], 1)), by_row(np.concatenate([-s, s], 1))


def halves(w):
    n = w.shape[1] // COLS
    return w.reshape(2, KT // 2, P, n, COLS).transpose(3, 0, 2, 1, 4).reshape(n, 2, P, KT // 2 * COLS)


def ffn_layout(gate, up, down):
    k = lambda w: w.reshape(KT, P, FF_STEPS, FF_STEP)
    gu = np.stack([k(gate), k(up)], 3).transpose(2, 1, 0, 3, 4)
    gu = gu.reshape(FF_STEPS, P, KT * COLS)
    dn = down.reshape(FF_STEPS, 2, P, D).transpose(0, 2, 1, 3).reshape(FF_STEPS, P, 4 * UNIT)
    first = gu[0]
    second = np.concatenate([gu[1:, :, 6 * UNIT:], dn[:-1]], 2)
    loop = np.stack([gu[1:, :, :6 * UNIT], second], 1)
    last = dn[-1].reshape(P, 2, 2 * UNIT).transpose(1, 0, 2)
    return first, loop, last


def layout(i):
    t = {}
    t["x"] = i["x"].reshape(SEQ, D)
    w = i["w_in"]
    sizes = [256, 256, 256, 512, 512, 512, 256, 256, 256, 512, 64, 8]
    mq, mk, mv, dq, dk, dv, sq, sk, sv, iq, ik, iw = np.split(w, np.cumsum(sizes)[:-1], axis=2)
    groups = np.concatenate([iq, dq, dk, dv, mq, mk, sq, sk, mv, sv], 2)
    t["w1_groups"] = np.stack([halves(g) for g in groups])
    kv = np.concatenate([i["w_in_2"][0][:, 3072:3584]], 1)
    t["next_first"] = np.stack([t["w1_groups"][1, 0], halves(kv)[0]])
    narrow = np.concatenate([ik, iw], 2)
    t["w1_narrow"] = narrow.reshape(LAYERS, 2, KT // 2, P, NARROW).transpose(0, 1, 3, 2, 4)\
        .reshape(LAYERS, 2, P, KT // 2 * NARROW)
    t["w1_out"] = np.stack([halves(g) for g in i["w_out"]])
    ff = [ffn_layout(i["w_gate"][l], i["w_up"][l], i["w_down"][l]) for l in range(LAYERS)]
    ff.append(ffn_layout(i["w_ffn_in_2"][0][:, :DFF], i["w_ffn_in_2"][0][:, DFF:], i["w_ffn_out_2"][0]))
    for n, name in enumerate(("ff_first", "ff_loop", "ff_last")):
        t[name] = np.stack([f[n] for f in ff])
    again = lambda a: np.concatenate([a, a[-1:]])
    t["attn_norm_g"] = i["attn_norm_g"]
    t["ffn_norm_g"] = i["ffn_norm_g"]
    t["next_norm_g"] = np.concatenate([i["attn_norm_g"][1:], i["g_pre_mix_2"]])
    t["head_gains"] = again(np.concatenate([i["q_norm_g"], i["k_norm_g"]], 1))
    t["diff_lambda"] = again(i["diff_lambda"])
    t["diff_subln_g"] = again(i["diff_subln_g"])
    first = [0.8 - 0.6 * np.exp(-0.3 * l) for l in range(LAYERS + 1)]
    t["lam_init"] = np.array([[v, 1.0 - v] for v in first], np.float32)
    t["rope_c"], t["rope_s"] = rope_tables()
    w2 = i["w_in_2"][0]
    widths = [1024, 1024, 1024, 256, 256, 256, 256, 256, 256, GATES, 1024, 1024, 1024, 1024, 1024]
    u, v, q, kc, vc, ks, vs, kw, vw, ng, xr, rg, ma, mb, mc = np.split(w2, np.cumsum(widths)[:-1], axis=1)
    half = lambda a, n: a[:, n * COLS:(n + 1) * COLS]
    cols = [kc, vc, q, ks, vs, kw, vw, v, u]

    def branch(gate, w):
        return [half(gate, 0), half(w, 0), half(gate, 1), half(w, 1)]

    a, b, c = i["w_br_a_2"][0], i["w_br_b_2"][0], i["w_br_c_2"][0]
    cols += branch(ma, a) + [xr, rg] + branch(mb, b) + [mc, c, i["w_o_2"][0]]
    t["w2_groups"] = halves(np.concatenate(cols, 1))
    t["w2_narrow"] = ng.reshape(2, KT // 2, P, GATES).transpose(0, 2, 1, 3).reshape(2, P, KT // 2 * GATES)
    comp = np.stack([i["nsa_wk1_2"][0].reshape(COMP_K, P, SEQ), i["nsa_wv1_2"][0].reshape(COMP_K, P, SEQ)], 2)
    t["w2_comp"] = comp.reshape(2, 2, 4, P, COLS).transpose(0, 1, 3, 2, 4).reshape(2, 2, P, 4 * COLS)
    wk2 = i["nsa_wk2_2"][0].reshape(2, P, HD).transpose(1, 0, 2)
    wk2 = np.concatenate([wk2, wk2], 2).reshape(P, 256)
    wv2 = i["nsa_wv2_2"][0].reshape(2, P, HD).transpose(1, 0, 2).reshape(P, 128)
    pos = lambda e: e.reshape(COMP_K, P).T
    t["small2"] = np.concatenate([wk2, wv2, pos(i["nsa_pe_k_2"][0]), pos(i["nsa_pe_v_2"][0])], 1)
    ch = lambda e: e[0].reshape(KT, P).T
    cw = i["rnn_conv_w_2"][0].reshape(4, KT, P).transpose(2, 1, 0).reshape(P, 4 * KT)
    t["channel2"] = np.concatenate([i["gmlp_bs_2"][0].T, cw, ch(i["rnn_conv_b_2"]), ch(i["rnn_ba_2"]),
                                    ch(i["rnn_bx_2"]), ch(i["rnn_lam_2"])], 1)
    t["w_s"] = i["gmlp_ws_2"][0].transpose(2, 0, 1)
    g = lambda w: w[0].reshape(KT, P, HD).transpose(1, 0, 2).reshape(P, KT * HD)
    t["w_gates"] = np.stack([g(i["rnn_wa_2"]), g(i["rnn_wx_2"])])
    t["rows2"] = np.concatenate([i["gmlp_ln_g_2"], i["gmlp_ln_b_2"], i["g_post_mix_2"], i["g_pre_ffn_2"],
                                 i["g_post_ffn_2"]])
    return {k: np.ascontiguousarray(v) for k, v in t.items()}


def kernel(**inputs):
    import concourse.bacc as bacc
    from concourse.bass_utils import run_bass_kernel_spmd

    nc = bacc.Bacc("TRN2", target_bir_lowering=False, num_devices=1)
    arrays = layout({k: np.asarray(v) for k, v in inputs.items()})
    t = {k: nc.dram_tensor(f"in_{k}", v.shape, mybir.dt.from_np(v.dtype), kind="ExternalInput").ap()
         for k, v in arrays.items()}
    t["out"] = nc.dram_tensor("out_x", (SEQ, D), F32, kind="ExternalOutput").ap()
    block_one_and_two(nc, t)
    r = run_bass_kernel_spmd(nc, [{f"in_{k}": v for k, v in arrays.items()}], core_ids=[0])
    return r.results[0]["out_x"].reshape(1, SEQ, D)
```
